# Optimizing a Trainium2 kernel written in Bass

```python
import math
import jax, jax.numpy as jnp
from jax import lax
import numpy as np
import jax
import jax.numpy as jnp

D_MODEL = 1024
BATCH = 1
SEQ = 256
DEPTH = 2

CHUNK = 64
Q_BLOCK = 128
N_GROUPS = 4
GROUP_WIDTH = D_MODEL // N_GROUPS
D_MIX = N_GROUPS * GROUP_WIDTH
HEAD_DIM = 64
N_HEADS_G = GROUP_WIDTH // HEAD_DIM
DIFF_D = HEAD_DIM // 2
Q_LORA = 256
KV_LORA = 128
QK_NOPE = 64
QK_ROPE = 32
V_HEAD = HEAD_DIM
ROPE_THETA = 10000.0
IDX_HEADS = 8
IDX_DIM = 32
TOPK_MAX = 256
BAND_CHUNKS = 8
REL_CLIP = 128
D_FF = 2816
N_EXPERTS = 8
TOP_K = 2
D_FF_EXPERT = 3584
N_DENSE = (DEPTH + 1) // 2
N_MOE = DEPTH // 2
EPS = 1e-6

IN_LAYOUT = (
    ('a_q', N_HEADS_G * 2 * DIFF_D), ('a_k', N_HEADS_G * 2 * DIFF_D), ('a_v', N_HEADS_G * 2 * DIFF_D),
    ('b_qd', Q_LORA), ('b_kvd', KV_LORA), ('b_kr', QK_ROPE),
    ('c_q', GROUP_WIDTH), ('c_k', GROUP_WIDTH), ('c_v', GROUP_WIDTH),
    ('c_qi', IDX_HEADS * IDX_DIM), ('c_ki', IDX_DIM), ('c_wi', IDX_HEADS),
    ('d_q', GROUP_WIDTH), ('d_k', GROUP_WIDTH), ('d_v', GROUP_WIDTH),
)
D_IN = int(sum(w for _, w in IN_LAYOUT))
IN_SPLITS = tuple(int(v) for v in np.cumsum([w for _, w in IN_LAYOUT])[:-1])


def rmsnorm(x, g):
    xf = x.astype(jnp.float32)
    y = xf * lax.rsqrt(jnp.mean(xf * xf, axis=-1, keepdims=True) + EPS)
    return (y * g.astype(jnp.float32)).astype(x.dtype)

def adaln(x, g, shift, scale):
    return rmsnorm(x, g) * (1 + scale[:, None, :]) + shift[:, None, :]

def alibi_slopes(n):
    return 2.0 ** (-8.0 * jnp.arange(1, n + 1, dtype=jnp.float32) / n)

def rope_tables(s):
    inv = ROPE_THETA ** (-jnp.arange(0, QK_ROPE, 2, dtype=jnp.float32) / QK_ROPE)
    ang = jnp.arange(s, dtype=jnp.float32)[:, None] * inv[None, :]
    return jnp.cos(ang), jnp.sin(ang)

def apply_rope(x, cos, sin):
    x1, x2 = jnp.split(x, 2, axis=-1)
    cs = cos[None, :, None, :].astype(x.dtype)
    sn = sin[None, :, None, :].astype(x.dtype)
    return jnp.concatenate([x1 * cs - x2 * sn, x1 * sn + x2 * cs], axis=-1)

def to_blocks(a):
    b, s = a.shape[:2]
    return jnp.moveaxis(a.reshape(b, s // Q_BLOCK, Q_BLOCK, *a.shape[2:]), 1, 0)

def from_blocks(a):
    nb, b, qb = a.shape[:3]
    return jnp.moveaxis(a, 0, 1).reshape(b, nb * qb, *a.shape[3:])

def sweep_query_blocks(fn, *qs):
    nb = qs[0].shape[1] // Q_BLOCK
    out = lax.map(lambda a: fn(*a), (jnp.arange(nb), *[to_blocks(q) for q in qs]))
    return from_blocks(out)

def chunk_mask(blk, s_len):
    t = blk * Q_BLOCK + jnp.arange(Q_BLOCK)
    s = jnp.arange(s_len)
    return t, s, (s[None, :] // CHUNK) <= (t[:, None] // CHUNK)

def diff_attention(q, k, v, lam_vecs, norm_g, layer_idx):
    b, s_len, h = q.shape[:3]
    lam_init = 0.8 - 0.6 * math.exp(-0.3 * layer_idx)
    lv = lam_vecs.astype(jnp.float32)
    lam = jnp.exp(jnp.sum(lv[0] * lv[1])) - jnp.exp(jnp.sum(lv[2] * lv[3])) + lam_init
    slopes = alibi_slopes(h)
    scale = DIFF_D ** -0.5

    def block(blk, qb):
        t, s, mask = chunk_mask(blk, s_len)
        bias = -slopes[:, None, None] * jnp.abs(t[:, None] - s[None, :]).astype(jnp.float32)
        bias = jnp.where(mask[None], bias, -jnp.inf)
        logits = jnp.einsum('bqhcd,bshcd->bchqs', qb, k).astype(jnp.float32) * scale + bias[None, None]
        p = jax.nn.softmax(logits, axis=-1)
        p = p[:, 0] - lam * p[:, 1]
        return jnp.einsum('bhqs,bshe->bqhe', p.astype(v.dtype), v)

    o = sweep_query_blocks(block, q)
    o = rmsnorm(o, norm_g) * (1.0 - lam_init)
    return o.reshape(b, s_len, h * 2 * DIFF_D)

def latent_attention(qd, kvd, kr, q_norm_g, kv_norm_g, w_uq, w_ukv, cos, sin):
    b, s_len = qd.shape[:2]
    h = N_HEADS_G
    q = (rmsnorm(qd, q_norm_g) @ w_uq).reshape(b, s_len, h, QK_NOPE + QK_ROPE)
    q = jnp.concatenate([q[..., :QK_NOPE], apply_rope(q[..., QK_NOPE:], cos, sin)], axis=-1)
    kv = (rmsnorm(kvd, kv_norm_g) @ w_ukv).reshape(b, s_len, h, QK_NOPE + V_HEAD)
    k_nope, v = kv[..., :QK_NOPE], kv[..., QK_NOPE:]
    k_rope = apply_rope(kr[:, :, None, :], cos, sin)
    k = jnp.concatenate([k_nope, jnp.broadcast_to(k_rope, (b, s_len, h, QK_ROPE))], axis=-1)
    scale = (QK_NOPE + QK_ROPE) ** -0.5

    def block(blk, qb):
        _, _, mask = chunk_mask(blk, s_len)
        logits = jnp.einsum('bqhd,bshd->bhqs', qb, k).astype(jnp.float32) * scale
        logits = jnp.where(mask[None, None], logits, -jnp.inf)
        p = jax.nn.softmax(logits, axis=-1)
        return jnp.einsum('bhqs,bshd->bqhd', p.astype(v.dtype), v)

    return sweep_query_blocks(block, q).reshape(b, s_len, h * V_HEAD)

def indexed_sparse_attention(q, k, v, q_idx, k_idx, w_idx):
    b, s_len, h, dh = q.shape
    n_sel = min(TOPK_MAX, s_len // 4)
    slopes = alibi_slopes(h)
    scale = dh ** -0.5
    w = w_idx.astype(jnp.float32) * (IDX_HEADS ** -0.5 * IDX_DIM ** -0.5)

    def block(blk, qb, qib, wb):
        t, _, mask = chunk_mask(blk, s_len)
        score = jax.nn.relu(jnp.einsum('bqhd,bsd->bqhs', qib, k_idx).astype(jnp.float32))
        score = jnp.einsum('bqhs,bqh->bqs', score, wb)
        score = jnp.where(mask[None], score, -jnp.inf)
        top_val, top_idx = lax.top_k(score, n_sel)
        valid = jnp.isfinite(top_val)
        k_sel = jax.vmap(lambda kk, ii: kk[ii])(k, top_idx)
        v_sel = jax.vmap(lambda vv, ii: vv[ii])(v, top_idx)
        logits = jnp.einsum('bqhd,bqnhd->bhqn', qb, k_sel).astype(jnp.float32) * scale
        dist = jnp.abs(t[None, :, None] - top_idx).astype(jnp.float32)
        logits = logits - slopes[None, :, None, None] * dist[:, None]
        logits = jnp.where(valid[:, None], logits, -jnp.inf)
        p = jax.nn.softmax(logits, axis=-1)
        return jnp.einsum('bhqn,bqnhd->bqhd', p.astype(v.dtype), v_sel)

    return sweep_query_blocks(block, q, q_idx, w).reshape(b, s_len, h * dh)

def chunk_band_attention(q, k, v, rel_bias):
    b, s_len, h, dh = q.shape
    nc = s_len // CHUNK
    band = (BAND_CHUNKS + 1) * CHUNK
    qc = q.reshape(b, nc, CHUNK, h, dh)
    pad = ((0, 0), (BAND_CHUNKS * CHUNK, 0), (0, 0), (0, 0))
    kp = jnp.pad(k, pad).reshape(b, nc + BAND_CHUNKS, CHUNK, h, dh)
    vp = jnp.pad(v, pad).reshape(b, nc + BAND_CHUNKS, CHUNK, h, dh)
    k_band = jnp.concatenate([kp[:, j:j + nc] for j in range(BAND_CHUNKS + 1)], axis=2)
    v_band = jnp.concatenate([vp[:, j:j + nc] for j in range(BAND_CHUNKS + 1)], axis=2)
    i = jnp.arange(CHUNK)
    j = jnp.arange(band)
    rel = BAND_CHUNKS * CHUNK + i[:, None] - j[None, :]
    bias = rel_bias[:, jnp.clip(rel, -REL_CLIP, REL_CLIP) + REL_CLIP].astype(jnp.float32)
    key_chunk = jnp.arange(nc)[:, None] - BAND_CHUNKS + (j // CHUNK)[None, :]
    valid = key_chunk >= 0
    logits = jnp.einsum('bnqhd,bnkhd->bnhqk', qc, k_band).astype(jnp.float32) * (dh ** -0.5)
    logits = logits + bias[None, None]
    logits = jnp.where(valid[None, :, None, None, :], logits, -jnp.inf)
    p = jax.nn.softmax(logits, axis=-1)
    o = jnp.einsum('bnhqk,bnkhd->bnqhd', p.astype(v.dtype), v_band)
    return o.reshape(b, s_len, h * dh)

def swiglu(h, w1, w3, w2):
    return (jax.nn.silu(h @ w1) * (h @ w3)) @ w2

def moe_swiglu(h, router, w1, w3, w2):
    b, s_len, d = h.shape
    ht = h.reshape(-1, d)
    logits = (ht @ router).astype(jnp.float32)
    top_val, top_idx = lax.top_k(logits, TOP_K)
    gates = jax.nn.softmax(top_val, axis=-1)
    combine = jnp.sum(jax.nn.one_hot(top_idx, N_EXPERTS, dtype=jnp.float32) * gates[..., None], axis=1)
    out = jnp.zeros_like(ht)
    for e in range(N_EXPERTS):
        out = out + combine[:, e:e + 1].astype(ht.dtype) * swiglu(ht, w1[e], w3[e], w2[e])
    return out.reshape(b, s_len, d)

def first_inputs(seed: int = 0) -> dict:
    key = jax.random.key(seed)
    ks = jax.random.split(key, 24)
    h = N_HEADS_G

    def nrm(k, shape, fan_in, s=1.0):
        return jax.random.normal(k, shape, jnp.float32) * (s * fan_in ** -0.5)

    def gain(k, shape):
        return 1.0 + 0.1 * jax.random.normal(k, shape, jnp.float32)

    return {
        'x': jax.random.normal(ks[0], (BATCH, SEQ, D_MODEL), jnp.float32),
        'c': jax.random.normal(ks[1], (BATCH, D_MODEL), jnp.float32),
        'ada_w': nrm(ks[2], (DEPTH, D_MODEL, 6 * D_MODEL), D_MODEL, 0.5),
        'ada_b': 0.02 * jax.random.normal(ks[3], (DEPTH, 6 * D_MODEL), jnp.float32),
        'mix_norm_g': gain(ks[4], (DEPTH, D_MODEL)),
        'ffn_norm_g': gain(ks[5], (DEPTH, D_MODEL)),
        'w_in': nrm(ks[6], (DEPTH, D_MODEL, D_IN), D_MODEL),
        'w_out': nrm(ks[7], (DEPTH, D_MIX, D_MODEL), D_MIX),
        'diff_lambda': 0.1 * jax.random.normal(ks[8], (DEPTH, 4, DIFF_D), jnp.float32),
        'diff_norm_g': gain(ks[9], (DEPTH, 2 * DIFF_D)),
        'mla_q_norm_g': gain(ks[10], (DEPTH, Q_LORA)),
        'mla_kv_norm_g': gain(ks[11], (DEPTH, KV_LORA)),
        'mla_w_uq': nrm(ks[12], (DEPTH, Q_LORA, h * (QK_NOPE + QK_ROPE)), Q_LORA),
        'mla_w_ukv': nrm(ks[13], (DEPTH, KV_LORA, h * (QK_NOPE + V_HEAD)), KV_LORA),
        'band_rel_bias': 0.2 * jax.random.normal(ks[14], (DEPTH, h, 2 * REL_CLIP + 1), jnp.float32),
        'ffn_w1': nrm(ks[15], (N_DENSE, D_MODEL, D_FF), D_MODEL),
        'ffn_w3': nrm(ks[16], (N_DENSE, D_MODEL, D_FF), D_MODEL),
        'ffn_w2': nrm(ks[17], (N_DENSE, D_FF, D_MODEL), D_FF),
        'moe_router': nrm(ks[18], (N_MOE, D_MODEL, N_EXPERTS), D_MODEL),
        'moe_w1': nrm(ks[19], (N_MOE, N_EXPERTS, D_MODEL, D_FF_EXPERT), D_MODEL),
        'moe_w3': nrm(ks[20], (N_MOE, N_EXPERTS, D_MODEL, D_FF_EXPERT), D_MODEL),
        'moe_w2': nrm(ks[21], (N_MOE, N_EXPERTS, D_FF_EXPERT, D_MODEL), D_FF_EXPERT),
        'final_norm_g': gain(ks[22], (D_MODEL,)),
    }

def first_block(x, c, ada_w, ada_b, mix_norm_g, ffn_norm_g, w_in, w_out, diff_lambda, diff_norm_g,
              mla_q_norm_g, mla_kv_norm_g, mla_w_uq, mla_w_ukv, band_rel_bias,
              ffn_w1, ffn_w3, ffn_w2, moe_router, moe_w1, moe_w3, moe_w2, final_norm_g):
    b, s_len, _ = x.shape
    h = N_HEADS_G
    cos, sin = rope_tables(s_len)
    for l in range(DEPTH):
        mod = jax.nn.silu(c) @ ada_w[l] + ada_b[l]
        sh_m, sc_m, g_m, sh_f, sc_f, g_f = jnp.split(mod, 6, axis=-1)
        hn = adaln(x, mix_norm_g[l], sh_m, sc_m)
        (a_q, a_k, a_v, b_qd, b_kvd, b_kr, c_q, c_k, c_v,
         c_qi, c_ki, c_wi, d_q, d_k, d_v) = jnp.split(hn @ w_in[l], IN_SPLITS, axis=-1)
        o_a = diff_attention(a_q.reshape(b, s_len, h, 2, DIFF_D), a_k.reshape(b, s_len, h, 2, DIFF_D),
                             a_v.reshape(b, s_len, h, 2 * DIFF_D), diff_lambda[l], diff_norm_g[l], l)
        o_b = latent_attention(b_qd, b_kvd, b_kr, mla_q_norm_g[l], mla_kv_norm_g[l],
                               mla_w_uq[l], mla_w_ukv[l], cos, sin)
        o_c = indexed_sparse_attention(c_q.reshape(b, s_len, h, HEAD_DIM), c_k.reshape(b, s_len, h, HEAD_DIM),
                                       c_v.reshape(b, s_len, h, HEAD_DIM),
                                       c_qi.reshape(b, s_len, IDX_HEADS, IDX_DIM), c_ki, c_wi)
        o_d = chunk_band_attention(d_q.reshape(b, s_len, h, HEAD_DIM), d_k.reshape(b, s_len, h, HEAD_DIM),
                                   d_v.reshape(b, s_len, h, HEAD_DIM), band_rel_bias[l])
        y = jnp.concatenate([o_a, o_b, o_c, o_d], axis=-1) @ w_out[l]
        x = x + g_m[:, None, :] * y
        hn = adaln(x, ffn_norm_g[l], sh_f, sc_f)
        if l % 2 == 0:
            f = swiglu(hn, ffn_w1[l // 2], ffn_w3[l // 2], ffn_w2[l // 2])
        else:
            f = moe_swiglu(hn, moe_router[l // 2], moe_w1[l // 2], moe_w3[l // 2], moe_w2[l // 2])
        x = x + g_f[:, None, :] * f
    return rmsnorm(x, final_norm_g)


DEPTH_2 = 1

GRID_W = 64
CTX_LEN = 256
MLSTM_HEADS = 4
MLSTM_DH = 128
MLSTM_W = MLSTM_HEADS * MLSTM_DH
MLSTM_CHUNK = 64
QK_CONV = 3
N_GATES = 4 * MLSTM_HEADS
ATTN_HEADS = 8
KV_HEADS = 2
ATTN_DH = 64
ATTN_W = ATTN_HEADS * ATTN_DH
KV_W = KV_HEADS * ATTN_DH
GQA_GROUP = ATTN_HEADS // KV_HEADS
WINDOW = 128
ATTN_BLOCK = 128
ROPE_BASE = 10000.0
ROPE_AXIS_PAIRS = ATTN_DH // 4
MIX_W = MLSTM_W + ATTN_W
IN_SPLITS_2 = (2 * MLSTM_W, 3 * MLSTM_W, 4 * MLSTM_W, 4 * MLSTM_W + N_GATES,
             4 * MLSTM_W + N_GATES + ATTN_W, 4 * MLSTM_W + N_GATES + ATTN_W + KV_W)
IN_COLS = 4 * MLSTM_W + N_GATES + ATTN_W + 2 * KV_W
FFN_CONV = 3


def rmsnorm_2(x, g):
    xf = x.astype(jnp.float32)
    y = xf * lax.rsqrt(jnp.mean(xf * xf, axis=-1, keepdims=True) + EPS)
    return (y * g.astype(jnp.float32)).astype(x.dtype)

def modulate(h, shift, scale):
    return h * (1 + scale) + shift

def dwconv(x, w, b):
    k = w.shape[0]
    y = lax.conv_general_dilated(x, w[:, None, :], window_strides=(1,), padding=[(k // 2, k // 2)],
                                 dimension_numbers=('NWC', 'WIO', 'NWC'),
                                 feature_group_count=x.shape[-1])
    return y + b

def heads_first(t, n_heads):
    b, l, _ = t.shape
    return t.reshape(b, l, n_heads, -1).transpose(0, 2, 1, 3)

def axial_rope(n_tokens):
    rows = n_tokens // GRID_W
    r, col = jnp.meshgrid(jnp.arange(rows, dtype=jnp.float32), jnp.arange(GRID_W, dtype=jnp.float32),
                          indexing='ij')
    inv = ROPE_BASE ** (-jnp.arange(ROPE_AXIS_PAIRS, dtype=jnp.float32) / ROPE_AXIS_PAIRS)
    ang = jnp.stack([r.reshape(-1)[:, None] * inv, col.reshape(-1)[:, None] * inv], axis=1)
    return jnp.cos(ang), jnp.sin(ang)

def apply_rope_2(x, cos, sin):
    b, l, h, _ = x.shape
    xr = x.astype(jnp.float32).reshape(b, l, h, 2, 2, ROPE_AXIS_PAIRS)
    x0, x1 = xr[..., 0, :], xr[..., 1, :]
    cs, sn = cos[:, None], sin[:, None]
    y = jnp.stack([x0 * cs - x1 * sn, x0 * sn + x1 * cs], axis=-2)
    return y.reshape(b, l, h, ATTN_DH).astype(x.dtype)

def project_tokens(h, w_in, qk_conv_w, qk_conv_b, gate_b):
    b, l, _ = h.shape
    u = h @ w_in
    qk, v_m, o_m, gates, q_a, k_a, v_a = jnp.split(u, IN_SPLITS_2, axis=-1)
    q_m, k_m = jnp.split(jax.nn.silu(dwconv(qk, qk_conv_w, qk_conv_b)), 2, axis=-1)
    q_m = heads_first(q_m, MLSTM_HEADS).astype(jnp.float32)
    k_m = heads_first(k_m, MLSTM_HEADS).astype(jnp.float32) * (MLSTM_DH ** -0.5)
    v_m = heads_first(v_m, MLSTM_HEADS).astype(jnp.float32)
    g = (gates + gate_b).astype(jnp.float32).reshape(b, l, 4, MLSTM_HEADS).transpose(2, 0, 3, 1)
    gates = (g[0], jax.nn.log_sigmoid(g[1]), g[2], jax.nn.log_sigmoid(g[3]))
    q_a = q_a.reshape(b, l, ATTN_HEADS, ATTN_DH)
    k_a = k_a.reshape(b, l, KV_HEADS, ATTN_DH)
    v_a = v_a.reshape(b, l, KV_HEADS, ATTN_DH)
    return q_m, k_m, v_m, o_m, gates, q_a, k_a, v_a

def init_state(b):
    return (jnp.zeros((b, MLSTM_HEADS, MLSTM_DH, MLSTM_DH), jnp.float32),
            jnp.zeros((b, MLSTM_HEADS, MLSTM_DH), jnp.float32),
            jnp.zeros((b, MLSTM_HEADS), jnp.float32))

def mlstm_scan(q, k, v, log_i, log_f, init, return_h):
    b, h, l, dh = k.shape
    nc = l // MLSTM_CHUNK
    chunk = lambda t: t.reshape((b, h, nc, MLSTM_CHUNK) + t.shape[3:])
    k, v, li, lf = chunk(k), chunk(v), chunk(log_i), chunk(log_f)
    cum = jnp.cumsum(lf, axis=-1)
    cum_end = cum[..., -1]
    g = cum_end[..., None] - cum + li
    m_loc = jnp.max(g, axis=-1)
    w = jnp.exp(g - m_loc[..., None])
    c_loc = jnp.einsum('bhnsd,bhnse->bhnde', w[..., None] * k, v)
    n_loc = jnp.einsum('bhns,bhnsd->bhnd', w, k)

    def step(carry, inp):
        c_st, n_st, m_st = carry
        c_l, n_l, m_l, bt = inp
        m_new = jnp.maximum(bt + m_st, m_l)
        a = jnp.exp(bt + m_st - m_new)
        s = jnp.exp(m_l - m_new)
        return (a[..., None, None] * c_st + s[..., None, None] * c_l,
                a[..., None] * n_st + s[..., None] * n_l, m_new), (c_st, n_st, m_st)

    final, starts = lax.scan(step, init, tuple(jnp.moveaxis(t, 2, 0) for t in (c_loc, n_loc, m_loc, cum_end)))
    if not return_h:
        return None, final
    c0, n0, m0 = (jnp.moveaxis(t, 0, 2) for t in starts)
    q = chunk(q)
    a_log = cum + m0[..., None]
    d_log = cum[..., :, None] - cum[..., None, :] + li[..., None, :]
    order = jnp.tril(jnp.ones((MLSTM_CHUNK, MLSTM_CHUNK), dtype=bool))
    d_log = jnp.where(order, d_log, -jnp.inf)
    m_t = jnp.maximum(a_log, jnp.max(d_log, axis=-1))
    dec = jnp.exp(d_log - m_t[..., None])
    inter = jnp.exp(a_log - m_t)
    s = jnp.einsum('bhntd,bhnsd->bhnts', q, k) * dec
    num = jnp.einsum('bhnts,bhnse->bhnte', s, v) + inter[..., None] * jnp.einsum('bhntd,bhnde->bhnte', q, c0)
    den = jnp.sum(s, axis=-1) + inter * jnp.einsum('bhntd,bhnd->bhnt', q, n0)
    hid = num / jnp.maximum(jnp.abs(den), jnp.exp(-m_t))[..., None]
    return hid.reshape(b, h, l, dh), final

def mlstm_bidirectional(q, k, v, gates, init_f, init_b, return_h):
    li_f, lf_f, li_b, lf_b = gates
    flip = lambda t: jnp.flip(t, axis=2)
    h_f, st_f = mlstm_scan(q, k, v, li_f, lf_f, init_f, return_h)
    h_b, st_b = mlstm_scan(flip(q), flip(k), flip(v), flip(li_b), flip(lf_b), init_b, return_h)
    hid = h_f + flip(h_b) if return_h else None
    return hid, st_f, st_b

def mlstm_merge(h, o, gain):
    b, _, l, _ = h.shape
    hn = h * lax.rsqrt(jnp.mean(h * h, axis=-1, keepdims=True) + EPS)
    hn = hn.transpose(0, 2, 1, 3).reshape(b, l, MLSTM_W) * gain.astype(jnp.float32)
    return (hn * jax.nn.sigmoid(o.astype(jnp.float32))).astype(o.dtype)

def window_attention(q, k, v, k_ctx, v_ctx, sink):
    b, l = q.shape[:2]
    nb = l // ATTN_BLOCK
    qb = q.reshape(b, nb, ATTN_BLOCK, KV_HEADS, GQA_GROUP, ATTN_DH)

    def band(t):
        tb = jnp.pad(t.reshape(b, nb, ATTN_BLOCK, KV_HEADS, ATTN_DH), ((0, 0), (1, 1), (0, 0), (0, 0), (0, 0)))
        return jnp.concatenate([tb[:, :-2], tb[:, 1:-1], tb[:, 2:]], axis=2)

    kb, vb = band(k), band(v)
    n_band = 3 * ATTN_BLOCK
    qpos = jnp.arange(l).reshape(nb, ATTN_BLOCK)
    kpos = qpos[:, :1] - ATTN_BLOCK + jnp.arange(n_band)
    valid = ((jnp.abs(kpos[:, None, :] - qpos[:, :, None]) <= WINDOW)
             & (kpos >= 0)[:, None, :] & (kpos < l)[:, None, :])
    s_band = jnp.einsum('bnqhgd,bnkhd->bnhgqk', qb, kb).astype(jnp.float32)
    s_band = jnp.where(valid[None, :, None, None], s_band, -jnp.inf)
    s_ctx = jnp.einsum('bnqhgd,bchd->bnhgqc', qb, k_ctx).astype(jnp.float32)
    s_sink = jnp.broadcast_to(sink.astype(jnp.float32).reshape(KV_HEADS, GQA_GROUP, 1, 1),
                              s_band.shape[:-1] + (1,))
    p = jax.nn.softmax(jnp.concatenate([s_band, s_ctx, s_sink], axis=-1), axis=-1).astype(v.dtype)
    out = (jnp.einsum('bnhgqk,bnkhd->bnqhgd', p[..., :n_band], vb)
           + jnp.einsum('bnhgqc,bchd->bnqhgd', p[..., n_band:n_band + k_ctx.shape[1]], v_ctx))
    return out.reshape(b, l, ATTN_W)

def context_attention(q, k, v, sink):
    b, n = q.shape[:2]
    qg = q.reshape(b, n, KV_HEADS, GQA_GROUP, ATTN_DH)
    s = jnp.einsum('bqhgd,bkhd->bhgqk', qg, k).astype(jnp.float32)
    s_sink = jnp.broadcast_to(sink.astype(jnp.float32).reshape(KV_HEADS, GQA_GROUP, 1, 1), s.shape[:-1] + (1,))
    p = jax.nn.softmax(jnp.concatenate([s, s_sink], axis=-1), axis=-1)[..., :-1].astype(v.dtype)
    return jnp.einsum('bhgqk,bkhd->bqhgd', p, v).reshape(b, n, ATTN_W)

def conv_glu(h, w_up, conv_w, conv_b, w_down):
    a, val = jnp.split(h @ w_up, 2, axis=-1)
    a = jax.nn.gelu(dwconv(a, conv_w, conv_b))
    return (a * val) @ w_down

def second_inputs(seed: int = 0) -> dict:
    key = jax.random.key(seed)
    ks = jax.random.split(key, 20)
    nrm = lambda k, shape, s: jax.random.normal(k, shape, jnp.float32) * s
    f_bias = jnp.linspace(3.0, 6.0, MLSTM_HEADS, dtype=jnp.float32)
    zero_h = jnp.zeros((MLSTM_HEADS,), jnp.float32)
    gate_base = jnp.stack([zero_h, f_bias, zero_h, f_bias]).reshape(-1)
    return {
        'x': nrm(ks[0], (BATCH, SEQ, D_MODEL), 1.0),
        'c': nrm(ks[1], (BATCH, D_MODEL), 1.0),
        'ctx': nrm(ks[2], (BATCH, CTX_LEN, D_MODEL), 1.0),
        'c_ctx': nrm(ks[3], (D_MODEL,), 1.0),
        'w_ada': nrm(ks[4], (DEPTH_2, D_MODEL, 6 * D_MODEL), 0.5 * D_MODEL ** -0.5),
        'b_ada': nrm(ks[5], (DEPTH_2, 6 * D_MODEL), 0.02),
        'norm_mix': 1.0 + nrm(ks[6], (DEPTH_2, D_MODEL), 0.02),
        'norm_ffn': 1.0 + nrm(ks[7], (DEPTH_2, D_MODEL), 0.02),
        'w_in': nrm(ks[8], (DEPTH_2, D_MODEL, IN_COLS), D_MODEL ** -0.5),
        'gate_b': gate_base[None, :] + nrm(ks[9], (DEPTH_2, N_GATES), 0.1),
        'qk_conv_w': nrm(ks[10], (DEPTH_2, QK_CONV, 2 * MLSTM_W), QK_CONV ** -0.5),
        'qk_conv_b': nrm(ks[11], (DEPTH_2, 2 * MLSTM_W), 0.02),
        'mlstm_norm': 1.0 + nrm(ks[12], (DEPTH_2, MLSTM_W), 0.02),
        'attn_sink': nrm(ks[13], (DEPTH_2, ATTN_HEADS), 0.5),
        'w_out': nrm(ks[14], (DEPTH_2, MIX_W, D_MODEL), MIX_W ** -0.5),
        'w_up': nrm(ks[15], (DEPTH_2, D_MODEL, 2 * D_FF), D_MODEL ** -0.5),
        'ffn_conv_w': nrm(ks[16], (DEPTH_2, FFN_CONV, D_FF), FFN_CONV ** -0.5),
        'ffn_conv_b': nrm(ks[17], (DEPTH_2, D_FF), 0.02),
        'w_down': nrm(ks[18], (DEPTH_2, D_FF, D_MODEL), D_FF ** -0.5),
        'final_norm': 1.0 + nrm(ks[19], (D_MODEL,), 0.02),
    }

def second_block(x, c, ctx, c_ctx, w_ada, b_ada, norm_mix, norm_ffn, w_in, gate_b, qk_conv_w, qk_conv_b,
              mlstm_norm, attn_sink, w_out, w_up, ffn_conv_w, ffn_conv_b, w_down, final_norm):
    cos, sin = axial_rope(x.shape[1])
    attn_scale = ATTN_DH ** -0.5
    for l in range(DEPTH_2):
        last = l == DEPTH_2 - 1
        sh_a, sc_a, g_a, sh_f, sc_f, g_f = jnp.split(
            (jax.nn.silu(c) @ w_ada[l] + b_ada[l])[:, None, :], 6, axis=-1)
        csh_a, csc_a, cg_a, csh_f, csc_f, cg_f = jnp.split(
            jax.nn.silu(c_ctx) @ w_ada[l] + b_ada[l], 6, axis=-1)

        hc = modulate(rmsnorm_2(ctx, norm_mix[l]), csh_a, csc_a)
        qm_c, km_c, vm_c, om_c, gates_c, qa_c, ka_c, va_c = project_tokens(
            hc, w_in[l], qk_conv_w[l], qk_conv_b[l], gate_b[l])
        zero = init_state(ctx.shape[0])
        hm_c, st_f, st_b = mlstm_bidirectional(qm_c, km_c, vm_c, gates_c, zero, zero, not last)

        hx = modulate(rmsnorm_2(x, norm_mix[l]), sh_a, sc_a)
        qm, km, vm, om, gates_x, qa, ka, va = project_tokens(hx, w_in[l], qk_conv_w[l], qk_conv_b[l], gate_b[l])
        hm, _, _ = mlstm_bidirectional(qm, km, vm, gates_x, st_f, st_b, True)
        y_m = mlstm_merge(hm, om, mlstm_norm[l])
        y_a = window_attention(apply_rope_2(qa, cos, sin) * attn_scale, apply_rope_2(ka, cos, sin), va,
                               ka_c, va_c, attn_sink[l])
        x = x + g_a * (jnp.concatenate([y_m, y_a], axis=-1) @ w_out[l])
        x = x + g_f * conv_glu(modulate(rmsnorm_2(x, norm_ffn[l]), sh_f, sc_f),
                               w_up[l], ffn_conv_w[l], ffn_conv_b[l], w_down[l])

        if not last:
            y_mc = mlstm_merge(hm_c, om_c, mlstm_norm[l])
            y_ac = context_attention(qa_c * attn_scale, ka_c, va_c, attn_sink[l])
            ctx = ctx + cg_a * (jnp.concatenate([y_mc, y_ac], axis=-1) @ w_out[l])
            ctx = ctx + cg_f * conv_glu(modulate(rmsnorm_2(ctx, norm_ffn[l]), csh_f, csc_f),
                                        w_up[l], ffn_conv_w[l], ffn_conv_b[l], w_down[l])
    return rmsnorm_2(x, final_norm)


def setup_inputs(seed=0):
    out = dict(first_inputs(seed))
    for name, value in second_inputs(seed + 1).items():
        if name != "x":
            out[name + "_2"] = value
    return out


def reference(
    x, c, ada_w, ada_b, mix_norm_g, ffn_norm_g, w_in, w_out, diff_lambda, diff_norm_g,
    mla_q_norm_g, mla_kv_norm_g, mla_w_uq, mla_w_ukv, band_rel_bias, ffn_w1, ffn_w3, ffn_w2,
    moe_router, moe_w1, moe_w3, moe_w2, final_norm_g, c_2, ctx_2, c_ctx_2, w_ada_2, b_ada_2,
    norm_mix_2, norm_ffn_2, w_in_2, gate_b_2, qk_conv_w_2, qk_conv_b_2, mlstm_norm_2,
    attn_sink_2, w_out_2, w_up_2, ffn_conv_w_2, ffn_conv_b_2, w_down_2, final_norm_2,
):
    x = first_block(
        x, c, ada_w, ada_b, mix_norm_g, ffn_norm_g, w_in, w_out, diff_lambda, diff_norm_g,
        mla_q_norm_g, mla_kv_norm_g, mla_w_uq, mla_w_ukv, band_rel_bias, ffn_w1, ffn_w3, ffn_w2,
        moe_router, moe_w1, moe_w3, moe_w2, final_norm_g,
    )
    return second_block(
        x, c_2, ctx_2, c_ctx_2, w_ada_2, b_ada_2, norm_mix_2, norm_ffn_2, w_in_2, gate_b_2,
        qk_conv_w_2, qk_conv_b_2, mlstm_norm_2, attn_sink_2, w_out_2, w_up_2, ffn_conv_w_2,
        ffn_conv_b_2, w_down_2, final_norm_2,
    )


_drawn_inputs = setup_inputs


def setup_inputs(seed=0):
    import zlib

    import numpy as np

    out = dict(_drawn_inputs(seed))
    spreads = {}
    factors = {'diff_lambda': 3.683,
     'mla_q_norm_g': 8.0,
     'mla_kv_norm_g': 3.783,
     'band_rel_bias': 3.748,
     'norm_mix_2': 8.0,
     'norm_ffn_2': 8.0,
     'qk_conv_b_2': 200.0,
     'mlstm_norm_2': 30.576,
     'attn_sink_2': 8.0,
     'ffn_conv_b_2': 23.379}
    for name, (base, spread) in spreads.items():
        noise = np.random.default_rng([zlib.crc32(name.encode()), seed]).standard_normal(out[name].shape)
        drawn = base * np.exp(spread * noise) if base else spread * noise
        out[name] = jnp.asarray(drawn.astype(out[name].dtype))
    for name, factor in factors.items():
        out[name] = (out[name] * factor).astype(out[name].dtype)
    return out
```

```python
import numpy as np
from contextlib import ExitStack

import concourse.bass as bass
from concourse import mybir

F32 = mybir.dt.float32
ALU = mybir.AluOpType
ACT = mybir.ActivationFunctionType
AX = mybir.AxisListType

P = 128
D = 1024
KT = D // P
L = 256
NT = L // P
EPS = 1e-6
NEG = -1e30
TAKEN = -3e38
HEADS = 4
GROUP = 256
FF = 2816
FFE = 3584
NE = 8
TOPK = 64
CHUNK = 64
RING = 7
SLOT = 2048
CT = 2
CW = CT * P
MODS = 6 * D // P

CONST_A = [("ident", 128), ("ones", 128), ("flip", 128), ("mask", 512), ("alibi", 2048), ("cos96", 256),
           ("sin96", 256), ("perm96", 96), ("cos32", 256), ("sin32", 256), ("perm32", 32), ("pick", 1024)]
CONST_B = [("upto_f", 512), ("upto_b", 512), ("past_f", 512), ("past_b", 512), ("mask_f", 512), ("mask_b", 512),
           ("window", 1024), ("cosA", 256), ("sinA", 256), ("permA", 64)]
VECS = [("c", 8), ("c2", 16), ("ada_b0", 48), ("ada_b1", 48), ("ada_b2", 48), ("mix_g0", 8), ("mix_g1", 8),
        ("ffn_g0", 8), ("ffn_g1", 8), ("final_g", 8), ("mix_g2", 8), ("ffn_g2", 8), ("final_g2", 8),
        ("qn_g0", 2), ("qn_g1", 2), ("kvn_g0", 1), ("kvn_g1", 1), ("conv_w", 24), ("conv_b", 8),
        ("mlstm_g", 4), ("fconv_w", 66), ("fconv_b", 22)]
ROWS = [("lam0", 128), ("lam1", 128), ("dng0", 64), ("dng1", 64), ("gate_b", 16), ("sink", 8)]


def columns(table):
    at, out = 0, {}
    for name, width in table:
        out[name] = (at, width)
        at += width
    return out, at


COLS_A, WIDTH_A = columns(CONST_A)
COLS_B, WIDTH_B = columns(CONST_B)
COLS_V, WIDTH_V = columns(VECS)
COLS_R, WIDTH_R = columns(ROWS)


class Stream:

    def __init__(self, nc, ctx):
        self.slots = [ctx.enter_context(nc.sbuf_tensor(f"ring{i}", [P, SLOT], F32)) for i in range(RING)]
        self.loaded = [ctx.enter_context(nc.semaphore(f"loaded{i}")) for i in range(RING)]
        self.freed = [ctx.enter_context(nc.semaphore(f"freed{i}")) for i in range(RING)]
        self.items = []
        self.arrival = []
        self.total = [0] * RING
        self.issued = 0
        self.taken = 0

    def add(self, *parts):
        s = len(self.items) % RING
        self.total[s] += 16 * len(parts)
        self.items.append(parts)
        self.arrival.append(self.total[s])

    def take(self):
        self.taken += 1
        return self.taken - 1

    def wait(self, eng, n):
        eng.wait_ge(self.loaded[n % RING], self.arrival[n])

    def free(self, ins, n):
        ins.then_inc(self.freed[n % RING], 1)

    def view(self, n, kt, width, at=0):
        return self.slots[n % RING][:, at:at + kt * width].rearrange("p (k w) -> p k w", k=kt)

    def issue_one(self, sp, n):
        if n >= RING:
            sp.wait_ge(self.freed[n % RING], n // RING)
        for at, kt, width, src in self.items[n]:
            sp.dma_start(self.view(n, kt, width, at), src).then_inc(self.loaded[n % RING], 16)

    def issue(self, sp):
        end = min(self.taken + RING, len(self.items))
        while self.issued < end:
            self.issue_one(sp, self.issued)
            self.issued += 1


class Kit:

    def signals(self, phase):
        if self.old is not None:
            self.old.ctx.close()
        self.old, self.now = self.now, Signals(self.nc, phase)
        return self.now

    def clear_old(self, pool):
        if self.old is not None:
            for sem in self.old.made.values():
                pool.sem_clear(sem)


class Signals:

    def __init__(self, nc, phase):
        self.nc, self.ctx, self.phase, self.made = nc, ExitStack(), phase, {}

    def __call__(self, name):
        if name not in self.made:
            self.made[name] = self.ctx.enter_context(self.nc.semaphore(f"{self.phase}_{name}"))
        return self.made[name]


class Link:

    def __init__(self, eng, sem):
        self.eng, self.sem, self.n = eng, sem, 0

    def __call__(self, ins):
        self.n += 1
        ins.then_inc(self.sem, 1)
        self.eng.wait_ge(self.sem, self.n)


def bcast(ap, n):
    return ap.unsqueeze(1).to_broadcast([ap.shape[0], n, ap.shape[1]])


def spread(ap, n):
    return ap.unsqueeze(2).to_broadcast([ap.shape[0], ap.shape[1], n])


def w_tiles(w, c0, width):
    return w.rearrange("(k p) n -> p k n", p=P)[:, :, c0:c0 + width]


def plan_stream(K, A):
    st = K.stream

    def cols(w, c0, width):
        kt = w.shape[0] // P
        st.add((0, kt, width, w_tiles(w, c0, width)))

    def ada(w):
        for j in range(0, 6 * D, CW):
            cols(w, j, CW)

    def mixer(l):
        w = A["w_in"][l]
        for c0, c1 in IN_ITEMS:
            cols(w, c0, c1 - c0)
        st.add((0, 2, 384, A["mla_w_uq"][l].rearrange("(k p) n -> p k n", p=P)),
               (768, 1, 512, A["mla_w_ukv"][l].rearrange("(k p) n -> p k n", p=P)))
        for c0 in range(0, D, CW):
            cols(A["w_out"][l], c0, CW)

    def ffn(w1, w3, w2, o3, ff):
        for c0 in range(0, ff, CW):
            cols(w1, c0, CW)
            cols(w3, o3 + c0, CW)
            st.add((0, CT, D, w2.rearrange("(k p) n -> p k n", p=P)[:, c0 // P:c0 // P + CT, :]))

    ada(A["ada_w"][0])
    mixer(0)
    ffn(A["ffn_w1"][0], A["ffn_w3"][0], A["ffn_w2"][0], 0, FF)
    ada(A["ada_w"][1])
    mixer(1)
    K.moe_first = len(st.items)
    for e in range(NE):
        ffn(A["moe_w1"][0, e], A["moe_w3"][0, e], A["moe_w2"][0, e], 0, FFE)
    ada(A["w_ada_2"][0])
    w = A["w_in_2"][0]
    for c0 in (0, 256, 512, 768, 1024, 1280, 1536, 1792, 2064, 2320, 2576):
        cols(w, c0, CW)
    cols(w, 2048, 16)
    for c0 in range(0, D, CW):
        cols(A["w_out_2"][0], c0, CW)
    ffn(A["w_up_2"][0], A["w_up_2"][0], A["w_down_2"][0], FF, FF)


IN_ITEMS = [(0, 256), (256, 512), (512, 768), (768, 1024), (1024, 1184), (1184, 1440), (1440, 1696), (1696, 1952),
            (1952, 2208), (2208, 2248), (2248, 2504), (2504, 2760), (2760, 3016)]



def phase_load(K, A):
    nc = K.nc
    with ExitStack() as ctx:
        s = K.signals("load")
        with nc.Block() as block:
            @block.scalar
            def _(act):
                act.dma_start(K.vec[:], A["vecs"]).then_inc(s("vec"), 16)
                act.dma_start(K.row[:], A["rows"].partition_broadcast(P) if False else
                              bass.AP(tensor=A["rows"].tensor, offset=0, ap=[[0, P], [1, WIDTH_R]])).then_inc(s("in"), 16)
                act.dma_start(K.ca[:], A["const_a"]).then_inc(s("in"), 16)
                act.dma_start(K.xT[:], A["xT"].rearrange("(k p) t -> p k t", p=P)).then_inc(s("in"), 16)
                act.wait_ge(s("vec"), 16)
                act.activation(K.silu_c[:, 0:8], K.v("c"), ACT.Silu).then_inc(s("silu"), 1)
                act.activation(K.silu_c[:, 8:24], K.v("c2"), ACT.Silu).then_inc(s("silu"), 1)
                act.wait_ge(s("in"), 48)
                act.wait_ge(s("silu"), 2)

            @block.gpsimd
            def _(pool):
                K.clear_old(pool)

            @block.sync
            def _(sp):
                K.stream.issue(sp)


def phase_ada(K, l):
    nc, st = K.nc, K.stream
    nv = 2 if l == 2 else 1
    cs = K.silu_c[:, 8:24] if l == 2 else K.silu_c[:, 0:8]
    cs = cs.rearrange("p (k v) -> p k v", v=nv)
    ps = K.ps[:, 0, 0:MODS * nv]
    with ExitStack() as ctx:
        s = K.signals(f"ada{l}")
        with nc.Block() as block:
            @block.tensor
            def _(pe):
                for j in range(MODS // CT):
                    n = st.take()
                    st.wait(pe, n)
                    w = st.view(n, KT, CW)
                    for m in range(CT):
                        col = (CT * j + m) * nv
                        for k in range(KT):
                            mm = pe.matmul(ps[:, col:col + nv], w[:, k, m * P:(m + 1) * P], cs[:, k, :],
                                           start=(k == 0), stop=(k == KT - 1))
                    st.free(mm, n)
                mm = pe.matmul(K.ps[:, 1, 0:1], K.a("ident"), K.a("ones")[:, 0:1], start=True, stop=True)
                mm.then_inc(s("mod"), 1)

            @block.vector
            def _(dve):
                link = Link(dve, s("chain"))
                dve.wait_ge(s("mod"), 1)
                pv = ps.rearrange("p (j v) -> p v j", v=nv)
                for v in range(nv):
                    dve.tensor_tensor(K.mod[:, v, :], pv[:, v, :], K.v(f"ada_b{l}"), ALU.add)
                link(dve.memset(K.scratch1[:], 1.0))
                dve.tensor_scalar(K.gain[:, 0, :], K.mod[:, 0, 8:16], 1.0, None, ALU.add)
                dve.tensor_scalar(K.gain[:, 1, :], K.mod[:, 0, 32:40], 1.0, None, ALU.add)
                if nv == 2:
                    dve.tensor_scalar(K.gain[:, 2, :], K.mod[:, 1, 8:16], 1.0, None, ALU.add)
                link(dve.memset(K.scratch1[:], 0.0))
                dve.tensor_tensor(K.gain[:, 0, :], K.gain[:, 0, :], K.v(f"mix_g{l}"), ALU.mult)
                dve.tensor_tensor(K.gain[:, 1, :], K.gain[:, 1, :], K.v(f"ffn_g{l}"), ALU.mult)
                if nv == 2:
                    dve.tensor_tensor(K.gain[:, 2, :], K.gain[:, 2, :], K.v(f"mix_g{l}"), ALU.mult)

            @block.gpsimd
            def _(pool):
                K.clear_old(pool)

            @block.sync
            def _(sp):
                st.issue(sp)


def phase_norm(K, name, src, dst, gain, shift, out=None):
    nc = K.nc
    with ExitStack() as ctx:
        s = K.signals(name)
        sq = ctx.enter_context(nc.sbuf_tensor(f"{name}_sq", [P, KT, L], F32))
        rs = ctx.enter_context(nc.sbuf_tensor(f"{name}_rs", [P, 3, L], F32))
        with nc.Block() as block:
            @block.scalar
            def _(act):
                for k in range(KT):
                    act.activation(sq[:, k, :], src[:, k, :], ACT.Square).then_inc(s("sq"), 1)
                act.wait_ge(s("ms"), 1)
                act.activation(rs[:, 1, :], rs[:, 0, :], ACT.Sqrt).then_inc(s("root"), 1)
                if out is not None:
                    act.wait_ge(s("y"), 1)
                    act.dma_start(out, dst[:]).then_inc(s("stored"), 16)
                    act.wait_ge(s("stored"), 16)

            @block.tensor
            def _(pe):
                for k in range(KT):
                    pe.wait_ge(s("sq"), k + 1)
                    mm = pe.matmul(K.ps[:, 0, 0:L], K.a("ones"), sq[:, k, :], start=(k == 0), stop=(k == KT - 1))
                mm.then_inc(s("sum"), 1)

            @block.vector
            def _(dve):
                link = Link(dve, s("chain"))
                dve.wait_ge(s("sum"), 1)
                dve.tensor_scalar(rs[:, 0, :], K.ps[:, 0, 0:L], 1.0 / D, EPS, ALU.mult, ALU.add).then_inc(s("ms"), 1)
                dve.wait_ge(s("root"), 1)
                link(dve.reciprocal(rs[:, 2, :], rs[:, 1, :]))
                dve.wait_ge(s("sq"), KT)
                link(dve.tensor_tensor(sq[:], src[:], bcast(rs[:, 2, :], KT), ALU.mult))
                for k in range(KT):
                    if shift is None:
                        y = dve.tensor_scalar(dst[:, k, :], sq[:, k, :], gain[:, k:k + 1], None, ALU.mult)
                    else:
                        y = dve.tensor_scalar(dst[:, k, :], sq[:, k, :], gain[:, k:k + 1], shift[:, k:k + 1],
                                              ALU.mult, ALU.add)
                y.then_inc(s("y"), 1)

            @block.gpsimd
            def _(pool):
                K.clear_old(pool)

            @block.sync
            def _(sp):
                K.stream.issue(sp)


def phase_project(K, name, jobs):
    nc, st = K.nc, K.stream
    with ExitStack() as ctx:
        s = K.signals(name)
        done = [s("evicted_act"), s("evicted_dve")]
        with nc.Block() as block:
            @block.tensor
            def _(pe):
                have = -1
                for j, (n, lhsT, rhs, kt, rows, width, _, last) in enumerate(jobs):
                    if n > have:
                        st.wait(pe, n)
                        have = n
                    if j >= 4:
                        pe.wait_ge(done[j % 2], (j - 4) // 2 + 1)
                    for k in range(kt):
                        mm = pe.matmul(K.ps[0:rows, j % 4, 0:width], lhsT(k), rhs(k), start=(k == 0), stop=(k == kt - 1))
                    mm.then_inc(s("product"), 1)
                    if last:
                        pe.wait_ge(s("product"), j + 1)
                        pe.sem_inc(st.freed[n % RING], 1)

            @block.scalar
            def _(act):
                for j, job in enumerate(jobs):
                    if j % 2 == 0:
                        act.wait_ge(s("product"), j + 1)
                        for out, part, func in job[6]:
                            ev = act.activation(out, part(K.ps[:, j % 4, :]), func or ACT.Copy)
                        ev.then_inc(done[0], 1)

            @block.vector
            def _(dve):
                for j, job in enumerate(jobs):
                    if j % 2 == 1:
                        dve.wait_ge(s("product"), j + 1)
                        for out, part, func in job[6]:
                            assert func is None
                            ev = dve.tensor_copy(out, part(K.ps[:, j % 4, :]))
                        ev.then_inc(done[1], 1)

            @block.gpsimd
            def _(pool):
                K.clear_old(pool)

            @block.sync
            def _(sp):
                st.issue(sp)


def feature_job(K, n, c0, rows, hT, outs, w, last=False, func=None):
    ev = [(dst, (lambda b, r0=r0, r=r: b[r0:r0 + r, 0:L]), func) for dst, r0, r in outs]
    return (n, lambda k: w[:, k, c0:c0 + rows], lambda k: hT[:, k, :], KT, rows, L, ev, last)


def token_job(K, n, c0, width, hT, T, dst, w, last=False, shape=None):
    if shape is None:
        part = lambda b: b[:, 0:width]
    else:
        part = lambda b: b[:, 0:width].rearrange("p (a e) -> p a e", a=shape)
    return (n, lambda k: hT[:, k, T * P:(T + 1) * P], lambda k: w[:, k, c0:c0 + width], KT, P, width,
            [(dst, part, None)], last)


def mixer_projections(K, B):
    st, hT = K.stream, K.hT
    jobs = []

    def item(width):
        n = st.take()
        return n, st.view(n, KT, width)

    def split(dst, first, size):
        return [(dst[:, first + i, :], i * size, size) for i in range(P // size)]

    def split_pair(dst, size):
        n, w = item(CW)
        for i in range(CT):
            jobs.append(feature_job(K, n, i * P, P, hT, split(dst, (P // size) * i, size), w, last=(i == 1)))

    def values(g):
        n, w = item(CW)
        for T in range(NT):
            jobs.append(token_job(K, n, 0, GROUP, hT, T, B.v[:, g, T, :], w, last=(T == 1)))

    split_pair(B.qa, 32)
    split_pair(B.ka, 32)
    values(0)
    n, w = item(CW)
    for i in range(CT):
        jobs.append(feature_job(K, n, i * P, P, hT, [(B.qdT[:, i, :], 0, P)], w, last=(i == 1)))
    n, w = item(160)
    jobs.append(feature_job(K, n, 0, P, hT, [(B.kvdT[:, 0, :], 0, P)], w))
    jobs.append(feature_job(K, n, P, 32, hT, [(B.krT[:, 0, :], 0, 32)], w, last=True))
    split_pair(B.qc, 64)
    split_pair(B.kc, 64)
    values(2)
    split_pair(B.qi, 32)
    n, w = item(40)
    jobs.append(feature_job(K, n, 0, 32, hT, [(B.ki[:, 0, :], 0, 32)], w))
    for T in range(NT):
        jobs.append(token_job(K, n, 32, 8, hT, T, B.wi[:, T, :], w, last=(T == 1)))
    split_pair(B.qd, 64)
    split_pair(B.kd, 64)
    values(3)
    return jobs


def phase_latent(K, l, B):
    nc, st = K.nc, K.stream
    lam_init = 0.8 - 0.6 * float(np.exp(-0.3 * l))
    with ExitStack() as ctx:
        s = K.signals(f"lat{l}")

        def sb(name, shape):
            return ctx.enter_context(nc.sbuf_tensor(f"lat{l}_{name}", shape, F32))

        sq = sb("sq", [P, 3, L])
        rs = sb("rs", [P, 2, 3, L])
        qraw = sb("qraw", [96, 4, L])
        qn = sb("qn", [P, 3, L])
        rot = sb("rot", [96, 4, L])
        lam = sb("lam", [P, 2, 32])
        lam2 = sb("lam2", [P, 4])
        rev = sb("rev", [P, 2, HEADS, L])
        n = st.take()
        wq = st.view(n, 2, 384)
        wkv = st.view(n, 1, 512, 768)[:, 0, :].rearrange("p (h c) -> p h c", h=HEADS)
        with nc.Block() as block:
            @block.scalar
            def _(act):
                for T in range(NT):
                    act.dma_start(rev[:, T], bass.AP(tensor=K.band.tensor, offset=l * HEADS * 511 + P * (1 - T),
                                                     ap=[[1, P], [511, HEADS], [1, L]])).then_inc(s("band"), 16)
                act.activation(sq[:, 0:2, :], B.qdT[:], ACT.Square)
                act.activation(sq[:, 2:3, :], B.kvdT[:], ACT.Square).then_inc(s("sq"), 1)
                act.wait_ge(s("ms"), 1)
                act.activation(rs[:, 1, 0:2, :], rs[:, 0, 0:2, :], ACT.Sqrt).then_inc(s("root"), 1)
                act.wait_ge(s("lamdot"), 1)
                act.activation(lam2[:, 2:4], lam2[:, 0:2], ACT.Exp).then_inc(s("lamexp"), 1)
                for h in range(HEADS):
                    act.wait_ge(s("q"), 2 * (h // 2) + 2)
                    act.activation(qraw[:, h, :], K.ps[0:96, 2 + h // 2, (h % 2) * L:(h % 2 + 1) * L], ACT.Copy)\
                       .then_inc(s("qraw"), 1)
                for h in range(HEADS):
                    act.wait_ge(s("kv"), h + 1)
                    act.activation(B.kb[0:64, h, :], K.ps[0:64, 4 + h % 2, 0:L], ACT.Copy).then_inc(s("kev"), 1)
                for T in range(NT):
                    act.wait_ge(s("kv"), HEADS + 1 + T)
                    act.activation(B.v[:, 1, T, :], K.ps[:, 4 + T, 0:GROUP], ACT.Copy)

            @block.tensor
            def _(pe):
                pe.wait_ge(s("sq"), 1)
                for k in range(2):
                    pe.matmul(K.ps[:, 0, 0:L], K.a("ones"), sq[:, k, :], start=(k == 0), stop=(k == 1))
                pe.matmul(K.ps[:, 1, 0:L], K.a("ones"), sq[:, 2, :], start=True, stop=True)
                pe.matmul(K.ps[0:32, 1, L:2 * L], K.a("perm32")[0:32], B.krT[:, 0, :], start=True, stop=True)\
                    .then_inc(s("sum"), 1)
                pe.wait_ge(s("band"), 16 * NT)
                for T in range(NT):
                    for half in range(2):
                        pe.matmul(K.ps[:, 6 + half, :], K.a("flip"), rev[:, T, 2 * half:2 * half + 2, :],
                                  start=True, stop=True).then_inc(s("bias"), 1)
                    if T == 0:
                        pe.wait_ge(s("biased"), 2)
                st.wait(pe, n)
                pe.wait_ge(s("qn"), 1)
                for h in range(HEADS):
                    for k in range(2):
                        mm = pe.matmul(K.ps[0:96, 2 + h // 2, (h % 2) * L:(h % 2 + 1) * L],
                                       wq[:, k, h * 96:(h + 1) * 96], qn[:, k, :], start=(k == 0), stop=(k == 1))
                    mm.then_inc(s("q"), 1)
                for h in range(HEADS):
                    if h >= 2:
                        pe.wait_ge(s("kev"), h - 1)
                    pe.matmul(K.ps[0:64, 4 + h % 2, 0:L], wkv[:, h, 0:64], qn[:, 2, :], start=True, stop=True)\
                        .then_inc(s("kv"), 1)
                for T in range(NT):
                    pe.wait_ge(s("kev"), 3 + T)
                    mm = pe.matmul(K.ps[:, 4 + T, 0:GROUP], qn[:, 2, T * P:(T + 1) * P], wkv[:, :, 64:128],
                                   start=True, stop=True)
                    mm.then_inc(s("kv"), 1)
                for h in range(HEADS):
                    pe.wait_ge(s("qraw"), h + 1)
                    pe.wait_ge(s("biased"), 4)
                    pe.matmul(K.ps[0:96, 6 + h // 2, (h % 2) * L:(h % 2 + 1) * L], K.a("perm96")[0:96], qraw[:, h, :],
                              start=True, stop=True).then_inc(s("qrot"), 1)
                pe.wait_ge(s("qrot"), HEADS)
                pe.sem_inc(st.freed[n % RING], 1)

            @block.vector
            def _(dve):
                link = Link(dve, s("chain"))
                dve.wait_ge(s("sum"), 1)
                dve.tensor_scalar(rs[:, 0, 0, :], K.ps[:, 0, 0:L], 1.0 / 256, EPS, ALU.mult, ALU.add)
                dve.tensor_scalar(rs[:, 0, 1, :], K.ps[:, 1, 0:L], 1.0 / 128, EPS, ALU.mult, ALU.add)\
                    .then_inc(s("ms"), 1)
                lv = K.r(f"lam{l}").rearrange("p (a b e) -> p a b e", a=2, b=2)
                link(dve.tensor_tensor(lam[:], lv[:, :, 0, :], lv[:, :, 1, :], ALU.mult))
                dve.tensor_reduce(lam2[:, 0:2], lam[:], AX.X, ALU.add).then_inc(s("lamdot"), 1)
                link(dve.tensor_tensor(rot[0:32, 0, :], K.ps[0:32, 1, L:2 * L], K.a("sin32")[0:32], ALU.mult))
                link(dve.tensor_tensor(rot[0:32, 1, :], B.krT[:, 0, :], K.a("cos32")[0:32], ALU.mult))
                link(dve.tensor_tensor(rot[0:32, 2, :], rot[0:32, 0, :], rot[0:32, 1, :], ALU.add))
                link(dve.tensor_copy(B.kb[64:96, :, :], bcast(rot[0:32, 2, :], HEADS)))
                dve.wait_ge(s("root"), 1)
                link(dve.reciprocal(rs[:, 0, 0:2, :], rs[:, 1, 0:2, :]))
                for k in range(3):
                    g = K.v(f"qn_g{l}")[:, k:k + 1] if k < 2 else K.v(f"kvn_g{l}")
                    src = B.qdT[:, k, :] if k < 2 else B.kvdT[:, 0, :]
                    nn = dve.scalar_tensor_tensor(out=qn[:, k, :], in0=src, scalar=g, in1=rs[:, 0, k // 2, :],
                                                  op0=ALU.mult, op1=ALU.mult)
                nn.then_inc(s("qn"), 1)
                dve.wait_ge(s("lamexp"), 1)
                link(dve.tensor_tensor(K.lam[:, 0:1], lam2[:, 2:3], lam2[:, 3:4], ALU.subtract))
                dve.tensor_scalar(K.lam[:, 1:2], K.lam[:, 0:1], -1.0, -lam_init, ALU.mult, ALU.add)
                for T in range(NT):
                    for half in range(2):
                        dve.wait_ge(s("bias"), 2 * T + half + 1)
                        dve.tensor_tensor(B.band[:, T, 2 * half:2 * half + 2, :],
                                          K.ps[:, 6 + half, :].rearrange("p (h t) -> p h t", h=2),
                                          bcast(K.mask(T), 2), ALU.add).then_inc(s("biased"), 1)
                for h in range(HEADS):
                    dve.wait_ge(s("qrot"), 2 * (h // 2) + 2)
                    link(dve.tensor_tensor(rot[:, 3, :], K.ps[0:96, 6 + h // 2, (h % 2) * L:(h % 2 + 1) * L],
                                           K.a("sin96")[0:96], ALU.mult))
                    link(dve.tensor_tensor(B.qb[:, h, :], qraw[:, h, :], K.a("cos96")[0:96], ALU.mult))
                    link(dve.tensor_tensor(B.qb[:, h, :], B.qb[:, h, :], rot[:, 3, :], ALU.add))

            @block.gpsimd
            def _(pool):
                K.clear_old(pool)

            @block.sync
            def _(sp):
                st.issue(sp)


def phase_index(K, l, B):
    nc = K.nc
    NH = 8
    with ExitStack() as ctx:
        s = K.signals(f"idx{l}")

        def sb(name, shape):
            return ctx.enter_context(nc.sbuf_tensor(f"idx{l}_{name}", shape, F32))

        relu = sb("relu", [P, 4, L])
        score = sb("score", [P, NT, 2, L])
        top = sb("top", [P, NT, 8])
        with nc.Block() as block:
            @block.tensor
            def _(pe):
                for u in range(NT * NH):
                    T, h = u % NT, u // NT
                    if u >= 4:
                        pe.wait_ge(s("relu"), u - 3)
                    pe.matmul(K.ps[:, u % 4, 0:L], B.qi[:, h, T * P:(T + 1) * P], B.ki[:, 0, :], start=True, stop=True)\
                        .then_inc(s("dot"), 1)

            @block.scalar
            def _(act):
                for u in range(NT * NH):
                    act.wait_ge(s("dot"), u + 1)
                    if u >= 4:
                        act.wait_ge(s("added"), u - 3)
                    act.activation(relu[:, u % 4, :], K.ps[:, u % 4, 0:L], ACT.Relu, scale=1.0 / 16)\
                       .then_inc(s("relu"), 1)

            @block.vector
            def _(dve):
                link = Link(dve, s("chain"))
                for u in range(NT * NH):
                    T, h = u % NT, u // NT
                    dve.wait_ge(s("relu"), u + 1)
                    if u >= NT:
                        dve.wait_ge(s("added"), u - NT + 1)
                    acc = K.mask(T) if h == 0 else score[:, T, h % 2, :]
                    dve.scalar_tensor_tensor(out=score[:, T, (h + 1) % 2, :], in0=relu[:, u % 4, :],
                                             scalar=B.wi[:, T, h:h + 1], in1=acc, op0=ALU.mult, op1=ALU.add)\
                        .then_inc(s("added"), 1)
                dve.wait_ge(s("added"), NT * NH)
                for r in range(TOPK // 8):
                    for T in range(NT):
                        a, b = score[:, T, r % 2, :], score[:, T, (r + 1) % 2, :]
                        link(dve.max(top[:, T, :], a))
                        link(dve.match_replace(b, top[:, T, :], a, TAKEN))
                for T in range(NT):
                    link(dve.tensor_scalar(score[:, T, 1, :], score[:, T, 0, :], TAKEN, NEG, ALU.not_equal, ALU.mult))
                    dve.tensor_tensor(B.sparse[:, T], K.alibi(T), bcast(score[:, T, 1, :], HEADS), ALU.add)

            @block.gpsimd
            def _(pool):
                K.clear_old(pool)

            @block.sync
            def _(sp):
                K.stream.issue(sp)


def phase_attention(K, name, B, batches, nm, nb, extra=0):
    nc = K.nc
    W = nb * P
    NB = len(batches)
    WS = W + extra
    with ExitStack() as ctx:
        s = K.signals(name)

        def sb(nm_, shape):
            return ctx.enter_context(nc.sbuf_tensor(f"{name}_{nm_}", shape, F32))

        S = sb("S", [P, 2, nm, WS])
        E = S
        PT = sb("PT", [P, 2, nm * nb, P])
        mx = sb("mx", [P, NB, nm])
        sm = sb("sm", [P, NB, nm])
        rc = sb("rc", [P, NB, nm])

        def scores(b, m):
            at = m * W
            return K.ps[:, 2 * (b % 2) + at // 512, at % 512:at % 512 + W]

        def all_scores(b):
            return K.ps[:, 2 * (b % 2):2 * (b % 2) + 2, :].rearrange("p a (m w) -> p (a m) w", w=W)

        def turned(i):
            return K.ps[:, 4 + i // 4, (i % 4) * P:(i % 4 + 1) * P]

        with nc.Block() as block:
            @block.tensor
            def _(pe):
                def do_scores(b):
                    if b >= 2:
                        pe.wait_ge(s("biased"), b - 1)
                    for m in range(nm):
                        for q, k, c0, c1 in batches[b][0](m):
                            mm = pe.matmul(scores(b, m)[:, c0:c1], q, k, start=True, stop=True)
                    mm.then_inc(s("scores"), 1)

                def do_turn(b):
                    pe.wait_ge(s("exp"), nm * (b + 1))
                    if b >= 1:
                        pe.wait_ge(s("turned_out"), 2 * b)
                    for i in range(nm * nb):
                        mm = pe.transpose(turned(i), E[:, b % 2, i // nb, (i % nb) * P:(i % nb + 1) * P], K.a("ident"))
                        if i % 4 == 3:
                            mm.then_inc(s("turned"), 1)

                def do_pv(b):
                    pe.wait_ge(s("turned_out"), 2 * b + 2)
                    if b >= 2:
                        pe.wait_ge(s("out"), b - 1)
                    for m in range(nm):
                        for kb in range(nb):
                            mm = pe.matmul(K.ps[:, 6 + b % 2, m * 64:(m + 1) * 64], PT[:, b % 2, m * nb + kb, :],
                                           batches[b][1](m, kb), start=(kb == 0), stop=(kb == nb - 1))
                    mm.then_inc(s("pv"), 1)

                do_scores(0)
                for b in range(NB):
                    if b + 1 < NB:
                        do_scores(b + 1)
                    do_turn(b)
                    do_pv(b)

            @block.scalar
            def _(act):
                def copy_out(b):
                    act.wait_ge(s("turned"), 2 * b + 1)
                    if b >= 2:
                        act.wait_ge(s("pv"), b - 1)
                    act.activation(PT[:, b % 2, 0:4, :], K.ps[:, 4, :].rearrange("p (i q) -> p i q", i=4), ACT.Copy)\
                       .then_inc(s("turned_out"), 1)

                for b in range(NB):
                    act.wait_ge(s("max"), b + 1)
                    if b >= 2:
                        act.wait_ge(s("turned"), 2 * (b - 1))
                    for m in range(nm):
                        act.activation(E[:, b % 2, m, :], S[:, b % 2, m, :], ACT.Exp, bias=mx[:, b, m:m + 1],
                                       accum_out=sm[:, b, m:m + 1]).then_inc(s("exp"), 1)
                    if b >= 1:
                        copy_out(b - 1)
                copy_out(NB - 1)

            @block.vector
            def _(dve):
                link = Link(dve, s("chain"))

                def do_bias(b):
                    dve.wait_ge(s("scores"), b + 1)
                    if b >= 2:
                        dve.wait_ge(s("exp"), nm * (b - 1))
                    out = S[:, b % 2, :, 0:W]
                    dve.scalar_tensor_tensor(out=out, in0=all_scores(b), scalar=batches[b][3], in1=batches[b][2],
                                             op0=ALU.mult, op1=ALU.add).then_inc(s("biased"), 1)
                    if extra:
                        dve.tensor_copy(S[:, b % 2, :, W:WS], batches[b][5]).then_inc(s("extra"), 1)
                        dve.wait_ge(s("extra"), b + 1)
                    dve.wait_ge(s("biased"), b + 1)
                    dve.tensor_reduce(mx[:, b, :], S[:, b % 2, :, :], AX.X, ALU.max, negate=True).then_inc(s("max"), 1)

                def do_out(b):
                    dve.wait_ge(s("turned"), 2 * b + 2)
                    if b >= 2:
                        dve.wait_ge(s("pv"), b - 1)
                    dve.tensor_copy(PT[:, b % 2, 4:8, :], K.ps[:, 5, :].rearrange("p (i q) -> p i q", i=4))\
                        .then_inc(s("turned_out"), 1)
                    link(dve.reciprocal(rc[:, b, :], sm[:, b, :]))
                    dve.wait_ge(s("pv"), b + 1)
                    dve.tensor_tensor(batches[b][4], K.ps[:, 6 + b % 2, 0:nm * 64].rearrange("p (m e) -> p m e", m=nm),
                                      spread(rc[:, b, :], 64), ALU.mult).then_inc(s("out"), 1)

                do_bias(0)
                for b in range(NB):
                    if b + 1 < NB:
                        do_bias(b + 1)
                    do_out(b)

            @block.gpsimd
            def _(pool):
                K.clear_old(pool)

            @block.sync
            def _(sp):
                K.stream.issue(sp)


def mixer_batches(K, B):
    out = []

    def heads(ap):
        return ap.rearrange("p (m e) -> p m e", m=HEADS)

    def batch(q, k, g, T, bias, scale, dst):
        return (lambda m: [(q(m)[:, T * P:(T + 1) * P], k(m), 0, L)],
                lambda m, kb: B.v[:, g, kb, m * 64:(m + 1) * 64], bias, scale, heads(dst), None)

    for T in range(NT):
        for c in range(2):
            out.append(batch(lambda m, c=c: B.qa[:, 2 * m + c, :], lambda m, c=c: B.ka[:, 2 * m + c, :], 0, T,
                             K.alibi(T), 32 ** -0.5, B.o[:, T, 0:GROUP] if c == 0 else B.o1[:, T, :]))
        out.append(batch(lambda m: B.qb[:, m, :], lambda m: B.kb[:, m, :], 1, T, bcast(K.mask(T), HEADS),
                         96 ** -0.5, B.o[:, T, GROUP:2 * GROUP]))
        out.append(batch(lambda m: B.qd[:, m, :], lambda m: B.kd[:, m, :], 3, T, B.band[:, T], 64 ** -0.5,
                         B.o[:, T, 3 * GROUP:4 * GROUP]))
        out.append(batch(lambda m: B.qc[:, m, :], lambda m: B.kc[:, m, :], 2, T, B.sparse[:, T], 64 ** -0.5,
                         B.o[:, T, 2 * GROUP:3 * GROUP]))
    return out


def phase_mix_out(K, l, B):
    nc, st = K.nc, K.stream
    lam_init = 0.8 - 0.6 * float(np.exp(-0.3 * l))
    with ExitStack() as ctx:
        s = K.signals(f"mix{l}")

        def sb(name, shape):
            return ctx.enter_context(nc.sbuf_tensor(f"mix{l}_{name}", shape, F32))

        od = sb("od", [P, NT, GROUP])
        sq = sb("sq", [P, NT, GROUP])
        st8 = sb("st8", [P, 3, NT * HEADS])
        gd = sb("gd", [P, 64])
        with nc.Block() as block:
            @block.vector
            def _(dve):
                link = Link(dve, s("chain"))
                dve.tensor_scalar(gd[:], K.r(f"dng{l}"), 1.0 - lam_init, None, ALU.mult)
                link(dve.scalar_tensor_tensor(out=od[:], in0=B.o1[:], scalar=K.lam[:, 1:2], in1=B.o[:, :, 0:GROUP],
                                              op0=ALU.mult, op1=ALU.add))
                link(dve.tensor_tensor(sq[:], od[:], od[:], ALU.mult))
                link(dve.tensor_reduce(st8[:, 0, :], sq[:].rearrange("p t (h e) -> p (t h) e", h=HEADS), AX.X, ALU.add))
                dve.tensor_scalar(st8[:, 1, :], st8[:, 0, :], 1.0 / 64, EPS, ALU.mult, ALU.add).then_inc(s("ms"), 1)
                dve.wait_ge(s("root"), 1)
                link(dve.reciprocal(st8[:, 0, :], st8[:, 2, :]))
                ov = od[:].rearrange("p t (h e) -> p (t h) e", h=HEADS)
                link(dve.tensor_tensor(ov, ov, spread(st8[:, 0, :], 64), ALU.mult))
                dve.tensor_tensor(sq[:].rearrange("p t (h e) -> p (t h) e", h=HEADS), ov, bcast(gd[:], NT * HEADS),
                                  ALU.mult).then_inc(s("diff"), 1)
                for i in range(KT):
                    dve.wait_ge(s("y"), i + 1)
                    dve.scalar_tensor_tensor(out=K.xT[:, i, :], in0=K.ps[:, 4 + i % 4, 0:L], scalar=K.mod[:, 0, 16 + i:17 + i],
                                             in1=K.xT[:, i, :], op0=ALU.mult, op1=ALU.add).then_inc(s("res"), 1)

            @block.scalar
            def _(act):
                act.wait_ge(s("ms"), 1)
                act.activation(st8[:, 2, :], st8[:, 1, :], ACT.Sqrt).then_inc(s("root"), 1)
                for i in range(KT):
                    act.wait_ge(s("turned"), i + 1)
                    act.activation(K.hT[:, (i + 2) % KT, :], K.ps[:, i % 4, 0:L], ACT.Copy).then_inc(s("oT"), 1)

            @block.tensor
            def _(pe):
                for i in range(KT):
                    f = (i + 2) % KT
                    if f == 0:
                        pe.wait_ge(s("diff"), 1)
                    if i >= 4:
                        pe.wait_ge(s("oT"), i - 3)
                    for T in range(NT):
                        src = sq[:, T, f * P:(f + 1) * P] if f < 2 else B.o[:, T, f * P:(f + 1) * P]
                        mm = pe.transpose(K.ps[:, i % 4, T * P:(T + 1) * P], src, K.a("ident"))
                    mm.then_inc(s("turned"), 1)
                pe.wait_ge(s("oT"), KT)
                for c in range(KT // CT):
                    n = st.take()
                    st.wait(pe, n)
                    w = st.view(n, KT, CW)
                    for m in range(CT):
                        i = CT * c + m
                        if i >= 4:
                            pe.wait_ge(s("res"), i - 3)
                        for k in range(KT):
                            mm = pe.matmul(K.ps[:, 4 + i % 4, 0:L], w[:, k, m * P:(m + 1) * P], K.hT[:, k, :],
                                           start=(k == 0), stop=(k == KT - 1))
                        mm.then_inc(s("y"), 1)
                    pe.wait_ge(s("y"), CT * (c + 1))
                    pe.sem_inc(st.freed[n % RING], 1)

            @block.gpsimd
            def _(pool):
                K.clear_old(pool)

            @block.sync
            def _(sp):
                st.issue(sp)


class MixerBuffers:
    def __init__(self, nc, ctx, l):
        def sb(name, shape):
            return ctx.enter_context(nc.sbuf_tensor(f"mixer{l}_{name}", shape, F32))
        self.qa, self.ka = sb("qa", [32, 8, L]), sb("ka", [32, 8, L])
        self.qb, self.kb = sb("qb", [96, HEADS, L]), sb("kb", [96, HEADS, L])
        self.qc, self.kc = sb("qc", [64, HEADS, L]), sb("kc", [64, HEADS, L])
        self.qd, self.kd = sb("qd", [64, HEADS, L]), sb("kd", [64, HEADS, L])
        self.v = sb("v", [P, 4, NT, GROUP])
        self.sparse = sb("sparse", [P, NT, HEADS, L])
        self.band = sb("band", [P, NT, HEADS, L])


def mixer(K, l):
    nc = K.nc
    with ExitStack() as ctx:
        B = MixerBuffers(nc, ctx, l)
        phase_norm(K, f"mnorm{l}", K.xT, K.hT, K.gain[:, 0, :], K.mod[:, 0, 0:8])
        with ExitStack() as early:
            def sb(name, shape):
                return early.enter_context(nc.sbuf_tensor(f"mixer{l}_{name}", shape, F32))
            B.qi, B.ki = sb("qi", [32, 8, L]), sb("ki", [32, 1, L])
            B.qdT, B.kvdT, B.krT = sb("qdT", [P, 2, L]), sb("kvdT", [P, 1, L]), sb("krT", [32, 1, L])
            B.wi = sb("wi", [P, NT, 8])
            phase_project(K, f"proj{l}", mixer_projections(K, B))
            phase_latent(K, l, B)
            phase_index(K, l, B)
        B.o = ctx.enter_context(nc.sbuf_tensor(f"mixer{l}_o", [P, NT, D], F32))
        B.o1 = ctx.enter_context(nc.sbuf_tensor(f"mixer{l}_o1", [P, NT, GROUP], F32))
        phase_attention(K, f"att{l}", B, mixer_batches(K, B), HEADS, NT)
        phase_mix_out(K, l, B)


def phase_ffn(K, name, gate, conv=None):
    nc, st = K.nc, K.stream
    NF = FF // P
    with ExitStack() as ctx:
        s = K.signals(name)

        def sb(nm_, shape):
            return ctx.enter_context(nc.sbuf_tensor(f"{name}_{nm_}", shape, F32))

        g = sb("g", [P, 2, L])
        h = sb("h", [P, 2, L])
        pad = sb("pad", [P, 2, L + 2])
        y = sb("y", [P, 3, L])
        first = [st.take() for _ in range(3 * (NF // CT))][0]

        def items(i):
            return [first + 3 * (i // CT) + j for j in range(3)]

        def up(i, j):
            return K.ps[:, 4 + 2 * (i % 2) + j, 0:L]

        with nc.Block() as block:
            @block.tensor
            def _(pe):
                def do_up(i):
                    n1, n3, _ = items(i)
                    for j, n in enumerate((n1, n3)):
                        if i % CT == 0:
                            st.wait(pe, n)
                        w = st.view(n, KT, CW)
                        for k in range(KT):
                            mm = pe.matmul(up(i, j), w[:, k, (i % CT) * P:(i % CT + 1) * P], K.hT[:, k, :],
                                           start=(k == 0), stop=(k == KT - 1))
                        mm.then_inc(s("up"), 1)

                def end_up(i):
                    if i % CT == CT - 1:
                        pe.wait_ge(s("up"), 2 * i + 2)
                        n1, n3, _ = items(i)
                        pe.sem_inc(st.freed[n1 % RING], 1)
                        pe.sem_inc(st.freed[n3 % RING], 1)

                def do_down(i):
                    n2 = items(i)[2]
                    if i % CT == 0:
                        st.wait(pe, n2)
                    pe.wait_ge(s("h"), i + 1)
                    w = st.view(n2, CT, D)
                    for f in range(KT):
                        mm = pe.matmul(K.ps[:, f // 2, (f % 2) * L:(f % 2 + 1) * L], w[:, i % CT, f * P:(f + 1) * P],
                                       h[:, i % 2, :], start=(i == 0 and f % 2 == 0), stop=(i == NF - 1),
                                       skip_group_check=True)
                    if i % CT == CT - 1:
                        st.free(mm, n2)

                do_up(0)
                for i in range(1, NF):
                    do_up(i)
                    do_down(i - 1)
                    end_up(i)
                do_down(NF - 1)
                pe.matmul(K.ps[:, 4, 0:1], K.a("ident"), K.a("ones")[:, 0:1], start=True, stop=True).then_inc(s("down"), 1)

            @block.scalar
            def _(act):
                for i in range(NF):
                    if conv is None:
                        act.wait_ge(s("up"), 2 * i + 1)
                        act.activation(g[:, i % 2, :], up(i, 0), ACT.Silu).then_inc(s("g"), 1)
                        continue
                    act.wait_ge(s("up"), 2 * i + 1)
                    act.wait_ge(s("padded"), 2)
                    if i >= 2:
                        act.wait_ge(s("conv"), i - 1)
                    act.activation(pad[:, i % 2, 1:L + 1], up(i, 0), ACT.Copy).then_inc(s("pad"), 1)
                    act.wait_ge(s("conv"), i + 1)
                    act.activation(g[:, i % 2, :], y[:, 2, :], ACT.Gelu_apprx_tanh).then_inc(s("g"), 1)

            @block.vector
            def _(dve):
                link = Link(dve, s("chain"))
                if conv is not None:
                    dve.memset(pad[:, :, 0:1], 0.0).then_inc(s("padded"), 1)
                    dve.memset(pad[:, :, L + 1:L + 2], 0.0).then_inc(s("padded"), 1)
                for i in range(NF):
                    if conv is not None:
                        w, b = conv
                        dve.wait_ge(s("padded"), 2)
                        dve.wait_ge(s("pad"), i + 1)
                        q = pad[:, i % 2, :]
                        link(dve.tensor_scalar(y[:, 0, :], q[:, 1:L + 1], w(1, i), b(i), ALU.mult, ALU.add))
                        link(dve.scalar_tensor_tensor(out=y[:, 1, :], in0=q[:, 0:L], scalar=w(0, i), in1=y[:, 0, :],
                                                      op0=ALU.mult, op1=ALU.add))
                        dve.scalar_tensor_tensor(out=y[:, 2, :], in0=q[:, 2:L + 2], scalar=w(2, i), in1=y[:, 1, :],
                                                 op0=ALU.mult, op1=ALU.add).then_inc(s("conv"), 1)
                    dve.wait_ge(s("g"), i + 1)
                    dve.wait_ge(s("up"), 2 * i + 2)
                    dve.tensor_tensor(h[:, i % 2, :], g[:, i % 2, :], up(i, 1), ALU.mult).then_inc(s("h"), 1)
                dve.wait_ge(s("down"), 1)
                for f in range(KT):
                    dve.scalar_tensor_tensor(out=K.xT[:, f, :], in0=K.ps[:, f // 2, (f % 2) * L:(f % 2 + 1) * L],
                                             scalar=gate[:, f:f + 1], in1=K.xT[:, f, :], op0=ALU.mult, op1=ALU.add)

            @block.gpsimd
            def _(pool):
                K.clear_old(pool)

            @block.sync
            def _(sp):
                st.issue(sp)


def phase_route(K, A, cb):
    nc = K.nc
    with ExitStack() as ctx:
        s = K.signals("route")

        def sb(nm_, shape):
            return ctx.enter_context(nc.sbuf_tensor(f"route_{nm_}", shape, F32))

        wr = sb("wr", [P, KT, NE])
        lg = sb("lg", [P, NT, NE])
        top = sb("top", [P, NT, 8])
        e = sb("e", [P, NT, 4])
        m = sb("m", [P, NT, 8, NE])
        zero = sb("zero", [P, NE])
        ct = sb("ct", [NE, L])
        with nc.Block() as block:
            @block.tensor
            def _(pe):
                pe.wait_ge(s("wr"), 16)
                for T in range(NT):
                    for k in range(KT):
                        mm = pe.matmul(K.ps[:, T, 0:NE], K.hT[:, k, T * P:(T + 1) * P], wr[:, k, :],
                                       start=(k == 0), stop=(k == KT - 1))
                    mm.then_inc(s("logits"), 1)
                for T in range(NT):
                    pe.wait_ge(s("combine"), T + 1)
                    pe.transpose(K.ps[0:NE, 2, T * P:(T + 1) * P], m[:, T, 7, :], K.a("ident")).then_inc(s("ct"), 1)
                pe.wait_ge(s("ctout"), 1)
                for x in range(NE):
                    if x >= 4:
                        pe.wait_ge(s("cb"), x - 3)
                    pe.matmul(K.ps[:, 4 + x % 4, 0:L], K.a("pick")[0:NE, x * P:(x + 1) * P], ct[:], start=True, stop=True)\
                        .then_inc(s("spread"), 1)

            @block.scalar
            def _(act):
                act.dma_start(wr[:], A["moe_router"][0].rearrange("(k p) n -> p k n", p=P)).then_inc(s("wr"), 16)
                for T in range(NT):
                    act.wait_ge(s("gap"), T + 1)
                    act.activation(e[:, T, 1:2], e[:, T, 0:1], ACT.Exp).then_inc(s("exp"), 1)
                act.wait_ge(s("ct"), NT)
                act.activation(ct[:], K.ps[0:NE, 2, 0:L], ACT.Copy).then_inc(s("ctout"), 1)
                for x in range(NE):
                    act.wait_ge(s("spread"), x + 1)
                    act.activation(cb[:, x, :], K.ps[:, 4 + x % 4, 0:L], ACT.Copy).then_inc(s("cb"), 1)

            @block.vector
            def _(dve):
                link = Link(dve, s("chain"))
                link(dve.memset(zero[:], 0.0))
                for T in range(NT):
                    mk = m[:, T]
                    dve.wait_ge(s("logits"), T + 1)
                    link(dve.tensor_copy(lg[:, T, :], K.ps[:, T, 0:NE]))
                    link(dve.max(top[:, T, :], lg[:, T, :]))
                    dve.tensor_tensor(e[:, T, 0:1], top[:, T, 1:2], top[:, T, 0:1], ALU.subtract).then_inc(s("gap"), 1)
                    link(dve.tensor_scalar(mk[:, 0, :], lg[:, T, :], top[:, T, 0:1], None, ALU.is_equal))
                    link(dve.tensor_tensor_scan(mk[:, 1, :], mk[:, 0, :], zero[:], 0.0, ALU.add, ALU.add))
                    link(dve.scalar_tensor_tensor(out=mk[:, 2, :], in0=mk[:, 1, :], scalar=1.0, in1=mk[:, 0, :],
                                                  op0=ALU.is_equal, op1=ALU.mult))
                    link(dve.scalar_tensor_tensor(out=mk[:, 3, :], in0=mk[:, 2, :], scalar=NEG, in1=lg[:, T, :],
                                                  op0=ALU.mult, op1=ALU.add))
                    link(dve.tensor_scalar(mk[:, 4, :], mk[:, 3, :], top[:, T, 1:2], None, ALU.is_equal))
                    link(dve.tensor_tensor_scan(mk[:, 5, :], mk[:, 4, :], zero[:], 0.0, ALU.add, ALU.add))
                    link(dve.scalar_tensor_tensor(out=mk[:, 6, :], in0=mk[:, 5, :], scalar=1.0, in1=mk[:, 4, :],
                                                  op0=ALU.is_equal, op1=ALU.mult))
                    dve.wait_ge(s("exp"), T + 1)
                    link(dve.tensor_scalar(e[:, T, 2:3], e[:, T, 1:2], 1.0, None, ALU.add))
                    link(dve.reciprocal(e[:, T, 3:4], e[:, T, 2:3]))
                    link(dve.scalar_tensor_tensor(out=mk[:, 1, :], in0=mk[:, 6, :], scalar=e[:, T, 1:2], in1=mk[:, 2, :],
                                                  op0=ALU.mult, op1=ALU.add))
                    dve.tensor_scalar(mk[:, 7, :], mk[:, 1, :], e[:, T, 3:4], None, ALU.mult).then_inc(s("combine"), 1)

            @block.gpsimd
            def _(pool):
                K.clear_old(pool)

            @block.sync
            def _(sp):
                K.stream.issue(sp)


def phase_experts(K, A, cb):
    nc, st = K.nc, K.stream
    NF = FFE // P
    PER = 3 * NF // CT
    assert PER % RING == 0
    m0 = K.moe_first
    assert st.taken == m0 and st.issued == m0 + RING
    rounds = PER // RING
    w1 = A["moe_w1"][0].rearrange("e (k p) n -> p (e k) n", p=P)
    w3 = A["moe_w3"][0].rearrange("e (k p) n -> p (e k) n", p=P)
    w2 = A["moe_w2"][0].rearrange("e (k p) n -> p (e k) n", p=P)
    with ExitStack() as ctx:
        s = K.signals("moe")

        def sb(nm_, shape):
            return ctx.enter_context(nc.sbuf_tensor(f"moe_{nm_}", shape, F32))

        g = sb("g", [P, 2, L])
        u = sb("u", [P, 2, L])
        h = sb("h", [P, 2, L])

        def items(i):
            return [m0 + 3 * (i // CT) + j for j in range(3)]

        def up(i, j):
            return K.ps[:, 4 + 2 * (i % 2) + j, 0:L]

        with nc.Block() as block:
            @block.tensor
            def _(pe):
                def body(e, first=False, last=False):
                    def arrived(n):
                        pe.wait_ge(st.loaded[n % RING], e * (16 * rounds) + st.arrival[n])

                    def do_up(i):
                        for j, n in enumerate(items(i)[0:2]):
                            if i % CT == 0:
                                arrived(n)
                            w = st.view(n, KT, CW)
                            for k in range(KT):
                                mm = pe.matmul(up(i, j), w[:, k, (i % CT) * P:(i % CT + 1) * P], K.hT[:, k, :],
                                               start=(k == 0), stop=(k == KT - 1))
                            mm.then_inc(s("up"), 1)

                    def end_up(i):
                        if i % CT == CT - 1:
                            pe.wait_ge(s("up"), e * (2 * NF) + 2 * i + 2)
                            for n in items(i)[0:2]:
                                pe.sem_inc(st.freed[n % RING], 1)

                    def do_down(i):
                        n2 = items(i)[2]
                        if i % CT == 0:
                            arrived(n2)
                        pe.wait_ge(s("h"), e * NF + i + 1)
                        w = st.view(n2, CT, D)
                        for f in range(KT):
                            mm = pe.matmul(K.ps[:, f // 2, (f % 2) * L:(f % 2 + 1) * L],
                                           w[:, i % CT, f * P:(f + 1) * P], h[:, i % 2, :],
                                           start=(first and i == 0 and f % 2 == 0), stop=(last and i == NF - 1),
                                           skip_group_check=True)
                        if i % CT == CT - 1:
                            st.free(mm, n2)

                    do_up(0)
                    for i in range(1, NF):
                        do_up(i)
                        do_down(i - 1)
                        end_up(i)
                    do_down(NF - 1)

                body(0, first=True)
                with pe.Fori(1, NE) as e:
                    body(e)
                pe.matmul(K.ps[:, 4, 0:1], K.a("ident"), K.a("ones")[:, 0:1], start=True, stop=True).then_inc(s("down"), 1)

            @block.scalar
            def _(act):
                with act.Fori(0, NE) as e:
                    for i in range(NF):
                        act.wait_ge(s("up"), e * (2 * NF) + 2 * i + 1)
                        act.activation(g[:, i % 2, :], up(i, 0), ACT.Silu).then_inc(s("g"), 1)

            @block.vector
            def _(dve):
                with dve.Fori(0, NE) as e:
                    for i in range(NF):
                        dve.wait_ge(s("g"), e * NF + i + 1)
                        dve.wait_ge(s("up"), e * (2 * NF) + 2 * i + 2)
                        dve.tensor_tensor(u[:, i % 2, :], g[:, i % 2, :], up(i, 1), ALU.mult).then_inc(s("u"), 1)
                        dve.wait_ge(s("u"), e * NF + i + 1)
                        dve.tensor_tensor(h[:, i % 2, :], u[:, i % 2, :], cb[:, bass.ds(e * L, L)], ALU.mult)\
                            .then_inc(s("h"), 1)
                dve.wait_ge(s("down"), 1)
                for f in range(KT):
                    dve.scalar_tensor_tensor(out=K.xT[:, f, :], in0=K.ps[:, f // 2, (f % 2) * L:(f % 2 + 1) * L],
                                             scalar=K.mod[:, 0, 40 + f:41 + f], in1=K.xT[:, f, :],
                                             op0=ALU.mult, op1=ALU.add)

            @block.gpsimd
            def _(pool):
                K.clear_old(pool)

            @block.sync
            def _(sp):
                def load(n, e):
                    j = n - m0
                    jj, de = j % PER, j // PER
                    c, kind = jj // 3, jj % 3
                    slot = n % RING
                    sp.wait_ge(st.freed[slot], e * rounds + n // RING)
                    if kind == 2:
                        src, kt, wd = w2[:, bass.ds((e + de) * NF + CT * c, CT), :], CT, D
                    else:
                        src = (w1, w3)[kind][:, bass.ds((e + de) * KT, KT), CW * c:CW * (c + 1)]
                        kt, wd = KT, CW
                    sp.dma_start(st.view(n, kt, wd), src).then_inc(st.loaded[slot], 16)

                with sp.Fori(0, NE - 1) as e:
                    for n in range(m0 + RING, m0 + RING + PER):
                        load(n, e)
                st.issued = m0 + RING + (NE - 1) * PER
                st.taken = m0 + NE * PER
                st.issue(sp)



MH = 4
DH = 128
VW = DH + 1


class SecondBuffers:
    def __init__(self, nc, ctx):
        def sb(name, shape):
            return ctx.enter_context(nc.sbuf_tensor(f"second_{name}", shape, F32))
        self.qm, self.km, self.kcm = sb("qm", [P, MH, L]), sb("km", [P, MH, L]), sb("kcm", [P, MH, L])
        self.va, self.vca = sb("va", [P, NT, MH, VW]), sb("vca", [P, NT, MH, VW])
        self.og = sb("og", [P, MH, L])
        self.qh = sb("qh", [64, 8, L])
        self.kh = sb("kh", [64, 2, 2 * L])
        self.vh = sb("vh", [P, 2 * NT, P])
        self.gt = sb("gt", [P, 2 * NT, 16])


def second_projections(K, B, pads):
    st = K.stream
    jobs = []
    qpad, kpad, kcpad, hc = pads

    def item(width):
        n = st.take()
        return n, st.view(n, KT, width)

    def heads(sources):
        for half in range(MH // CT):
            n, w = item(CW)
            for j, (src, dst) in enumerate(sources):
                for i in range(CT):
                    jobs.append(feature_job(K, n, i * P, P, src, [(dst(CT * half + i), 0, P)], w,
                                            last=(i == 1 and j == len(sources) - 1)))

    heads([(K.hT, lambda h: qpad[:, h, 1:L + 1])])
    heads([(K.hT, lambda h: kpad[:, h, 1:L + 1]), (hc, lambda h: kcpad[:, h, 1:L + 1])])
    for half in range(MH // CT):
        n, w = item(CW)
        for src, dst, c in ((K.hT, B.va, 0), (hc, B.vca, 1)):
            for T in range(NT):
                jobs.append(token_job(K, n, 0, CW, src, T, dst[:, T, CT * half:CT * (half + 1), 0:DH], w,
                                      last=(T == 1 and c == 1), shape=CT))
    heads([(K.hT, lambda h: B.og[:, h, :])])
    for half in range(2):
        n, w = item(CW)
        for j in range(CT):
            i = CT * half + j
            jobs.append(feature_job(K, n, j * P, P, K.hT, [(B.qh[:, 2 * i, :], 0, 64), (B.qh[:, 2 * i + 1, :], 64, 64)],
                                    w, last=(j == 1)))
    n, w = item(CW)
    for src, c in ((K.hT, 0), (hc, 1)):
        jobs.append(feature_job(K, n, 0, P, src, [(B.kh[:, 0, c * L:(c + 1) * L], 0, 64),
                                                  (B.kh[:, 1, c * L:(c + 1) * L], 64, 64)], w))
        for T in range(NT):
            jobs.append(token_job(K, n, P, P, src, T, B.vh[:, NT * c + T, :], w, last=(c == 1 and T == 1)))
    n, w = item(16)
    for src, c in ((K.hT, 0), (hc, 1)):
        for T in range(NT):
            jobs.append(token_job(K, n, 0, 16, src, T, B.gt[:, NT * c + T, :], w, last=(c == 1 and T == 1)))
    return jobs


def phase_shape(K, B, pads, lf):
    nc = K.nc
    qpad, kpad, kcpad, _ = pads
    with ExitStack() as ctx:
        s = K.signals("shape")

        def sb(nm_, shape):
            return ctx.enter_context(nc.sbuf_tensor(f"shape_{nm_}", shape, F32))

        y = sb("y", [P, 4, L])
        ab = sb("ab", [P, 3, 2 * NT, 16])
        t1 = sb("t1", [64, 2, L])
        tiles = [(qpad, i, i, B.qm) for i in range(MH)] + [(kpad, i, 4 + i, B.km) for i in range(MH)] + \
                [(kcpad, i, 4 + i, B.kcm) for i in range(MH)]
        ropes = [B.qh[:, i, :] for i in range(8)] + [B.kh[:, i, 0:L] for i in range(2)]
        with nc.Block() as block:
            @block.tensor
            def _(pe):
                for i, x in enumerate(ropes):
                    if i >= 4:
                        pe.wait_ge(s("roped"), i - 3)
                    pe.matmul(K.ps[0:64, i % 4, 0:L], K.b("permA")[0:64], x, start=True, stop=True)\
                        .then_inc(s("swapped"), 1)

            @block.scalar
            def _(act):
                act.activation(B.og[:], B.og[:], ACT.Sigmoid)
                act.wait_ge(s("gb"), 1)
                act.activation(ab[:, 0], B.gt[:], ACT.Abs).then_inc(s("abs"), 1)
                act.wait_ge(s("abs"), 1)
                act.activation(ab[:, 1], ab[:, 0], ACT.Exp, scale=-1.0).then_inc(s("ex"), 1)
                act.wait_ge(s("ex"), 1)
                act.activation(ab[:, 2], ab[:, 1], ACT.Ln, bias=1.0).then_inc(s("ln"), 1)
                for i, (_, h, _, dst) in enumerate(tiles):
                    act.wait_ge(s("conv"), i + 1)
                    act.activation(dst[:, h, :], y[:, 2 + i % 2, :], ACT.Silu).then_inc(s("silu"), 1)

            @block.vector
            def _(dve):
                link = Link(dve, s("chain"))
                dve.tensor_tensor(B.gt[:], B.gt[:], bcast(K.r("gate_b"), 2 * NT), ALU.add).then_inc(s("gb"), 1)
                dve.memset(B.va[:, :, :, DH:VW], 1.0)
                dve.memset(B.vca[:, :, :, DH:VW], 1.0)
                for i, x in enumerate(ropes):
                    dve.wait_ge(s("swapped"), i + 1)
                    link(dve.tensor_tensor(t1[:, 0, :], K.ps[0:64, i % 4, 0:L], K.b("sinA")[0:64], ALU.mult))
                    link(dve.tensor_tensor(t1[:, 1, :], x, K.b("cosA")[0:64], ALU.mult))
                    link(dve.tensor_tensor(x, t1[:, 0, :], t1[:, 1, :], ALU.add))
                    link(dve.memset(K.scratch1[:], 0.0))
                    dve.sem_inc(s("roped"), 1)
                for i, (src, h, c, _) in enumerate(tiles):
                    x = src[:, h, :]
                    wv = K.v("conv_w")
                    link(dve.tensor_scalar(y[:, 0, :], x[:, 1:L + 1], wv[:, 8 + c:9 + c], K.v("conv_b")[:, c:c + 1],
                                           ALU.mult, ALU.add))
                    link(dve.scalar_tensor_tensor(out=y[:, 1, :], in0=x[:, 0:L], scalar=wv[:, c:c + 1],
                                                  in1=y[:, 0, :], op0=ALU.mult, op1=ALU.add))
                    if i >= 2:
                        dve.wait_ge(s("silu"), i - 1)
                    dve.scalar_tensor_tensor(out=y[:, 2 + i % 2, :], in0=x[:, 2:L + 2], scalar=wv[:, 16 + c:17 + c],
                                             in1=y[:, 1, :], op0=ALU.mult, op1=ALU.add).then_inc(s("conv"), 1)
                    dve.wait_ge(s("conv"), i + 1)
                dve.wait_ge(s("ln"), 1)
                link(dve.tensor_scalar(ab[:, 0], B.gt[:], 0.0, None, ALU.min))
                dve.tensor_tensor(lf[:], ab[:, 0], ab[:, 2], ALU.subtract)

            @block.gpsimd
            def _(pool):
                K.clear_old(pool)

            @block.sync
            def _(sp):
                K.stream.issue(sp)


def phase_state(K, B, lf, C0, mB):
    nc = K.nc
    with ExitStack() as ctx:
        s = K.signals("state")

        def sb(nm_, shape):
            return ctx.enter_context(nc.sbuf_tensor(f"state_{nm_}", shape, F32))

        gr = sb("gr", [MH, 2, L])
        mr = sb("mr", [MH, 2, 2])
        dm = sb("dm", [MH, 2, MH])
        wc = sb("wc", [P, 2, NT, MH])
        kw = sb("kw", [P, 2, MH, NT, DH])
        col = {0: ("past_f", 0, 4), 1: ("past_b", 8, 12)}
        with nc.Block() as block:
            @block.tensor
            def _(pe):
                for d in range(2):
                    tab, ci, cf = col[d]
                    t = K.b(tab).rearrange("p (r s) -> p r s", r=NT)
                    o = K.ps[0:MH, d, 0:L]
                    for r in range(NT):
                        pe.matmul(o, lf[:, NT + r, cf:cf + MH], t[:, r, :], start=(r == 0), stop=False,
                                  skip_group_check=True)
                    for r in range(NT):
                        pe.matmul(o[:, r * P:(r + 1) * P], B.gt[:, NT + r, ci:ci + MH], K.a("ident"), start=False,
                                  stop=False, skip_group_check=True)
                    for r in range(NT):
                        mm = pe.matmul(K.ps[0:MH, d, L:L + 1], lf[:, NT + r, cf:cf + MH], K.a("ones")[:, 0:1],
                                       start=False, stop=(r == NT - 1), skip_group_check=True)
                    mm.then_inc(s("g"), 1)
                for h in range(MH):
                    for T in range(NT):
                        mm = pe.transpose(K.ps[:, 2 + h, T * P:(T + 1) * P], B.kcm[:, h, T * P:(T + 1) * P], K.a("ident"))
                    mm.then_inc(s("kt"), 1)
                for d in range(2):
                    pe.wait_ge(s("w"), d + 1)
                    for T in range(NT):
                        mm = pe.transpose(K.ps[:, 6, (2 * d + T) * MH:(2 * d + T + 1) * MH], gr[:, d, T * P:(T + 1) * P],
                                          K.a("ident")[0:MH, 0:MH])
                    mm.then_inc(s("wt"), 1)
                for d in range(2):
                    pe.wait_ge(s("dm"), d + 1)
                    pe.matmul(K.ps[:, 7, d * MH:(d + 1) * MH], K.a("ones")[0:MH], dm[:, d, :], start=True, stop=True)\
                        .then_inc(s("mB"), 1)
                for d in range(2):
                    for h in range(MH):
                        u = d * MH + h
                        pe.wait_ge(s("kw"), 2 * u + 2)
                        if u >= 2:
                            pe.wait_ge(s("c0"), u - 1)
                        for T in range(NT):
                            mm = pe.matmul(K.ps[:, u % 2, 0:VW], kw[:, d, h, T, :], B.vca[:, T, h, :],
                                           start=(T == 0), stop=(T == NT - 1))
                        mm.then_inc(s("c"), 1)

            @block.scalar
            def _(act):
                for d in range(2):
                    act.wait_ge(s("m"), d + 1)
                    act.activation(gr[:, d, :], K.ps[0:MH, d, 0:L], ACT.Exp, bias=mr[:, d, 0:1]).then_inc(s("w"), 1)
                for u in range(2 * MH):
                    act.wait_ge(s("c"), u + 1)
                    act.activation(C0[:, u, :], K.ps[:, u % 2, 0:VW], ACT.Copy).then_inc(s("c0"), 1)

            @block.vector
            def _(dve):
                link = Link(dve, s("chain"))
                for d in range(2):
                    dve.wait_ge(s("g"), d + 1)
                    dve.tensor_reduce(mr[:, d, 0:1], K.ps[0:MH, d, 0:L + 1], AX.X, ALU.max, negate=True)\
                        .then_inc(s("m"), 1)
                    dve.wait_ge(s("m"), d + 1)
                    dve.tensor_scalar(dm[:, d, :], K.a("ident")[0:MH, 0:MH], mr[:, d, 0:1], -1.0, ALU.mult, ALU.mult)\
                        .then_inc(s("dm"), 1)
                dve.wait_ge(s("mB"), 2)
                dve.tensor_copy(mB[:], K.ps[:, 7, 0:2 * MH])
                dve.wait_ge(s("wt"), 2)
                link(dve.tensor_scalar(wc[:].rearrange("p d t h -> p (d t h)"), K.ps[:, 6, 0:4 * MH], DH ** -0.5, None,
                                       ALU.mult))
                dve.wait_ge(s("kt"), MH)
                for d in range(2):
                    for h in range(MH):
                        for T in range(NT):
                            dve.tensor_scalar(kw[:, d, h, T, :], K.ps[:, 2 + h, T * P:(T + 1) * P],
                                              wc[:, d, T, h:h + 1], None, ALU.mult).then_inc(s("kw"), 1)

            @block.gpsimd
            def _(pool):
                K.clear_old(pool)

            @block.sync
            def _(sp):
                K.stream.issue(sp)


def phase_mlstm(K, B, lf, C0, mB, hid):
    nc = K.nc
    units = [(d, h, T) for d in range(2) for h in range(MH) for T in range(NT)]
    U = len(units)
    with ExitStack() as ctx:
        s = K.signals("mlstm")

        def sb(nm_, shape):
            return ctx.enter_context(nc.sbuf_tensor(f"mlstm_{nm_}", shape, F32))

        G = sb("G", [P, 2, NT, L + 2])
        gi = sb("gi", [P, 2, NT, P])
        Dm = sb("Dm", [P, 2, L + 1])
        E = sb("E", [P, 2, L + 1])
        S = sb("S", [P, 2, L])
        ST = sb("ST", [P, 2, L])
        nm = sb("nm", [P, U, 4])
        cm = sb("cm", [P, 2, VW])
        inter = sb("inter", [P, 2, VW])
        hd = sb("hd", [P, 2, DH])
        col = {0: ("upto_f", "past_f", "mask_f", 0, 4), 1: ("upto_b", "past_b", "mask_b", 8, 12)}
        tabs = {n: K.b(n).rearrange("p (r s) -> p r s", r=NT) for d in range(2) for n in col[d][0:3]}
        with nc.Block() as block:
            @block.tensor
            def _(pe):
                def front(u):
                    d, h, T = units[u]
                    g = u // NT
                    pe.wait_ge(s("G"), g + 1)
                    if u >= 2:
                        pe.wait_ge(s("S"), u - 1)
                    for r in range(NT):
                        mm = pe.matmul(K.ps[:, u % 2, 0:L + 2], tabs[col[d][0]][:, r, T * P:(T + 1) * P],
                                       G[:, g % 2, r, :], start=(r == 0), stop=(r == NT - 1))
                    mm.then_inc(s("D"), 1)
                    pe.matmul(K.ps[:, 2 + u % 2, 0:L], B.qm[:, h, T * P:(T + 1) * P], B.km[:, h, :], start=True, stop=True)\
                        .then_inc(s("qk"), 1)

                def back(u):
                    d, h, T = units[u]
                    pe.wait_ge(s("S"), u + 1)
                    for r in range(NT):
                        mm = pe.transpose(K.ps[:, 4, r * P:(r + 1) * P], S[:, u % 2, r * P:(r + 1) * P], K.a("ident"))
                    mm.then_inc(s("turned"), 1)
                    if u >= 1:
                        pe.wait_ge(s("sum"), u)
                    pe.matmul(K.ps[:, 5, 0:VW], B.qm[:, h, T * P:(T + 1) * P], C0[:, d * MH + h, :], start=True, stop=True)\
                        .then_inc(s("qc"), 1)
                    pe.wait_ge(s("ST"), u + 1)
                    for r in range(NT):
                        mm = pe.matmul(K.ps[:, 6, 0:VW], ST[:, u % 2, r * P:(r + 1) * P], B.va[:, r, h, :],
                                       start=(r == 0), stop=(r == NT - 1))
                    mm.then_inc(s("sv"), 1)

                front(0)
                for u in range(U):
                    if u + 1 < U:
                        front(u + 1)
                    back(u)

            @block.scalar
            def _(act):
                for u in range(U):
                    act.wait_ge(s("m"), u + 1)
                    if u >= 2:
                        act.wait_ge(s("inter"), u - 1)
                    act.activation(E[:, u % 2, :], Dm[:, u % 2, :], ACT.Exp, bias=nm[:, u, 0:1])
                    act.activation(nm[:, u, 1:2], nm[:, u, 0:1], ACT.Exp).then_inc(s("E"), 1)
                    act.wait_ge(s("turned"), u + 1)
                    if u >= 2:
                        act.wait_ge(s("sv"), u - 1)
                    act.activation(ST[:, u % 2, :], K.ps[:, 4, 0:L], ACT.Copy).then_inc(s("ST"), 1)
                    act.wait_ge(s("qc"), u + 1)
                    act.wait_ge(s("E"), u + 1)
                    if u >= 2:
                        act.wait_ge(s("sum"), u - 1)
                    act.activation(inter[:, u % 2, :], K.ps[:, 5, 0:VW], ACT.Copy, scale=E[:, u % 2, L:L + 1])\
                       .then_inc(s("inter"), 1)

            @block.vector
            def _(dve):
                link = Link(dve, s("chain"))

                def build(g):
                    d, h = g // MH, g % MH
                    _, past, _, ci, cf = col[d]
                    if g >= 2:
                        dve.wait_ge(s("D"), NT * (g - 1))
                    for r in range(NT):
                        f = lf[:, r, cf + h:cf + h + 1]
                        dve.tensor_scalar(gi[:, g % 2, r, :], K.a("ident"), B.gt[:, r, ci + h:ci + h + 1], None, ALU.mult)
                        dve.tensor_scalar(G[:, g % 2, r, L:L + 2], K.a("ones")[:, 0:2], f, None, ALU.mult)
                        link(dve.tensor_scalar(G[:, g % 2, r, 0:L], tabs[past][:, r, :], f, None, ALU.mult))
                    for r in range(NT):
                        v = G[:, g % 2, r, r * P:(r + 1) * P]
                        x = dve.tensor_tensor(v, v, gi[:, g % 2, r, :], ALU.add)
                    x.then_inc(s("G"), 1)

                def first(u):
                    d, h, T = units[u]
                    dve.wait_ge(s("D"), u + 1)
                    if u >= 2:
                        dve.wait_ge(s("E"), u - 1)
                    dve.tensor_tensor(Dm[:, u % 2, 0:L], K.ps[:, u % 2, 0:L], tabs[col[d][2]][:, T, :], ALU.add)
                    link(dve.tensor_tensor(Dm[:, u % 2, L:L + 1], K.ps[:, u % 2, L:L + 1], mB[:, d * MH + h:d * MH + h + 1],
                                           ALU.add))
                    dve.tensor_reduce(nm[:, u, 0:1], Dm[:, u % 2, :], AX.X, ALU.max, negate=True).then_inc(s("m"), 1)

                def second(u):
                    dve.wait_ge(s("E"), u + 1)
                    dve.wait_ge(s("qk"), u + 1)
                    if u >= 2:
                        dve.wait_ge(s("turned"), u - 1)
                    dve.scalar_tensor_tensor(out=S[:, u % 2, :], in0=K.ps[:, 2 + u % 2, 0:L], scalar=DH ** -0.5,
                                             in1=E[:, u % 2, 0:L], op0=ALU.mult, op1=ALU.mult).then_inc(s("S"), 1)

                def third(u):
                    d, h, T = units[u]
                    dve.wait_ge(s("inter"), u + 1)
                    dve.wait_ge(s("sv"), u + 1)
                    dve.tensor_tensor(cm[:, u % 2, :], K.ps[:, 6, 0:VW], inter[:, u % 2, :], ALU.add).then_inc(s("sum"), 1)
                    dve.wait_ge(s("sum"), u + 1)
                    den = cm[:, u % 2, DH:VW]
                    link(dve.scalar_tensor_tensor(out=nm[:, u, 2:3], in0=den, scalar=-1.0, in1=den,
                                                  op0=ALU.mult, op1=ALU.max))
                    link(dve.tensor_tensor(nm[:, u, 3:4], nm[:, u, 2:3], nm[:, u, 1:2], ALU.max))
                    link(dve.reciprocal(nm[:, u, 2:3], nm[:, u, 3:4]))
                    out = hid[:, T, h, :]
                    if d == 0:
                        link(dve.tensor_scalar(out, cm[:, u % 2, 0:DH], nm[:, u, 2:3], None, ALU.mult))
                    else:
                        link(dve.scalar_tensor_tensor(out=out, in0=cm[:, u % 2, 0:DH], scalar=nm[:, u, 2:3], in1=out,
                                                      op0=ALU.mult, op1=ALU.add))

                build(0)
                build(1)
                first(0)
                for u in range(U):
                    if u % NT == 0 and u // NT >= 1 and u // NT + 1 < U // NT:
                        build(u // NT + 1)
                    if u + 1 < U:
                        first(u + 1)
                    second(u)
                    third(u)

            @block.gpsimd
            def _(pool):
                K.clear_old(pool)

            @block.sync
            def _(sp):
                K.stream.issue(sp)


def window_batches(K, B, oa):
    out = []
    for T in range(NT):
        for p in range(4):
            kv = p // 2
            out.append((
                lambda m, p=p, kv=kv, T=T: [(B.qh[:, 2 * p + m, T * P:(T + 1) * P], B.kh[:, kv, :], 0, 2 * L)],
                lambda m, kb, kv=kv: B.vh[:, kb, kv * 64:(kv + 1) * 64],
                bcast(K.b("window")[:, T * 2 * L:(T + 1) * 2 * L], 2), 64 ** -0.5,
                oa[:, T, 2 * p * 64:(2 * p + 2) * 64].rearrange("p (m e) -> p m e", m=2),
                K.r("sink")[:, 2 * p:2 * p + 2].unsqueeze(2)))
    return out


def phase_second_out(K, B, hid, oa):
    nc, st = K.nc, K.stream
    with ExitStack() as ctx:
        s = K.signals("sout")

        def sb(nm_, shape):
            return ctx.enter_context(nc.sbuf_tensor(f"sout_{nm_}", shape, F32))

        sq = sb("sq", [P, NT * MH, DH])
        st8 = sb("st8", [P, 3, NT * MH])
        with nc.Block() as block:
            @block.vector
            def _(dve):
                link = Link(dve, s("chain"))
                hv = hid[:].rearrange("p t h e -> p (t h) e")
                link(dve.tensor_tensor(sq[:], hv, hv, ALU.mult))
                link(dve.tensor_reduce(st8[:, 0, :], sq[:], AX.X, ALU.add))
                dve.tensor_scalar(st8[:, 1, :], st8[:, 0, :], 1.0 / DH, EPS, ALU.mult, ALU.add).then_inc(s("ms"), 1)
                dve.wait_ge(s("root"), 1)
                link(dve.reciprocal(st8[:, 0, :], st8[:, 2, :]))
                dve.tensor_tensor(sq[:], hv, spread(st8[:, 0, :], DH), ALU.mult).then_inc(s("hn"), 1)
                for h in range(MH):
                    dve.wait_ge(s("turned"), 5 + h)
                    dve.scalar_tensor_tensor(out=K.hT[:, h, :], in0=K.ps[:, h, 0:L], scalar=K.v("mlstm_g")[:, h:h + 1],
                                             in1=B.og[:, h, :], op0=ALU.mult, op1=ALU.mult).then_inc(s("ym"), 1)
                for i in range(KT):
                    dve.wait_ge(s("y"), i + 1)
                    dve.scalar_tensor_tensor(out=K.xT[:, i, :], in0=K.ps[:, 4 + i % 4, 0:L], scalar=K.mod[:, 0, 16 + i:17 + i],
                                             in1=K.xT[:, i, :], op0=ALU.mult, op1=ALU.add).then_inc(s("res"), 1)

            @block.scalar
            def _(act):
                act.wait_ge(s("ms"), 1)
                act.activation(st8[:, 2, :], st8[:, 1, :], ACT.Sqrt).then_inc(s("root"), 1)
                for i in range(4):
                    act.wait_ge(s("turned"), i + 1)
                    act.activation(K.hT[:, 4 + i, :], K.ps[:, i, 0:L], ACT.Copy).then_inc(s("ya"), 1)

            @block.tensor
            def _(pe):
                for i in range(4):
                    for T in range(NT):
                        mm = pe.transpose(K.ps[:, i, T * P:(T + 1) * P], oa[:, T, i * P:(i + 1) * P], K.a("ident"))
                    mm.then_inc(s("turned"), 1)
                pe.wait_ge(s("hn"), 1)
                for h in range(MH):
                    pe.wait_ge(s("ya"), h + 1)
                    for T in range(NT):
                        mm = pe.transpose(K.ps[:, h, T * P:(T + 1) * P], sq[:, T * MH + h, :], K.a("ident"))
                    mm.then_inc(s("turned"), 1)
                pe.wait_ge(s("ym"), MH)
                for c in range(KT // CT):
                    n = st.take()
                    st.wait(pe, n)
                    w = st.view(n, KT, CW)
                    for m in range(CT):
                        i = CT * c + m
                        if i >= 4:
                            pe.wait_ge(s("res"), i - 3)
                        for k in range(KT):
                            mm = pe.matmul(K.ps[:, 4 + i % 4, 0:L], w[:, k, m * P:(m + 1) * P], K.hT[:, k, :],
                                           start=(k == 0), stop=(k == KT - 1))
                        mm.then_inc(s("y"), 1)
                    pe.wait_ge(s("y"), CT * (c + 1))
                    pe.sem_inc(st.freed[n % RING], 1)

            @block.gpsimd
            def _(pool):
                K.clear_old(pool)

            @block.sync
            def _(sp):
                st.issue(sp)


def phase_second_load(K, A, cT, pads):
    nc = K.nc
    with ExitStack() as ctx:
        s = K.signals("sload")
        with nc.Block() as block:
            @block.scalar
            def _(act):
                act.dma_start(cT[:], A["ctxT"].rearrange("(k p) t -> p k t", p=P)).then_inc(s("in"), 16)
                act.dma_start(K.cb_[:], A["const_b"]).then_inc(s("in"), 16)
                act.wait_ge(s("in"), 32)

            @block.vector
            def _(dve):
                for pad in pads[0:3]:
                    dve.memset(pad[:, :, 0:1], 0.0)
                    dve.memset(pad[:, :, L + 1:L + 2], 0.0)

            @block.gpsimd
            def _(pool):
                K.clear_old(pool)

            @block.sync
            def _(sp):
                K.stream.issue(sp)


def second_mixer(K, A):
    nc = K.nc
    with ExitStack() as ctx:
        def sb(name, shape, c=ctx):
            return c.enter_context(nc.sbuf_tensor(f"sm_{name}", shape, F32))
        K.cb_ = sb("const_b", [P, WIDTH_B])
        B = SecondBuffers(nc, ctx)
        lf = sb("lf", [P, 2 * NT, 16])
        with ExitStack() as early:
            pads = [sb(n, [P, MH, L + 2], early) for n in ("qpad", "kpad", "kcpad")]
            cT = sb("cT", [P, KT, L], early)
            pads.append(cT)
            phase_second_load(K, A, cT, pads)
            phase_norm(K, "cnorm", cT, cT, K.gain[:, 2, :], K.mod[:, 1, 0:8])
            phase_norm(K, "xnorm", K.xT, K.hT, K.gain[:, 0, :], K.mod[:, 0, 0:8])
            phase_project(K, "sproj", second_projections(K, B, pads))
            phase_shape(K, B, pads, lf)
        C0, mB = sb("C0", [P, 2 * MH, VW]), sb("mB", [P, 2 * MH])
        hid, oa = sb("hid", [P, NT, MH, DH]), sb("oa", [P, NT, 512])
        phase_state(K, B, lf, C0, mB)
        phase_mlstm(K, B, lf, C0, mB, hid)
        phase_attention(K, "win", B, window_batches(K, B, oa), 2, 4, extra=1)
        phase_second_out(K, B, hid, oa)


def build(nc, A, outT):
    with ExitStack() as ctx:
        K = Kit()
        K.nc, K.old, K.now = nc, None, None

        def sb(name, shape):
            return ctx.enter_context(nc.sbuf_tensor(name, shape, F32))

        K.band = A["band"]
        K.stream = Stream(nc, ctx)
        K.ps = ctx.enter_context(nc.psum_tensor("ps", [P, 8, 512], F32))
        K.ca = sb("const_a", [P, WIDTH_A])
        K.vec = sb("vec", [P, WIDTH_V])
        K.row = sb("row", [P, WIDTH_R])
        K.xT, K.hT = sb("xT", [P, KT, L]), sb("hT", [P, KT, L])
        K.silu_c = sb("silu_c", [P, 24])
        K.mod, K.gain = sb("mod", [P, 2, MODS]), sb("gain", [P, 3, KT])
        K.lam, K.scratch1 = sb("lam", [P, 2]), sb("scratch1", [P, 64])
        K.a = lambda n: K.ca[:, COLS_A[n][0]:sum(COLS_A[n])]
        K.b = lambda n: K.cb_[:, COLS_B[n][0]:sum(COLS_B[n])]
        K.v = lambda n: K.vec[:, COLS_V[n][0]:sum(COLS_V[n])]
        K.r = lambda n: K.row[:, COLS_R[n][0]:sum(COLS_R[n])]
        K.mask = lambda T: K.a("mask")[:, T * L:(T + 1) * L]
        K.alibi = lambda T: K.a("alibi")[:, T * HEADS * L:(T + 1) * HEADS * L].rearrange("p (h s) -> p h s", h=HEADS)
        plan_stream(K, A)

        phase_load(K, A)
        phase_ada(K, 0)
        mixer(K, 0)
        phase_norm(K, "fnorm0", K.xT, K.hT, K.gain[:, 1, :], K.mod[:, 0, 24:32])
        phase_ffn(K, "ffn0", K.mod[:, 0, 40:48])
        phase_ada(K, 1)
        mixer(K, 1)
        phase_norm(K, "fnorm1", K.xT, K.hT, K.gain[:, 1, :], K.mod[:, 0, 24:32])
        with nc.sbuf_tensor("cb", [P, NE * L], F32) as cb:
            phase_route(K, A, cb[:].rearrange("p (e t) -> p e t", e=NE))
            phase_experts(K, A, cb)
        phase_norm(K, "final1", K.xT, K.xT, K.v("final_g"), None)
        phase_ada(K, 2)
        second_mixer(K, A)
        phase_norm(K, "fnorm2", K.xT, K.hT, K.gain[:, 1, :], K.mod[:, 0, 24:32])
        fw, fb = K.v("fconv_w"), K.v("fconv_b")
        NF = FF // P
        phase_ffn(K, "ffn2", K.mod[:, 0, 40:48],
                  conv=(lambda j, i: fw[:, j * NF + i:j * NF + i + 1], lambda i: fb[:, i:i + 1]))
        phase_norm(K, "final2", K.xT, K.hT, K.v("final_g2"), None, out=outT.rearrange("(k p) t -> p k t", p=P))
        K.old.ctx.close()
        K.now.ctx.close()
        assert K.stream.taken == len(K.stream.items) == K.stream.issued



def rope_rows(pos, base=10000.0, pairs=16):
    inv = (base ** (-np.arange(pairs, dtype=np.float32) / pairs)).astype(np.float32)
    ang = pos[None, :].astype(np.float32) * inv[:, None]
    return np.cos(ang), np.sin(ang)


def swap_matrix(n, first, half):
    m = np.eye(n, dtype=np.float32)
    for b in range(first, n, 2 * half):
        for i in range(half):
            x, y = b + i, b + half + i
            m[[x, y]] = m[[y, x]]
    return m


def tables():
    t, r = np.arange(L), np.arange(P)
    f = np.float32

    def tok(m):
        return np.concatenate([m[T * P:(T + 1) * P].reshape(P, -1) for T in range(NT)], axis=1).astype(f)

    def rows(m):
        out = np.zeros((P, m.shape[1]), f)
        out[:m.shape[0]] = m
        return out

    chunk = np.where(t[None, :] // CHUNK <= t[:, None] // CHUNK, 0.0, NEG)
    slopes = 2.0 ** (-8.0 * np.arange(1, HEADS + 1) / HEADS)
    alibi = -slopes[None, :, None] * np.abs(t[:, None] - t[None, :])[:, None, :]
    alibi = np.where(chunk[:, None, :] < 0, NEG, alibi)
    cos, sin = rope_rows(t)
    cos32, sin32 = np.concatenate([cos, cos]), np.concatenate([-sin, sin])
    cos96 = np.concatenate([np.ones((64, L)), cos32])
    sin96 = np.concatenate([np.zeros((64, L)), sin32])
    pick = np.zeros((P, NE, P))
    for e in range(NE):
        pick[e, e] = 1
    a = {"ident": np.eye(P), "ones": np.ones((P, P)), "flip": np.eye(P)[::-1], "mask": tok(chunk), "alibi": tok(alibi),
         "cos96": rows(cos96), "sin96": rows(sin96), "perm96": rows(swap_matrix(96, 64, 16)), "cos32": rows(cos32),
         "sin32": rows(sin32), "perm32": rows(swap_matrix(32, 0, 16)), "pick": pick.reshape(P, -1)}
    (cr, sr), (cc, sc) = rope_rows(t // 64), rope_rows(t % 64)
    far = np.abs(t[:, None] - t[None, :]) > 128
    window = np.concatenate([np.where(far, NEG, 0.0), np.zeros((L, L))], axis=1)
    b = {"upto_f": tok(t[:, None] <= t[None, :]), "upto_b": tok(t[:, None] >= t[None, :]),
         "past_f": tok(t[:, None] > t[None, :]), "past_b": tok(t[:, None] < t[None, :]),
         "mask_f": tok(np.where(t[None, :] <= t[:, None], 0.0, NEG)),
         "mask_b": tok(np.where(t[None, :] >= t[:, None], 0.0, NEG)), "window": tok(window),
         "cosA": rows(np.concatenate([cr, cr, cc, cc])), "sinA": rows(np.concatenate([-sr, sr, -sc, sc])),
         "permA": rows(swap_matrix(64, 0, 16))}
    out = []
    for names, d in ((CONST_A, a), (CONST_B, b)):
        out.append(np.ascontiguousarray(np.concatenate([d[n].astype(f) for n, _ in names], axis=1)))
        assert all(d[n].shape[1] == w for n, w in names)
    return out


def feature_columns(v):
    v = np.asarray(v)
    v = v.reshape(-1, v.shape[-1])
    return v.reshape(v.shape[0], -1, P).transpose(2, 0, 1).reshape(P, -1)


WEIGHTS = ["ada_w", "w_in", "w_out", "mla_w_uq", "mla_w_ukv", "ffn_w1", "ffn_w3", "ffn_w2", "moe_router", "moe_w1",
           "moe_w3", "moe_w2", "w_ada_2", "w_in_2", "w_out_2", "w_up_2", "w_down_2"]


def kernel(**inp):
    import concourse.bacc as bacc
    from concourse.bass_utils import run_bass_kernel_spmd as run

    fc = feature_columns
    x = {k: np.asarray(v) for k, v in inp.items()}
    c2 = np.stack([x["c_2"][0], x["c_ctx_2"]])
    vec = {"c": fc(x["c"]), "c2": c2.reshape(2, KT, P).transpose(2, 1, 0).reshape(P, -1),
           "ada_b0": fc(x["ada_b"][0]), "ada_b1": fc(x["ada_b"][1]), "ada_b2": fc(x["b_ada_2"][0]),
           "mix_g0": fc(x["mix_norm_g"][0]), "mix_g1": fc(x["mix_norm_g"][1]), "ffn_g0": fc(x["ffn_norm_g"][0]),
           "ffn_g1": fc(x["ffn_norm_g"][1]), "final_g": fc(x["final_norm_g"]), "mix_g2": fc(x["norm_mix_2"]),
           "ffn_g2": fc(x["norm_ffn_2"]), "final_g2": fc(x["final_norm_2"]), "qn_g0": fc(x["mla_q_norm_g"][0]),
           "qn_g1": fc(x["mla_q_norm_g"][1]), "kvn_g0": fc(x["mla_kv_norm_g"][0]), "kvn_g1": fc(x["mla_kv_norm_g"][1]),
           "conv_w": fc(x["qk_conv_w_2"][0]), "conv_b": fc(x["qk_conv_b_2"][0]), "mlstm_g": fc(x["mlstm_norm_2"][0]),
           "fconv_w": fc(x["ffn_conv_w_2"][0]), "fconv_b": fc(x["ffn_conv_b_2"][0])}
    row = {"lam0": x["diff_lambda"][0], "lam1": x["diff_lambda"][1], "dng0": x["diff_norm_g"][0],
           "dng1": x["diff_norm_g"][1], "gate_b": x["gate_b_2"][0], "sink": x["attn_sink_2"][0]}
    rb = x["band_rel_bias"]
    band = np.concatenate([np.repeat(rb[:, :, -1:], 127, axis=2), rb[:, :, ::-1], np.repeat(rb[:, :, 0:1], 127, axis=2)],
                          axis=2)
    const_a, const_b = tables()
    arrays = {n: x[n] for n in WEIGHTS}
    arrays.update(vecs=np.concatenate([vec[n] for n, _ in VECS], axis=1),
                  rows=np.concatenate([row[n].reshape(-1) for n, _ in ROWS])[None, :],
                  band=band, const_a=const_a, const_b=const_b, xT=x["x"][0].T, ctxT=x["ctx_2"][0].T)
    arrays = {n: np.ascontiguousarray(a) for n, a in arrays.items()}
    nc = bacc.Bacc("TRN2", target_bir_lowering=False, num_devices=1)
    A = {n: nc.dram_tensor("in_" + n, a.shape, F32, kind="ExternalInput").ap() for n, a in arrays.items()}
    outT = nc.dram_tensor("outT", (D, L), F32, kind="ExternalOutput").ap()
    build(nc, A, outT)
    r = run(nc, [{"in_" + n: a for n, a in arrays.items()}], core_ids=[0])
    return np.ascontiguousarray(r.results[0]["outT"].T)[None]
```

```python
import numpy as np
from contextlib import ExitStack

import concourse.bass as bass
from concourse import mybir

F32 = mybir.dt.float32
ALU = mybir.AluOpType
ACT = mybir.ActivationFunctionType
AX = mybir.AxisListType

P = 128
D = 1024
KT = D // P
L = 256
NT = L // P
EPS = 1e-6
NEG = -1e30
TAKEN = -3e38
HEADS = 4
GROUP = 256
FF = 2816
FFE = 3584
NE = 8
TOPK = 64
CHUNK = 64
RING = 7
SLOT = 2048
CT = 2
CW = CT * P
ADA_W = 2 * D
ADA_N = 3 * KT
MODS = 6 * D // P

CONST_A = [("ident", 128), ("ones", 128), ("flip", 128), ("mask", 512), ("alibi", 2048), ("cos96", 256),
           ("sin96", 256), ("perm96", 96), ("cos32", 256), ("sin32", 256), ("perm32", 32), ("pick", 1024)]
CONST_B = [("upto_f", 512), ("upto_b", 512), ("past_f", 512), ("past_b", 512), ("mask_f", 512), ("mask_b", 512),
           ("window", 1024), ("cosA", 256), ("sinA", 256), ("permA", 64)]
CONST_C = [("before", 512), ("slots", 256), ("slot_of", 2)]
VECS = [("c", 8), ("c2", 16), ("ada_b0", 48), ("ada_b1", 48), ("ada_b2", 48), ("mix_g0", 8), ("mix_g1", 8),
        ("ffn_g0", 8), ("ffn_g1", 8), ("final_g", 8), ("mix_g2", 8), ("ffn_g2", 8), ("final_g2", 8),
        ("qn_g0", 2), ("qn_g1", 2), ("kvn_g0", 1), ("kvn_g1", 1), ("conv_w", 24), ("conv_b", 8),
        ("mlstm_g", 4), ("fconv_w", 66), ("fconv_b", 22)]
ROWS = [("lam0", 128), ("lam1", 128), ("dng0", 64), ("dng1", 64), ("gate_b", 16), ("sink", 8)]


def columns(table):
    at, out = 0, {}
    for name, width in table:
        out[name] = (at, width)
        at += width
    return out, at


COLS_A, WIDTH_A = columns(CONST_A)
COLS_B, WIDTH_B = columns(CONST_B)
COLS_C, WIDTH_C = columns(CONST_C)
COLS_V, WIDTH_V = columns(VECS)
COLS_R, WIDTH_R = columns(ROWS)


class Stream:

    def __init__(self, nc, ctx):
        self.slots = [ctx.enter_context(nc.sbuf_tensor(f"ring{i}", [P, SLOT], F32)) for i in range(RING)]
        self.loaded = [ctx.enter_context(nc.semaphore(f"loaded{i}")) for i in range(RING)]
        self.freed = [ctx.enter_context(nc.semaphore(f"freed{i}")) for i in range(RING)]
        self.items = []
        self.arrival = []
        self.total = [0] * RING
        self.issued = 0
        self.taken = 0
        self.at = {"pe": 0, "dve": 0}
        self.reader = []

    def add(self, *parts, reader="pe"):
        s = len(self.items) % RING
        self.reader.append(reader)
        self.total[s] += 16 * len(parts)
        self.items.append(parts)
        self.arrival.append(self.total[s])

    def take(self, reader="pe"):
        n = self.reader.index(reader, self.at[reader])
        self.at[reader] = n + 1
        self.taken = max(self.taken, n + 1)
        return n

    def wait(self, eng, n):
        eng.wait_ge(self.loaded[n % RING], self.arrival[n])

    def free(self, ins, n):
        ins.then_inc(self.freed[n % RING], 1)

    def view(self, n, kt, width, at=0):
        return self.slots[n % RING][:, at:at + kt * width].rearrange("p (k w) -> p k w", k=kt)

    def issue_one(self, sp, n):
        if n >= RING:
            sp.wait_ge(self.freed[n % RING], n // RING)
        for at, kt, width, src in self.items[n]:
            sp.dma_start(self.view(n, kt, width, at), src).then_inc(self.loaded[n % RING], 16)

    def issue(self, sp):
        end = min(self.taken + RING, len(self.items))
        while self.issued < end:
            self.issue_one(sp, self.issued)
            self.issued += 1


class Kit:

    def signals(self, phase):
        if self.old is not None:
            self.old.ctx.close()
        self.old, self.now = self.now, Signals(self.nc, phase)
        return self.now

    def clear_old(self, pool):
        if self.old is not None:
            for sem in self.old.made.values():
                pool.sem_clear(sem)


class Signals:

    def __init__(self, nc, phase):
        self.nc, self.ctx, self.phase, self.made = nc, ExitStack(), phase, {}

    def __call__(self, name):
        if name not in self.made:
            self.made[name] = self.ctx.enter_context(self.nc.semaphore(f"{self.phase}_{name}"))
        return self.made[name]


class Link:

    def __init__(self, eng, sem):
        self.eng, self.sem, self.n = eng, sem, 0

    def __call__(self, ins):
        self.n += 1
        ins.then_inc(self.sem, 1)
        self.eng.wait_ge(self.sem, self.n)


def bcast(ap, n):
    return ap.unsqueeze(1).to_broadcast([ap.shape[0], n, ap.shape[1]])


def spread(ap, n):
    return ap.unsqueeze(2).to_broadcast([ap.shape[0], ap.shape[1], n])


def w_tiles(w, c0, width):
    return w.rearrange("(k p) n -> p k n", p=P)[:, :, c0:c0 + width]


def share(things, x, n):
    return things[len(things) * x // n:len(things) * (x + 1) // n]


def plan_stream(K, A):
    st = K.stream

    def cols(w, c0, width):
        kt = w.shape[0] // P
        st.add((0, kt, width, w_tiles(w, c0, width)))

    def ada(l, i):
        w, j, k = K.ada_w[l], i // KT, i % KT
        st.add((0, 1, ADA_W, w[k * P:(k + 1) * P, j * ADA_W:(j + 1) * ADA_W].unsqueeze(1)), reader="dve")

    def mixer(l):
        w = A["w_in"][l]
        for x, (c0, c1) in enumerate(IN_ITEMS):
            cols(w, c0, c1 - c0)
            for args in share(K.ada_project[l], x, len(IN_ITEMS)):
                ada(*args)
        st.add((0, 2, 384, A["mla_w_uq"][l].rearrange("(k p) n -> p k n", p=P)),
               (768, 1, 512, A["mla_w_ukv"][l].rearrange("(k p) n -> p k n", p=P)))
        for c0 in range(0, D, CW):
            cols(A["w_out"][l], c0, CW)

    def ffn(w1, w3, w2, o3, ff, beside=()):
        for c0 in range(0, ff, CW):
            for args in share(beside, c0 // CW, ff // CW):
                ada(*args)
            cols(w1, c0, CW)
            cols(w3, o3 + c0, CW)
            st.add((0, CT, D, w2.rearrange("(k p) n -> p k n", p=P)[:, c0 // P:c0 // P + CT, :]))

    for i in range(KT):
        ada(0, i)
    mixer(0)
    ffn(A["ffn_w1"][0], A["ffn_w3"][0], A["ffn_w2"][0], 0, FF, K.ada_ffn)
    mixer(1)
    K.moe_first = len(st.items)
    for e in range(NE):
        ffn(A["moe_w1"][0, e], A["moe_w3"][0, e], A["moe_w2"][0, e], 0, FFE)
    w = A["w_in_2"][0]
    for x, (c0, width) in enumerate(SECOND_ITEMS):
        cols(w, c0, width)
        for args in share(K.ada_project[2], x, len(SECOND_ITEMS)):
            ada(*args)
    for c0 in range(0, D, CW):
        cols(A["w_out_2"][0], c0, CW)
    ffn(A["w_up_2"][0], A["w_up_2"][0], A["w_down_2"][0], FF, FF)


SECOND_ITEMS = [(c0, CW) for c0 in (0, 256, 512, 768, 1024, 1280, 1536, 1792, 2064, 2320, 2576)] + [(2048, 16)]
IN_ITEMS = [(0, 256), (256, 512), (512, 768), (768, 1024), (1024, 1184), (1184, 1440), (1440, 1696), (1696, 1952),
            (1952, 2208), (2208, 2248), (2248, 2504), (2504, 2760), (2760, 3016)]




def ada_accumulate(K, dve, link, l, i, accs):
    st = K.stream
    nv = 2 if l == 2 else 1
    cs = (K.silu_c[:, 8:24] if l == 2 else K.silu_c[:, 0:8]).rearrange("p (k v) -> p k v", v=nv)
    k = i % KT
    n = st.take("dve")
    st.wait(dve, n)
    w = st.view(n, 1, ADA_W)[:, 0, :]
    for v, acc in enumerate(accs):
        c = cs[:, k, v:v + 1]
        if k == 0:
            x = dve.tensor_scalar(acc, w, c, None, ALU.mult)
        else:
            x = dve.scalar_tensor_tensor(out=acc, in0=w, scalar=c, in1=acc, op0=ALU.mult, op1=ALU.add)
        if v < len(accs) - 1:
            link(x)
    st.free(x, n)
    dve.wait_ge(st.freed[n % RING], n // RING + 1)


def ada_sum(K, pe, acc, bank, at, start):
    for m in range(ADA_W // P):
        mm = pe.matmul(K.ps[:, bank, at + m:at + m + 1], acc[:, m * P:(m + 1) * P], K.a("ones")[:, 0:1],
                       start=(start and m == 0), stop=True, skip_group_check=True)
    return mm


def ada_finish(K, dve, link, sums):
    nc_ = ADA_W // P
    for l, v, j, bank, at in sums:
        c0 = j * nc_
        dve.tensor_tensor(K.mod[l][:, v, c0:c0 + nc_], K.ps[:, bank, at:at + nc_], K.v(f"ada_b{l}")[:, c0:c0 + nc_],
                          ALU.add)
    link(dve.memset(K.scratch1[:], 1.0))
    for l, v, j, _, _ in sums:
        for third, c, which, name in ((0, KT, 2 * v, f"mix_g{l}"), (2, 4 * KT, 1, f"ffn_g{l}")):
            if j == third:
                dve.scalar_tensor_tensor(out=K.gain[l][:, which, :], in0=K.mod[l][:, v, c:c + KT], scalar=1.0,
                                         in1=K.v(name), op0=ALU.add, op1=ALU.mult)


def phase_load(K, A):
    nc = K.nc
    with ExitStack() as ctx:
        s = K.signals("load")
        acc = ctx.enter_context(nc.sbuf_tensor("ada0_acc", [P, ADA_W], F32))
        with nc.Block() as block:
            @block.scalar
            def _(act):
                act.dma_start(K.vec[:], A["vecs"]).then_inc(s("vec"), 16)
                act.dma_start(K.ca[:], A["const_a"]).then_inc(s("in"), 16)
                act.dma_start(K.row[:], bass.AP(tensor=A["rows"].tensor, offset=0, ap=[[0, P], [1, WIDTH_R]]))\
                   .then_inc(s("in"), 16)
                act.dma_start(K.xT[:], A["xT"].rearrange("(k p) t -> p k t", p=P)).then_inc(s("in"), 16)
                act.wait_ge(s("vec"), 16)
                act.activation(K.silu_c[:, 0:8], K.v("c"), ACT.Silu).then_inc(s("silu"), 1)
                act.activation(K.silu_c[:, 8:24], K.v("c2"), ACT.Silu).then_inc(s("silu"), 1)
                act.wait_ge(s("in"), 48)

            @block.tensor
            def _(pe):
                pe.wait_ge(s("in"), 48)
                pe.wait_ge(s("acc"), 1)
                ada_sum(K, pe, acc, 7, 0, True).then_inc(s("mod"), 1)

            @block.vector
            def _(dve):
                link = Link(dve, s("chain"))
                dve.wait_ge(s("silu"), 2)
                for i in range(KT):
                    ada_accumulate(K, dve, link, 0, i, [acc[:]])
                dve.sem_inc(s("acc"), 1)
                dve.wait_ge(s("vec"), 16)
                dve.wait_ge(s("mod"), 1)
                ada_finish(K, dve, link, [(0, 0, 0, 7, 0)])

            @block.gpsimd
            def _(pool):
                K.clear_old(pool)

            @block.sync
            def _(sp):
                K.stream.issue(sp)


def phase_norm(K, name, src, dst, gain, shift, out=None, arrived=None):
    nc = K.nc
    with ExitStack() as ctx:
        s = K.signals(name)
        sq = ctx.enter_context(nc.sbuf_tensor(f"{name}_sq", [P, KT, L], F32))
        rs = ctx.enter_context(nc.sbuf_tensor(f"{name}_rs", [P, 3, L], F32))
        with nc.Block() as block:
            @block.scalar
            def _(act):
                if arrived is not None:
                    act.wait_ge(*arrived)
                for k in range(KT):
                    act.activation(sq[:, k, :], src[:, k, :], ACT.Square).then_inc(s("sq"), 1)
                act.wait_ge(s("ms"), 1)
                act.activation(rs[:, 1, :], rs[:, 0, :], ACT.Sqrt).then_inc(s("root"), 1)
                if shift is not None:
                    for k in range(KT):
                        act.wait_ge(s("y"), k + 1)
                        act.activation(dst[:, k, :], sq[:, k, :], ACT.Identity, bias=shift[:, k:k + 1])
                if out is not None:
                    act.wait_ge(s("y"), KT)
                    act.dma_start(out, dst[:]).then_inc(s("stored"), 16)
                    act.wait_ge(s("stored"), 16)

            @block.tensor
            def _(pe):
                for k in range(KT):
                    pe.wait_ge(s("sq"), k + 1)
                    mm = pe.matmul(K.ps[:, 0, 0:L], K.a("ones"), sq[:, k, :], start=(k == 0), stop=(k == KT - 1))
                mm.then_inc(s("sum"), 1)

            @block.vector
            def _(dve):
                link = Link(dve, s("chain"))
                dve.wait_ge(s("sum"), 1)
                dve.tensor_scalar(rs[:, 0, :], K.ps[:, 0, 0:L], 1.0 / D, EPS, ALU.mult, ALU.add).then_inc(s("ms"), 1)
                dve.wait_ge(s("root"), 1)
                link(dve.reciprocal(rs[:, 2, :], rs[:, 1, :]))
                dve.wait_ge(s("sq"), KT)
                for k in range(KT):
                    y = sq if shift is not None else dst
                    dve.scalar_tensor_tensor(out=y[:, k, :], in0=src[:, k, :], scalar=gain[:, k:k + 1],
                                             in1=rs[:, 2, :], op0=ALU.mult, op1=ALU.mult).then_inc(s("y"), 1)

            @block.gpsimd
            def _(pool):
                K.clear_old(pool)

            @block.sync
            def _(sp):
                K.stream.issue(sp)


def phase_project(K, name, jobs, beside=(), mod_of=None):
    nc, st = K.nc, K.stream
    with ExitStack() as ctx:
        s = K.signals(name)

        def on_dve(j):
            return j % 2 == 1 and not beside

        def evicted(j):
            if beside:
                return s("evicted_act"), j + 1
            return s(("evicted_act", "evicted_dve")[j % 2]), j // 2 + 1

        if mod_of is not None:
            acc = ctx.enter_context(nc.sbuf_tensor(f"{name}_acc", [P, 2, ADA_W], F32))
        with nc.Block() as block:
            @block.tensor
            def _(pe):
                have = -1
                done_with = None
                for j, (n, lhsT, rhs, kt, rows, width, _, last) in enumerate(jobs):
                    if n > have:
                        st.wait(pe, n)
                        have = n
                    if j >= 4:
                        pe.wait_ge(*evicted(j - 4))
                    for k in range(kt):
                        mm = pe.matmul(K.ps[0:rows, j % 4, 0:width], lhsT(k), rhs(k), start=(k == 0), stop=(k == kt - 1))
                        if done_with is not None:
                            st.free(mm, done_with)
                            done_with = None
                    mm.then_inc(s("product"), 1)
                    if last:
                        done_with = n
                pe.wait_ge(s("product"), len(jobs))
                pe.sem_inc(st.freed[done_with % RING], 1)
                if mod_of is not None:
                    pe.wait_ge(s("thirds"), 1)
                    for b in range(2):
                        mm = ada_sum(K, pe, acc[:, b, :], 7, b * 16, start=(b == 0))
                    mm.then_inc(s("mod"), 1)

            @block.scalar
            def _(act):
                for j, job in enumerate(jobs):
                    if not on_dve(j):
                        act.wait_ge(s("product"), j + 1)
                        for out, part, func in job[6]:
                            ev = act.activation(out, part(K.ps[:, j % 4, :]), func or ACT.Copy)
                        ev.then_inc(s("evicted_act"), 1)

            @block.vector
            def _(dve):
                link = Link(dve, s("chain"))
                for j, job in enumerate(jobs):
                    if on_dve(j):
                        dve.wait_ge(s("product"), j + 1)
                        for out, part, func in job[6]:
                            assert func is None
                            ev = dve.tensor_copy(out, part(K.ps[:, j % 4, :]))
                        ev.then_inc(s("evicted_dve"), 1)
                for l, i in beside:
                    ada_accumulate(K, dve, link, l, i, [acc[:, i // KT - 1, :]])
                if mod_of is not None:
                    dve.sem_inc(s("thirds"), 1)
                    dve.wait_ge(s("mod"), 1)
                    ada_finish(K, dve, link, [(mod_of, 0, 1, 7, 0), (mod_of, 0, 2, 7, 16)])

            @block.gpsimd
            def _(pool):
                K.clear_old(pool)

            @block.sync
            def _(sp):
                st.issue(sp)


def feature_job(K, n, c0, rows, hT, outs, w, last=False, func=None):
    ev = [(dst, (lambda b, r0=r0, r=r: b[r0:r0 + r, 0:L]), func) for dst, r0, r in outs]
    return (n, lambda k: w[:, k, c0:c0 + rows], lambda k: hT[:, k, :], KT, rows, L, ev, last)


def token_job(K, n, c0, width, hT, T, dst, w, last=False, shape=None):
    if shape is None:
        part = lambda b: b[:, 0:width]
    else:
        part = lambda b: b[:, 0:width].rearrange("p (a e) -> p a e", a=shape)
    return (n, lambda k: hT[:, k, T * P:(T + 1) * P], lambda k: w[:, k, c0:c0 + width], KT, P, width,
            [(dst, part, None)], last)


def mixer_projections(K, B):
    st, hT = K.stream, K.hT
    jobs = []

    def item(width):
        n = st.take()
        return n, st.view(n, KT, width)

    def split(dst, first, size):
        return [(dst[:, first + i, :], i * size, size) for i in range(P // size)]

    def split_pair(dst, size):
        n, w = item(CW)
        for i in range(CT):
            jobs.append(feature_job(K, n, i * P, P, hT, split(dst, (P // size) * i, size), w, last=(i == 1)))

    def values(g):
        n, w = item(CW)
        for T in range(NT):
            jobs.append(token_job(K, n, 0, GROUP, hT, T, B.v[:, g, T, :], w, last=(T == 1)))

    split_pair(B.qa, 32)
    split_pair(B.ka, 32)
    values(0)
    n, w = item(CW)
    for i in range(CT):
        jobs.append(feature_job(K, n, i * P, P, hT, [(B.qdT[:, i, :], 0, P)], w, last=(i == 1)))
    n, w = item(160)
    jobs.append(feature_job(K, n, 0, P, hT, [(B.kvdT[:, 0, :], 0, P)], w))
    jobs.append(feature_job(K, n, P, 32, hT, [(B.krT[:, 0, :], 0, 32)], w, last=True))
    split_pair(B.qc, 64)
    split_pair(B.kc, 64)
    values(2)
    split_pair(B.qi, 32)
    n, w = item(40)
    jobs.append(feature_job(K, n, 0, 32, hT, [(B.ki[:, 0, :], 0, 32)], w))
    for T in range(NT):
        jobs.append(token_job(K, n, 32, 8, hT, T, B.wi[:, T, :], w, last=(T == 1)))
    split_pair(B.qd, 64)
    split_pair(B.kd, 64)
    values(3)
    return jobs


def phase_latent(K, l, B):
    nc, st = K.nc, K.stream
    lam_init = 0.8 - 0.6 * float(np.exp(-0.3 * l))
    with ExitStack() as ctx:
        s = K.signals(f"lat{l}")

        def sb(name, shape):
            return ctx.enter_context(nc.sbuf_tensor(f"lat{l}_{name}", shape, F32))

        sq = sb("sq", [P, 3, L])
        rs = sb("rs", [P, 2, 3, L])
        qraw = sb("qraw", [96, 4, L])
        qn = sb("qn", [P, 3, L])
        rot = sb("rot", [96, 4, L])
        lam = sb("lam", [P, 2, 32])
        lam2 = sb("lam2", [P, 4])
        rev = sb("rev", [P, 2, HEADS, L])
        n = st.take()
        wq = st.view(n, 2, 384)
        wkv = st.view(n, 1, 512, 768)[:, 0, :].rearrange("p (h c) -> p h c", h=HEADS)
        with nc.Block() as block:
            @block.scalar
            def _(act):
                for T in range(NT):
                    act.dma_start(rev[:, T], bass.AP(tensor=K.band.tensor, offset=l * HEADS * 511 + P * (1 - T),
                                                     ap=[[1, P], [511, HEADS], [1, L]])).then_inc(s("band"), 16)
                act.activation(sq[:, 0:2, :], B.qdT[:], ACT.Square)
                act.activation(sq[:, 2:3, :], B.kvdT[:], ACT.Square).then_inc(s("sq"), 1)
                act.wait_ge(s("ms"), 1)
                act.activation(rs[:, 1, 0:2, :], rs[:, 0, 0:2, :], ACT.Sqrt).then_inc(s("root"), 1)
                act.wait_ge(s("lamdot"), 1)
                act.activation(lam2[:, 2:4], lam2[:, 0:2], ACT.Exp).then_inc(s("lamexp"), 1)
                for h in range(HEADS):
                    act.wait_ge(s("q"), 2 * (h // 2) + 2)
                    act.activation(qraw[:, h, :], K.ps[0:96, 2 + h // 2, (h % 2) * L:(h % 2 + 1) * L], ACT.Copy)\
                       .then_inc(s("qraw"), 1)
                for h in range(HEADS):
                    act.wait_ge(s("kv"), h + 1)
                    act.activation(B.kb[0:64, h, :], K.ps[0:64, 4 + h % 2, 0:L], ACT.Copy).then_inc(s("kev"), 1)
                for T in range(NT):
                    act.wait_ge(s("kv"), HEADS + 1 + T)
                    act.activation(B.v[:, 1, T, :], K.ps[:, 4 + T, 0:GROUP], ACT.Copy)

            @block.tensor
            def _(pe):
                pe.wait_ge(s("sq"), 1)
                for k in range(2):
                    pe.matmul(K.ps[:, 0, 0:L], K.a("ones"), sq[:, k, :], start=(k == 0), stop=(k == 1))
                pe.matmul(K.ps[:, 1, 0:L], K.a("ones"), sq[:, 2, :], start=True, stop=True)
                pe.matmul(K.ps[0:32, 1, L:2 * L], K.a("perm32")[0:32], B.krT[:, 0, :], start=True, stop=True)\
                    .then_inc(s("sum"), 1)
                pe.wait_ge(s("band"), 16 * NT)
                for T in range(NT):
                    for half in range(2):
                        pe.matmul(K.ps[:, 6 + half, :], K.a("flip"), rev[:, T, 2 * half:2 * half + 2, :],
                                  start=True, stop=True).then_inc(s("bias"), 1)
                    if T == 0:
                        pe.wait_ge(s("biased"), 2)
                st.wait(pe, n)
                pe.wait_ge(s("qn"), 1)
                for h in range(HEADS):
                    for k in range(2):
                        mm = pe.matmul(K.ps[0:96, 2 + h // 2, (h % 2) * L:(h % 2 + 1) * L],
                                       wq[:, k, h * 96:(h + 1) * 96], qn[:, k, :], start=(k == 0), stop=(k == 1))
                    mm.then_inc(s("q"), 1)
                for h in range(HEADS):
                    if h >= 2:
                        pe.wait_ge(s("kev"), h - 1)
                    pe.matmul(K.ps[0:64, 4 + h % 2, 0:L], wkv[:, h, 0:64], qn[:, 2, :], start=True, stop=True)\
                        .then_inc(s("kv"), 1)
                for T in range(NT):
                    pe.wait_ge(s("kev"), 3 + T)
                    mm = pe.matmul(K.ps[:, 4 + T, 0:GROUP], qn[:, 2, T * P:(T + 1) * P], wkv[:, :, 64:128],
                                   start=True, stop=True)
                    mm.then_inc(s("kv"), 1)
                for h in range(HEADS):
                    pe.wait_ge(s("qraw"), h + 1)
                    pe.wait_ge(s("biased"), 4)
                    pe.matmul(K.ps[0:96, 6 + h // 2, (h % 2) * L:(h % 2 + 1) * L], K.a("perm96")[0:96], qraw[:, h, :],
                              start=True, stop=True).then_inc(s("qrot"), 1)
                pe.wait_ge(s("qrot"), HEADS)
                pe.sem_inc(st.freed[n % RING], 1)

            @block.vector
            def _(dve):
                link = Link(dve, s("chain"))
                dve.wait_ge(s("sum"), 1)
                dve.tensor_scalar(rs[:, 0, 0, :], K.ps[:, 0, 0:L], 1.0 / 256, EPS, ALU.mult, ALU.add)
                dve.tensor_scalar(rs[:, 0, 1, :], K.ps[:, 1, 0:L], 1.0 / 128, EPS, ALU.mult, ALU.add)\
                    .then_inc(s("ms"), 1)
                lv = K.r(f"lam{l}").rearrange("p (a b e) -> p a b e", a=2, b=2)
                link(dve.tensor_tensor(lam[:], lv[:, :, 0, :], lv[:, :, 1, :], ALU.mult))
                dve.tensor_reduce(lam2[:, 0:2], lam[:], AX.X, ALU.add).then_inc(s("lamdot"), 1)
                link(dve.tensor_tensor(rot[0:32, 0, :], K.ps[0:32, 1, L:2 * L], K.a("sin32")[0:32], ALU.mult))
                link(dve.tensor_tensor(rot[0:32, 1, :], B.krT[:, 0, :], K.a("cos32")[0:32], ALU.mult))
                link(dve.tensor_tensor(rot[0:32, 2, :], rot[0:32, 0, :], rot[0:32, 1, :], ALU.add))
                link(dve.tensor_copy(B.kb[64:96, :, :], bcast(rot[0:32, 2, :], HEADS)))
                dve.wait_ge(s("root"), 1)
                link(dve.reciprocal(rs[:, 0, 0:2, :], rs[:, 1, 0:2, :]))
                for k in range(3):
                    g = K.v(f"qn_g{l}")[:, k:k + 1] if k < 2 else K.v(f"kvn_g{l}")
                    src = B.qdT[:, k, :] if k < 2 else B.kvdT[:, 0, :]
                    nn = dve.scalar_tensor_tensor(out=qn[:, k, :], in0=src, scalar=g, in1=rs[:, 0, k // 2, :],
                                                  op0=ALU.mult, op1=ALU.mult)
                nn.then_inc(s("qn"), 1)
                dve.wait_ge(s("lamexp"), 1)
                link(dve.tensor_tensor(K.lam[:, 0:1], lam2[:, 2:3], lam2[:, 3:4], ALU.subtract))
                dve.tensor_scalar(K.lam[:, 1:2], K.lam[:, 0:1], -1.0, -lam_init, ALU.mult, ALU.add)
                for T in range(NT):
                    for half in range(2):
                        dve.wait_ge(s("bias"), 2 * T + half + 1)
                        dve.tensor_tensor(B.band[:, T, 2 * half:2 * half + 2, :],
                                          K.ps[:, 6 + half, :].rearrange("p (h t) -> p h t", h=2),
                                          bcast(K.mask(T), 2), ALU.add).then_inc(s("biased"), 1)
                for h in range(HEADS):
                    dve.wait_ge(s("qrot"), 2 * (h // 2) + 2)
                    link(dve.tensor_tensor(rot[:, 3, :], K.ps[0:96, 6 + h // 2, (h % 2) * L:(h % 2 + 1) * L],
                                           K.a("sin96")[0:96], ALU.mult))
                    link(dve.tensor_tensor(B.qb[:, h, :], qraw[:, h, :], K.a("cos96")[0:96], ALU.mult))
                    link(dve.tensor_tensor(B.qb[:, h, :], B.qb[:, h, :], rot[:, 3, :], ALU.add))

            @block.gpsimd
            def _(pool):
                K.clear_old(pool)

            @block.sync
            def _(sp):
                st.issue(sp)


def phase_index(K, l, B):
    nc = K.nc
    NH = 8
    with ExitStack() as ctx:
        s = K.signals(f"idx{l}")

        def sb(name, shape):
            return ctx.enter_context(nc.sbuf_tensor(f"idx{l}_{name}", shape, F32))

        relu = sb("relu", [P, 4, L])
        score = sb("score", [P, NT, 2, L])
        top = sb("top", [P, NT, 8])
        with nc.Block() as block:
            @block.tensor
            def _(pe):
                for u in range(NT * NH):
                    T, h = u % NT, u // NT
                    if u >= 4:
                        pe.wait_ge(s("relu"), u - 3)
                    pe.matmul(K.ps[:, u % 4, 0:L], B.qi[:, h, T * P:(T + 1) * P], B.ki[:, 0, :], start=True, stop=True)\
                        .then_inc(s("dot"), 1)

            @block.scalar
            def _(act):
                for u in range(NT * NH):
                    act.wait_ge(s("dot"), u + 1)
                    if u >= 4:
                        act.wait_ge(s("added"), u - 3)
                    act.activation(relu[:, u % 4, :], K.ps[:, u % 4, 0:L], ACT.Relu, scale=1.0 / 16)\
                       .then_inc(s("relu"), 1)

            @block.vector
            def _(dve):
                link = Link(dve, s("chain"))
                for u in range(NT * NH):
                    T, h = u % NT, u // NT
                    dve.wait_ge(s("relu"), u + 1)
                    if u >= NT:
                        dve.wait_ge(s("added"), u - NT + 1)
                    acc = K.mask(T) if h == 0 else score[:, T, h % 2, :]
                    dve.scalar_tensor_tensor(out=score[:, T, (h + 1) % 2, :], in0=relu[:, u % 4, :],
                                             scalar=B.wi[:, T, h:h + 1], in1=acc, op0=ALU.mult, op1=ALU.add)\
                        .then_inc(s("added"), 1)
                dve.wait_ge(s("added"), NT * NH)
                for r in range(TOPK // 8):
                    for T in range(NT):
                        a, b = score[:, T, r % 2, :], score[:, T, (r + 1) % 2, :]
                        link(dve.max(top[:, T, :], a))
                        link(dve.match_replace(b, top[:, T, :], a, TAKEN))
                for T in range(NT):
                    link(dve.tensor_scalar(score[:, T, 1, :], score[:, T, 0, :], TAKEN, NEG, ALU.not_equal, ALU.mult))
                    dve.tensor_tensor(B.sparse[:, T], K.alibi(T), bcast(score[:, T, 1, :], HEADS), ALU.add)

            @block.gpsimd
            def _(pool):
                K.clear_old(pool)

            @block.sync
            def _(sp):
                K.stream.issue(sp)


def phase_attention(K, name, B, batches, nm, nb, extra=0):
    nc = K.nc
    W = nb * P
    NB = len(batches)
    WS = W + extra
    with ExitStack() as ctx:
        s = K.signals(name)

        def sb(nm_, shape):
            return ctx.enter_context(nc.sbuf_tensor(f"{name}_{nm_}", shape, F32))

        S = sb("S", [P, 3, nm, WS])
        PT = sb("PT", [P, 2, nm * nb, P])
        mx = sb("mx", [P, NB, nm])
        sm = sb("sm", [P, NB, nm])
        rc = sb("rc", [P, NB, nm])
        blocks = [batch[6] for batch in batches]

        def scores(b, m):
            at = m * W
            return K.ps[:, 2 * (b % 2) + at // 512, at % 512:at % 512 + W]

        def all_scores(b):
            w = blocks[b] * P
            return K.ps[:, 2 * (b % 2):2 * (b % 2) + 2, :].rearrange("p a (m w) -> p (a m) w", w=W)[:, :, 0:w]

        def half(b):
            return nm * blocks[b] // 2

        with nc.Block() as block:
            @block.tensor
            def _(pe):
                def do_scores(b):
                    if b >= 2:
                        pe.wait_ge(s("biased"), b - 1)
                    for m in range(nm):
                        q, k = batches[b][0](m)
                        w = blocks[b] * P
                        mm = pe.matmul(scores(b, m)[:, 0:w], q, k[:, 0:w], start=True, stop=True)
                    mm.then_inc(s("scores"), 1)

                def do_turn(b):
                    pe.wait_ge(s("exp"), nm * (b + 1))
                    for i in range(2 * half(b)):
                        if b >= 1 and i % half(b) == 0:
                            pe.wait_ge(s(("low_out", "high_out")[i // half(b)]), b)
                        at = i % half(b)
                        mm = pe.transpose(K.ps[:, 4 + i // half(b), at * P:(at + 1) * P],
                                          S[:, b % 3, i // blocks[b], (i % blocks[b]) * P:(i % blocks[b] + 1) * P],
                                          K.a("ident"))
                        if i % half(b) == half(b) - 1:
                            mm.then_inc(s("turned"), 1)

                def do_pv(b):
                    pe.wait_ge(s("low_out"), b + 1)
                    pe.wait_ge(s("high_out"), b + 1)
                    if b >= 1:
                        pe.wait_ge(s("out"), b)
                    for m in range(nm):
                        for kb in range(blocks[b]):
                            mm = pe.matmul(K.ps[:, 6, m * 64:(m + 1) * 64], PT[:, b % 2, m * blocks[b] + kb, :],
                                           batches[b][1](m, kb), start=(kb == 0), stop=(kb == blocks[b] - 1))
                    mm.then_inc(s("pv"), 1)

                do_scores(0)
                do_scores(1)
                for b in range(NB):
                    do_turn(b)
                    if b >= 1:
                        do_pv(b - 1)
                    if b + 2 < NB:
                        do_scores(b + 2)
                do_pv(NB - 1)

            @block.scalar
            def _(act):
                def exps(b):
                    act.wait_ge(s("max"), b + 1)
                    w = blocks[b] * P
                    for m in range(nm):
                        v = S[:, b % 3, m, 0:w + extra]
                        act.activation(v, v, ACT.Exp, bias=mx[:, b, m:m + 1], accum_out=sm[:, b, m:m + 1])\
                           .then_inc(s("exp"), 1)

                def copy_low(b):
                    act.wait_ge(s("turned"), 2 * b + 1)
                    if b >= 2:
                        act.wait_ge(s("pv"), b - 1)
                    h = half(b)
                    act.activation(PT[:, b % 2, 0:h, :], K.ps[:, 4, 0:h * P].rearrange("p (i q) -> p i q", i=h), ACT.Copy)\
                       .then_inc(s("low_out"), 1)

                exps(0)
                for b in range(NB):
                    if b + 1 < NB:
                        exps(b + 1)
                    copy_low(b)

            @block.vector
            def _(dve):
                link = Link(dve, s("chain"))

                def do_bias(b):
                    dve.wait_ge(s("scores"), b + 1)
                    if b >= 3:
                        dve.wait_ge(s("turned"), 2 * (b - 2))
                    w = blocks[b] * P
                    dve.scalar_tensor_tensor(out=S[:, b % 3, :, 0:w], in0=all_scores(b), scalar=batches[b][3],
                                             in1=batches[b][2][:, :, 0:w], op0=ALU.mult, op1=ALU.add)\
                        .then_inc(s("biased"), 1)
                    if extra:
                        dve.tensor_copy(S[:, b % 3, :, W:WS], batches[b][5]).then_inc(s("extra"), 1)
                        dve.wait_ge(s("extra"), b + 1)
                    dve.wait_ge(s("biased"), b + 1)
                    dve.tensor_reduce(mx[:, b, :], S[:, b % 3, :, 0:w + extra], AX.X, ALU.max, negate=True)\
                        .then_inc(s("max"), 1)

                def copy_high(b):
                    dve.wait_ge(s("turned"), 2 * b + 2)
                    if b >= 2:
                        dve.wait_ge(s("pv"), b - 1)
                    h = half(b)
                    dve.tensor_copy(PT[:, b % 2, h:2 * h, :], K.ps[:, 5, 0:h * P].rearrange("p (i q) -> p i q", i=h))\
                        .then_inc(s("high_out"), 1)
                    link(dve.reciprocal(rc[:, b, :], sm[:, b, :]))

                def do_out(b):
                    dve.wait_ge(s("pv"), b + 1)
                    dve.tensor_tensor(batches[b][4], K.ps[:, 6, 0:nm * 64].rearrange("p (m e) -> p m e", m=nm),
                                      spread(rc[:, b, :], 64), ALU.mult).then_inc(s("out"), 1)

                do_bias(0)
                do_bias(1)
                for b in range(NB):
                    copy_high(b)
                    if b >= 1:
                        do_out(b - 1)
                    if b + 2 < NB:
                        do_bias(b + 2)
                do_out(NB - 1)

            @block.gpsimd
            def _(pool):
                K.clear_old(pool)

            @block.sync
            def _(sp):
                K.stream.issue(sp)


def mixer_batches(K, B):
    out = []

    def heads(ap):
        return ap.rearrange("p (m e) -> p m e", m=HEADS)

    def batch(q, k, g, T, bias, scale, dst):
        return (lambda m: (q(m)[:, T * P:(T + 1) * P], k(m)),
                lambda m, kb: B.v[:, g, kb, m * 64:(m + 1) * 64], bias, scale, heads(dst), None, T + 1)

    for T in range(NT):
        for c in range(2):
            out.append(batch(lambda m, c=c: B.qa[:, 2 * m + c, :], lambda m, c=c: B.ka[:, 2 * m + c, :], 0, T,
                             K.alibi(T), 32 ** -0.5, B.o[:, T, 0:GROUP] if c == 0 else B.o1[:, T, :]))
        out.append(batch(lambda m: B.qb[:, m, :], lambda m: B.kb[:, m, :], 1, T, bcast(K.mask(T), HEADS),
                         96 ** -0.5, B.o[:, T, GROUP:2 * GROUP]))
        out.append(batch(lambda m: B.qd[:, m, :], lambda m: B.kd[:, m, :], 3, T, B.band[:, T], 64 ** -0.5,
                         B.o[:, T, 3 * GROUP:4 * GROUP]))
        out.append(batch(lambda m: B.qc[:, m, :], lambda m: B.kc[:, m, :], 2, T, B.sparse[:, T], 64 ** -0.5,
                         B.o[:, T, 2 * GROUP:3 * GROUP]))
    return out


def phase_mix_out(K, l, B):
    nc, st = K.nc, K.stream
    lam_init = 0.8 - 0.6 * float(np.exp(-0.3 * l))
    with ExitStack() as ctx:
        s = K.signals(f"mix{l}")

        def sb(name, shape):
            return ctx.enter_context(nc.sbuf_tensor(f"mix{l}_{name}", shape, F32))

        od = sb("od", [P, NT, GROUP])
        sq = sb("sq", [P, NT, GROUP])
        st8 = sb("st8", [P, 3, NT * HEADS])
        gd = sb("gd", [P, 64])
        with nc.Block() as block:
            @block.vector
            def _(dve):
                link = Link(dve, s("chain"))
                dve.tensor_scalar(gd[:], K.r(f"dng{l}"), 1.0 - lam_init, None, ALU.mult)
                link(dve.scalar_tensor_tensor(out=od[:], in0=B.o1[:], scalar=K.lam[:, 1:2], in1=B.o[:, :, 0:GROUP],
                                              op0=ALU.mult, op1=ALU.add))
                link(dve.tensor_tensor(sq[:], od[:], od[:], ALU.mult))
                link(dve.tensor_reduce(st8[:, 0, :], sq[:].rearrange("p t (h e) -> p (t h) e", h=HEADS), AX.X, ALU.add))
                dve.tensor_scalar(st8[:, 1, :], st8[:, 0, :], 1.0 / 64, EPS, ALU.mult, ALU.add).then_inc(s("ms"), 1)
                dve.wait_ge(s("root"), 1)
                link(dve.reciprocal(st8[:, 0, :], st8[:, 2, :]))
                ov = od[:].rearrange("p t (h e) -> p (t h) e", h=HEADS)
                link(dve.tensor_tensor(ov, ov, spread(st8[:, 0, :], 64), ALU.mult))
                dve.tensor_tensor(sq[:].rearrange("p t (h e) -> p (t h) e", h=HEADS), ov, bcast(gd[:], NT * HEADS),
                                  ALU.mult).then_inc(s("diff"), 1)
                for i in range(KT):
                    dve.wait_ge(s("y"), i + 1)
                    dve.scalar_tensor_tensor(out=K.xT[:, i, :], in0=K.ps[:, 4 + i % 4, 0:L], scalar=K.mod[l][:, 0, 16 + i:17 + i],
                                             in1=K.xT[:, i, :], op0=ALU.mult, op1=ALU.add).then_inc(s("res"), 1)

            @block.scalar
            def _(act):
                act.wait_ge(s("ms"), 1)
                act.activation(st8[:, 2, :], st8[:, 1, :], ACT.Sqrt).then_inc(s("root"), 1)
                for i in range(KT):
                    act.wait_ge(s("turned"), i + 1)
                    act.activation(K.hT[:, (i + 2) % KT, :], K.ps[:, i % 4, 0:L], ACT.Copy).then_inc(s("oT"), 1)

            @block.tensor
            def _(pe):
                for i in range(KT):
                    f = (i + 2) % KT
                    if f == 0:
                        pe.wait_ge(s("diff"), 1)
                    if i >= 4:
                        pe.wait_ge(s("oT"), i - 3)
                    for T in range(NT):
                        src = sq[:, T, f * P:(f + 1) * P] if f < 2 else B.o[:, T, f * P:(f + 1) * P]
                        mm = pe.transpose(K.ps[:, i % 4, T * P:(T + 1) * P], src, K.a("ident"))
                    mm.then_inc(s("turned"), 1)
                pe.wait_ge(s("oT"), KT)
                for c in range(KT // CT):
                    n = st.take()
                    st.wait(pe, n)
                    w = st.view(n, KT, CW)
                    for m in range(CT):
                        i = CT * c + m
                        if i >= 4:
                            pe.wait_ge(s("res"), i - 3)
                        for k in range(KT):
                            mm = pe.matmul(K.ps[:, 4 + i % 4, 0:L], w[:, k, m * P:(m + 1) * P], K.hT[:, k, :],
                                           start=(k == 0), stop=(k == KT - 1))
                        mm.then_inc(s("y"), 1)
                    pe.wait_ge(s("y"), CT * (c + 1))
                    pe.sem_inc(st.freed[n % RING], 1)

            @block.gpsimd
            def _(pool):
                K.clear_old(pool)

            @block.sync
            def _(sp):
                st.issue(sp)


class MixerBuffers:
    def __init__(self, nc, ctx, l):
        def sb(name, shape):
            return ctx.enter_context(nc.sbuf_tensor(f"mixer{l}_{name}", shape, F32))
        self.qa, self.ka = sb("qa", [32, 8, L]), sb("ka", [32, 8, L])
        self.qb, self.kb = sb("qb", [96, HEADS, L]), sb("kb", [96, HEADS, L])
        self.qc, self.kc = sb("qc", [64, HEADS, L]), sb("kc", [64, HEADS, L])
        self.qd, self.kd = sb("qd", [64, HEADS, L]), sb("kd", [64, HEADS, L])
        self.v = sb("v", [P, 4, NT, GROUP])
        self.sparse = sb("sparse", [P, NT, HEADS, L])
        self.band = sb("band", [P, NT, HEADS, L])


def mixer(K, l):
    nc = K.nc
    with ExitStack() as ctx:
        B = MixerBuffers(nc, ctx, l)
        phase_norm(K, f"mnorm{l}", K.xT, K.hT, K.gain[l][:, 0, :], K.mod[l][:, 0, 0:8])
        with ExitStack() as early:
            def sb(name, shape):
                return early.enter_context(nc.sbuf_tensor(f"mixer{l}_{name}", shape, F32))
            B.qi, B.ki = sb("qi", [32, 8, L]), sb("ki", [32, 1, L])
            B.qdT, B.kvdT, B.krT = sb("qdT", [P, 2, L]), sb("kvdT", [P, 1, L]), sb("krT", [32, 1, L])
            B.wi = sb("wi", [P, NT, 8])
            phase_project(K, f"proj{l}", mixer_projections(K, B), K.ada_project[l], l)
            phase_latent(K, l, B)
            phase_index(K, l, B)
        B.o = ctx.enter_context(nc.sbuf_tensor(f"mixer{l}_o", [P, NT, D], F32))
        B.o1 = ctx.enter_context(nc.sbuf_tensor(f"mixer{l}_o1", [P, NT, GROUP], F32))
        phase_attention(K, f"att{l}", B, mixer_batches(K, B), HEADS, NT)
        phase_mix_out(K, l, B)


def phase_ffn(K, name, gate, conv=None, beside=()):
    nc, st = K.nc, K.stream
    NF = FF // P
    with ExitStack() as ctx:
        s = K.signals(name)

        def sb(nm_, shape):
            return ctx.enter_context(nc.sbuf_tensor(f"{name}_{nm_}", shape, F32))

        g = sb("g", [P, 2, L])
        h = sb("h", [P, 2, L])
        pad = sb("pad", [P, 2, L + 2])
        y = sb("y", [P, 3, L])
        mine = [st.take() for _ in range(3 * (NF // CT))]

        def items(i):
            return mine[3 * (i // CT):3 * (i // CT) + 3]

        def up(i, j):
            return K.ps[:, 4 + i % 2, j * L:(j + 1) * L]

        thirds = []
        for x, (l, i) in enumerate(beside):
            if i % KT == KT - 1:
                first_acc = sum(len(third[2]) for third in thirds)
                accs = [first_acc + v for v in range(2 if l == 2 else 1)]
                thirds.append((l, i // KT, accs, min(NF * (x + 1) // len(beside) + 1, NF - 1)))
        if beside:
            acc = sb("acc", [P, 3, ADA_W])
        sums = [(l, v, j, 6, 16 * (2 * x + v)) for x, (l, j, accs, _) in enumerate(thirds) for v in range(len(accs))]

        with nc.Block() as block:
            @block.tensor
            def _(pe):
                def do_sums(x):
                    _, _, accs, _ = thirds[x]
                    pe.wait_ge(s("third"), x + 1)
                    for v, a in enumerate(accs):
                        mm = ada_sum(K, pe, acc[:, a, :], 6, 16 * (2 * x + v), start=(x == 0 and v == 0))
                    mm.then_inc(s("summed"), 1)

                def do_up(i):
                    n1, n3, _ = items(i)
                    for j, n in enumerate((n1, n3)):
                        if i % CT == 0:
                            st.wait(pe, n)
                        w = st.view(n, KT, CW)
                        for k in range(KT):
                            mm = pe.matmul(up(i, j), w[:, k, (i % CT) * P:(i % CT + 1) * P], K.hT[:, k, :],
                                           start=(k == 0), stop=(k == KT - 1))
                            if j == 1 and k == 0 and i % CT == CT - 1:
                                st.free(mm, n1)
                    mm.then_inc(s("up"), 1)

                def do_down(i):
                    n2 = items(i)[2]
                    if i % CT == 0:
                        st.wait(pe, n2)
                    pe.wait_ge(s("h"), i + 1)
                    w = st.view(n2, CT, D)
                    for f in range(KT):
                        mm = pe.matmul(K.ps[:, f // 2, (f % 2) * L:(f % 2 + 1) * L], w[:, i % CT, f * P:(f + 1) * P],
                                       h[:, i % 2, :], start=(i == 0 and f % 2 == 0), stop=(i == NF - 1),
                                       skip_group_check=True)
                        if f == 0 and (i + 1) % CT == CT - 1:
                            st.free(mm, items(i + 1)[1])
                    if i % CT == CT - 1:
                        st.free(mm, n2)

                do_up(0)
                for i in range(1, NF):
                    do_up(i)
                    do_down(i - 1)
                    for x, third in enumerate(thirds):
                        if third[3] == i:
                            do_sums(x)
                do_down(NF - 1)
                pe.matmul(K.ps[:, 4, 0:1], K.a("ident"), K.a("ones")[:, 0:1], start=True, stop=True).then_inc(s("down"), 1)

            @block.scalar
            def _(act):
                for i in range(NF):
                    if conv is None:
                        act.wait_ge(s("up"), i + 1)
                        act.activation(g[:, i % 2, :], up(i, 0), ACT.Silu).then_inc(s("g"), 1)
                        continue
                    act.wait_ge(s("up"), i + 1)
                    act.wait_ge(s("padded"), 2)
                    if i >= 2:
                        act.wait_ge(s("conv"), i - 1)
                    act.activation(pad[:, i % 2, 1:L + 1], up(i, 0), ACT.Copy).then_inc(s("pad"), 1)
                    act.wait_ge(s("conv"), i + 1)
                    act.activation(g[:, i % 2, :], y[:, 2, :], ACT.Gelu_apprx_tanh).then_inc(s("g"), 1)

            @block.vector
            def _(dve):
                link = Link(dve, s("chain"))
                if conv is not None:
                    dve.memset(pad[:, :, 0:1], 0.0).then_inc(s("padded"), 1)
                    dve.memset(pad[:, :, L + 1:L + 2], 0.0).then_inc(s("padded"), 1)
                for i in range(NF):
                    if conv is not None:
                        w, b = conv
                        dve.wait_ge(s("padded"), 2)
                        dve.wait_ge(s("pad"), i + 1)
                        q = pad[:, i % 2, :]
                        link(dve.tensor_scalar(y[:, 0, :], q[:, 1:L + 1], w(1, i), b(i), ALU.mult, ALU.add))
                        link(dve.scalar_tensor_tensor(out=y[:, 1, :], in0=q[:, 0:L], scalar=w(0, i), in1=y[:, 0, :],
                                                      op0=ALU.mult, op1=ALU.add))
                        dve.scalar_tensor_tensor(out=y[:, 2, :], in0=q[:, 2:L + 2], scalar=w(2, i), in1=y[:, 1, :],
                                                 op0=ALU.mult, op1=ALU.add).then_inc(s("conv"), 1)
                    for l, a in share(beside, i, NF):
                        x = [t[0:2] for t in thirds].index((l, a // KT))
                        ada_accumulate(K, dve, link, l, a, [acc[:, b, :] for b in thirds[x][2]])
                        if a % KT == KT - 1:
                            dve.sem_inc(s("third"), 1)
                    dve.wait_ge(s("g"), i + 1)
                    dve.tensor_tensor(h[:, i % 2, :], g[:, i % 2, :], up(i, 1), ALU.mult).then_inc(s("h"), 1)
                dve.wait_ge(s("down"), 1)
                for f in range(KT):
                    dve.scalar_tensor_tensor(out=K.xT[:, f, :], in0=K.ps[:, f // 2, (f % 2) * L:(f % 2 + 1) * L],
                                             scalar=gate[:, f:f + 1], in1=K.xT[:, f, :], op0=ALU.mult, op1=ALU.add)
                if beside:
                    dve.wait_ge(s("summed"), len(thirds))
                    ada_finish(K, dve, link, sums)

            @block.gpsimd
            def _(pool):
                K.clear_old(pool)

            @block.sync
            def _(sp):
                st.issue(sp)


def moe(K, A):
    nc = K.nc
    with ExitStack() as ctx:
        def sb(name, shape, dt=F32):
            return ctx.enter_context(nc.sbuf_tensor(f"moe_{name}", shape, dt))
        M = Kit()
        M.cc = sb("const_c", [P, WIDTH_C])
        M.c = lambda n: M.cc[:, COLS_C[n][0]:sum(COLS_C[n])]
        M.gate = sb("gate", [P, NE * L])
        M.rankB = sb("rankB", [P, NE * L])
        M.member = sb("member", [P, NT, NE + 1])
        M.rank = sb("rank", [P, NT, NE + 1])
        M.hk = sb("hk", [P, NT, D])
        M.count = sb("count", [1, NE + 1], mybir.dt.int32)
        phase_route(K, A, M)
        phase_experts(K, A, M)


def phase_route(K, A, M):
    nc = K.nc
    with ExitStack() as ctx:
        s = K.signals("route")

        def sb(nm_, shape):
            return ctx.enter_context(nc.sbuf_tensor(f"route_{nm_}", shape, F32))

        wr = sb("wr", [P, KT, NE])
        lg = sb("lg", [P, NT, NE])
        top = sb("top", [P, NT, 8])
        e = sb("e", [P, NT, 4])
        m = sb("m", [P, NT, 8, NE])
        zero = sb("zero", [P, NE])
        rows = sb("rows", [NE, 2, L])
        with nc.Block() as block:
            @block.tensor
            def _(pe):
                pe.wait_ge(s("wr"), 16)
                for T in range(NT):
                    for k in range(KT):
                        mm = pe.matmul(K.ps[:, T, 0:NE], K.hT[:, k, T * P:(T + 1) * P], wr[:, k, :],
                                       start=(k == 0), stop=(k == KT - 1))
                    mm.then_inc(s("logits"), 1)
                for i in range(NT * 2):
                    T, q = i // 2, i % 2
                    if i >= 2:
                        pe.wait_ge(s("hk"), i - 1)
                    for f in range(4):
                        mm = pe.transpose(K.ps[:, 6 + q, f * P:(f + 1) * P], K.hT[:, 4 * q + f, T * P:(T + 1) * P],
                                          K.a("ident"))
                    mm.then_inc(s("turned"), 1)
                pe.wait_ge(s("wr"), 32)
                pe.wait_ge(s("member"), NT)
                before = M.c("before").rearrange("p (r t) -> p r t", r=NT)
                for T in range(NT):
                    for r in range(NT):
                        mm = pe.matmul(K.ps[:, 3, T * NE:(T + 1) * NE], before[:, r, T * P:(T + 1) * P],
                                       M.member[:, r, 0:NE], start=(r == 0), stop=(r == NT - 1))
                for r in range(NT):
                    mm = pe.matmul(K.ps[0:1, 3, 2 * NE:3 * NE + 1], K.a("ones")[:, 0:1], M.member[:, r, :],
                                   start=(r == 0), stop=(r == NT - 1))
                mm.then_inc(s("numbers"), 1)
                pe.wait_ge(s("combine"), NT)
                pe.wait_ge(s("rank"), 1)
                for T in range(NT):
                    pe.transpose(K.ps[0:NE, 2, T * P:(T + 1) * P], m[:, T, 7, :], K.a("ident"))
                for T in range(NT):
                    mm = pe.transpose(K.ps[0:NE, 2, L + T * P:L + (T + 1) * P], M.rank[:, T, 0:NE], K.a("ident"))
                mm.then_inc(s("rows"), 1)
                pe.wait_ge(s("rows_out"), 1)
                pe.wait_ge(s("hk"), 2 * NT)
                for x in range(NE):
                    if x >= 4:
                        pe.wait_ge(s("gate"), x - 3)
                        pe.wait_ge(s("rankB"), x - 3)
                    for j in range(2):
                        mm = pe.matmul(K.ps[:, 4 * j + x % 4, 0:L], K.a("pick")[0:NE, x * P:(x + 1) * P], rows[:, j, :],
                                       start=True, stop=True)
                        mm.then_inc(s("spread"), 1)

            @block.scalar
            def _(act):
                act.dma_start(wr[:], A["moe_router"][0].rearrange("(k p) n -> p k n", p=P)).then_inc(s("wr"), 16)
                act.wait_ge(s("wr"), 16)
                act.dma_start(M.cc[:], A["const_c"]).then_inc(s("wr"), 16)
                for i in range(NT * 2):
                    T, q = i // 2, i % 2
                    act.wait_ge(s("turned"), i + 1)
                    act.activation(M.hk[:, T, q * 512:(q + 1) * 512], K.ps[:, 6 + q, :], ACT.Copy).then_inc(s("hk"), 1)
                for T in range(NT):
                    act.wait_ge(s("gap"), T + 1)
                    act.activation(e[:, T, 1:2], e[:, T, 0:1], ACT.Exp).then_inc(s("exp"), 1)
                act.wait_ge(s("rows"), 1)
                act.activation(rows[:], K.ps[0:NE, 2, :].rearrange("p (j t) -> p j t", j=2), ACT.Copy)\
                   .then_inc(s("rows_out"), 1)
                for x in range(NE):
                    act.wait_ge(s("spread"), 2 * x + 1)
                    act.activation(M.gate[:, x * L:(x + 1) * L], K.ps[:, x % 4, 0:L], ACT.Copy).then_inc(s("gate"), 1)

            @block.vector
            def _(dve):
                link = Link(dve, s("chain"))
                link(dve.memset(M.member[:], 0.0))
                link(dve.memset(M.rank[:], 0.0))
                link(dve.memset(zero[:], 0.0))
                for T in range(NT):
                    mk = m[:, T]
                    dve.wait_ge(s("logits"), T + 1)
                    link(dve.tensor_copy(lg[:, T, :], K.ps[:, T, 0:NE]))
                    link(dve.max(top[:, T, :], lg[:, T, :]))
                    dve.tensor_tensor(e[:, T, 0:1], top[:, T, 1:2], top[:, T, 0:1], ALU.subtract).then_inc(s("gap"), 1)
                    link(dve.tensor_scalar(mk[:, 0, :], lg[:, T, :], top[:, T, 0:1], None, ALU.is_equal))
                    link(dve.tensor_tensor_scan(mk[:, 1, :], mk[:, 0, :], zero[:], 0.0, ALU.add, ALU.add))
                    link(dve.scalar_tensor_tensor(out=mk[:, 2, :], in0=mk[:, 1, :], scalar=1.0, in1=mk[:, 0, :],
                                                  op0=ALU.is_equal, op1=ALU.mult))
                    link(dve.scalar_tensor_tensor(out=mk[:, 3, :], in0=mk[:, 2, :], scalar=NEG, in1=lg[:, T, :],
                                                  op0=ALU.mult, op1=ALU.add))
                    link(dve.tensor_scalar(mk[:, 4, :], mk[:, 3, :], top[:, T, 1:2], None, ALU.is_equal))
                    link(dve.tensor_tensor_scan(mk[:, 5, :], mk[:, 4, :], zero[:], 0.0, ALU.add, ALU.add))
                    link(dve.scalar_tensor_tensor(out=mk[:, 6, :], in0=mk[:, 5, :], scalar=1.0, in1=mk[:, 4, :],
                                                  op0=ALU.is_equal, op1=ALU.mult))
                    dve.tensor_tensor(M.member[:, T, 0:NE], mk[:, 2, :], mk[:, 6, :], ALU.add).then_inc(s("member"), 1)
                    dve.wait_ge(s("exp"), T + 1)
                    link(dve.tensor_scalar(e[:, T, 2:3], e[:, T, 1:2], 1.0, None, ALU.add))
                    link(dve.reciprocal(e[:, T, 3:4], e[:, T, 2:3]))
                    link(dve.scalar_tensor_tensor(out=mk[:, 1, :], in0=mk[:, 6, :], scalar=e[:, T, 1:2], in1=mk[:, 2, :],
                                                  op0=ALU.mult, op1=ALU.add))
                    dve.tensor_scalar(mk[:, 7, :], mk[:, 1, :], e[:, T, 3:4], None, ALU.mult).then_inc(s("combine"), 1)
                dve.wait_ge(s("numbers"), 1)
                dve.tensor_copy(M.count[:], K.ps[0:1, 3, 2 * NE:3 * NE + 1])
                dve.tensor_copy(M.rank[:, :, 0:NE], K.ps[:, 3, 0:NT * NE].rearrange("p (t e) -> p t e", t=NT))\
                    .then_inc(s("rank"), 1)
                for x in range(NE):
                    dve.wait_ge(s("spread"), 2 * x + 2)
                    dve.tensor_copy(M.rankB[:, x * L:(x + 1) * L], K.ps[:, 4 + x % 4, 0:L]).then_inc(s("rankB"), 1)

            @block.gpsimd
            def _(pool):
                K.clear_old(pool)

            @block.sync
            def _(sp):
                K.stream.issue(sp)


def phase_experts(K, A, M):
    nc, st = K.nc, K.stream
    NF = FFE // P
    PER = 3 * NF // CT
    assert PER % RING == 0
    m0 = K.moe_first
    assert st.taken == m0 and st.issued == m0 + RING
    rounds = PER // RING
    w1 = A["moe_w1"][0].rearrange("e (k p) n -> p (e k) n", p=P)
    w3 = A["moe_w3"][0].rearrange("e (k p) n -> p (e k) n", p=P)
    w2 = A["moe_w2"][0].rearrange("e (k p) n -> p (e k) n", p=P)
    with ExitStack() as ctx:
        s = K.signals("moe")

        def sb(nm_, shape):
            return ctx.enter_context(nc.sbuf_tensor(f"experts_{nm_}", shape, F32))

        g = sb("g", [P, 2, L])
        h = sb("h", [P, 2, L])
        pick_in = sb("pick_in", [P, NT, L])
        pick_out = sb("pick_out", [P, NT, L])
        xg = sb("xg", [P, KT, L])
        y = sb("y", [P, NT, D])

        def items(i):
            return [m0 + 3 * (i // CT) + j for j in range(3)]

        def up(i, j):
            return K.ps[:, 4 + i % 2, j * L:(j + 1) * L]

        with nc.Block() as block:
            @block.tensor
            def _(pe):
                def gather(e, N, last_item=None):
                    for f in range(KT):
                        if f >= 2:
                            pe.wait_ge(s(("xg_act", "xg_dve")[f % 2]), e * (KT // 2) + f // 2)
                        for r in range(NT):
                            mm = pe.matmul(K.ps[:, 6 + f % 2, 0:N], M.hk[:, r, f * P:(f + 1) * P],
                                           pick_in[:, r, 0:N], start=(r == 0), stop=(r == NT - 1))
                            if f == 0 and r == 0 and last_item is not None:
                                st.free(mm, last_item)
                        mm.then_inc(s("gathered"), 1)

                def expert(e, N):
                    rows = min(N, P)
                    tiles = (N + P - 1) // P

                    def arrived(n):
                        pe.wait_ge(st.loaded[n % RING], e * (16 * rounds) + st.arrival[n])

                    def do_up(i):
                        n1, n3, _ = items(i)
                        for j, n in enumerate((n1, n3)):
                            if i % CT == 0:
                                arrived(n)
                            w = st.view(n, KT, CW)
                            for k in range(KT):
                                if i == 0 and j == 0:
                                    pe.wait_ge(s(("xg_act", "xg_dve")[k % 2]), e * (KT // 2) + k // 2 + 1)
                                mm = pe.matmul(up(i, j)[:, 0:N], w[:, k, (i % CT) * P:(i % CT + 1) * P], xg[:, k, 0:N],
                                               start=(k == 0), stop=(k == KT - 1))
                                if j == 1 and k == 0 and i % CT == CT - 1:
                                    st.free(mm, n1)
                            mm = mm
                        mm.then_inc(s("up"), 1)

                    def do_down(i):
                        n2 = items(i)[2]
                        if i % CT == 0:
                            arrived(n2)
                        pe.wait_ge(s("h"), e * NF + i + 1)
                        if i == 0:
                            pe.wait_ge(s("added"), e * KT + 1)
                        w = st.view(n2, CT, D)
                        for t in range(tiles):
                            for half in range(2):
                                mm = pe.matmul(K.ps[0:rows, 2 * t + half, :], h[:, i % 2, t * P:t * P + rows],
                                               w[:, i % CT, half * 512:(half + 1) * 512],
                                               start=(i == 0), stop=(i == NF - 1), skip_group_check=True)
                                if t == 0 and half == 0 and i + 1 < NF and (i + 1) % CT == CT - 1:
                                    st.free(mm, items(i + 1)[1])
                        if i == NF - 1:
                            mm.then_inc(s("down"), 1)
                        elif i % CT == CT - 1:
                            st.free(mm, n2)

                    do_up(0)
                    for i in range(1, NF):
                        do_up(i)
                        do_down(i - 1)
                    do_down(NF - 1)

                def scatter(e, N):
                    rows = min(N, P)
                    tiles = (N + P - 1) // P
                    for f in range(KT):
                        if f >= 4:
                            pe.wait_ge(s("added"), e * KT + f - 2)
                        for t in range(tiles):
                            mm = pe.matmul(K.ps[:, f % 4, 0:L], y[0:rows, t, f * P:(f + 1) * P],
                                           pick_out[0:rows, t, :], start=(t == 0), stop=(t == tiles - 1))
                        mm.then_inc(s("scattered"), 1)

                def by_count(tokens, step):
                    with pe.If(tokens < 97):
                        step(96)
                    with pe.Else():
                        with pe.If(tokens < 129):
                            step(128)
                        with pe.Else():
                            step(L)

                pe.wait_ge(s("pick_in"), 1)
                gather(0, L)
                with pe.Fori(0, NE) as e:
                    tokens = pe.value_load(M.count[0:1, bass.ds(e, 1)], min_val=0, max_val=L)
                    by_count(tokens, lambda N: expert(e, N))
                    pe.wait_ge(s("pick_in"), e + 2)
                    next_tokens = pe.value_load(M.count[0:1, bass.ds(e + 1, 1)], min_val=0, max_val=L)
                    by_count(next_tokens, lambda N: gather(e + 1, N, items(NF - 1)[2]))
                    pe.wait_ge(s("y_act"), e * NT + NT)
                    pe.wait_ge(s("y_dve"), e * NT + NT)
                    pe.wait_ge(s("pick_out"), e + 1)
                    by_count(tokens, lambda N: scatter(e, N))

            @block.scalar
            def _(act):
                def take_tokens(e):
                    for f in range(0, KT, 2):
                        act.wait_ge(s("gathered"), e * KT + f + 1)
                        act.activation(xg[:, f, :], K.ps[:, 6, 0:L], ACT.Copy).then_inc(s("xg_act"), 1)

                take_tokens(0)
                with act.Fori(0, NE) as e:
                    for i in range(NF):
                        act.wait_ge(s("up"), e * NF + i + 1)
                        act.activation(g[:, i % 2, :], up(i, 0), ACT.Silu).then_inc(s("g"), 1)
                    act.wait_ge(s("down"), e + 1)
                    for t in range(NT):
                        act.activation(y[:, t, 0:512], K.ps[:, 2 * t, :], ACT.Copy).then_inc(s("y_act"), 1)
                    take_tokens(e + 1)

            @block.vector
            def _(dve):
                def pick_tokens(e):
                    for T in range(NT):
                        x = dve.tensor_scalar(pick_in[:, T, :], M.c("slots"), M.rank[:, T, bass.ds(e, 1)],
                                              M.member[:, T, bass.ds(e, 1)], ALU.is_equal, ALU.mult)
                    x.then_inc(s("pick_in"), 1)

                def take_tokens(e):
                    for f in range(1, KT, 2):
                        dve.wait_ge(s("gathered"), e * KT + f + 1)
                        dve.tensor_copy(xg[:, f, :], K.ps[:, 7, 0:L]).then_inc(s("xg_dve"), 1)

                pick_tokens(0)
                dve.sem_inc(s("added"), 1)
                take_tokens(0)
                with dve.Fori(0, NE) as e:
                    pick_tokens(e + 1)
                    for t in range(NT):
                        x = dve.scalar_tensor_tensor(out=pick_out[:, t, :], in0=M.rankB[:, bass.ds(e * L, L)],
                                                     scalar=M.c("slot_of")[:, t:t + 1], in1=M.gate[:, bass.ds(e * L, L)],
                                                     op0=ALU.is_equal, op1=ALU.mult)
                    x.then_inc(s("pick_out"), 1)
                    for i in range(NF):
                        dve.wait_ge(s("g"), e * NF + i + 1)
                        dve.tensor_tensor(h[:, i % 2, :], g[:, i % 2, :], up(i, 1), ALU.mult).then_inc(s("h"), 1)
                    dve.wait_ge(s("down"), e + 1)
                    for t in range(NT):
                        dve.tensor_copy(y[:, t, 512:1024], K.ps[:, 2 * t + 1, :]).then_inc(s("y_dve"), 1)
                    take_tokens(e + 1)
                    for f in range(KT):
                        dve.wait_ge(s("scattered"), e * KT + f + 1)
                        dve.scalar_tensor_tensor(out=K.xT[:, f, :], in0=K.ps[:, f % 4, 0:L],
                                                 scalar=K.mod[1][:, 0, 40 + f:41 + f], in1=K.xT[:, f, :],
                                                 op0=ALU.mult, op1=ALU.add).then_inc(s("added"), 1)

            @block.gpsimd
            def _(pool):
                K.clear_old(pool)

            @block.sync
            def _(sp):
                def load(n, e):
                    j = n - m0
                    jj, de = j % PER, j // PER
                    c, kind = jj // 3, jj % 3
                    slot = n % RING
                    sp.wait_ge(st.freed[slot], e * rounds + n // RING)
                    if kind == 2:
                        src, kt, wd = w2[:, bass.ds((e + de) * NF + CT * c, CT), :], CT, D
                    else:
                        src = (w1, w3)[kind][:, bass.ds((e + de) * KT, KT), CW * c:CW * (c + 1)]
                        kt, wd = KT, CW
                    sp.dma_start(st.view(n, kt, wd), src).then_inc(st.loaded[slot], 16)

                with sp.Fori(0, NE - 1) as e:
                    for n in range(m0 + RING, m0 + RING + PER):
                        load(n, e)
                st.issued = m0 + RING + (NE - 1) * PER
                st.taken = st.at["pe"] = m0 + NE * PER
                st.issue(sp)



MH = 4
DH = 128
VW = DH + 1


class SecondBuffers:
    def __init__(self, nc, ctx):
        def sb(name, shape):
            return ctx.enter_context(nc.sbuf_tensor(f"second_{name}", shape, F32))
        self.qm, self.km, self.kcm = sb("qm", [P, MH, L]), sb("km", [P, MH, L]), sb("kcm", [P, MH, L])
        self.va, self.vca = sb("va", [P, NT, MH, VW]), sb("vca", [P, NT, MH, VW])
        self.og = sb("og", [P, MH, L])
        self.qh = sb("qh", [64, 8, L])
        self.kh = sb("kh", [64, 2, 2 * L])
        self.vh = sb("vh", [P, 2 * NT, P])
        self.gt = sb("gt", [P, 2 * NT, 16])


def second_projections(K, B, pads):
    st = K.stream
    jobs = []
    qpad, kpad, kcpad, hc = pads

    def item(width):
        n = st.take()
        return n, st.view(n, KT, width)

    def heads(sources):
        for half in range(MH // CT):
            n, w = item(CW)
            for j, (src, dst) in enumerate(sources):
                for i in range(CT):
                    jobs.append(feature_job(K, n, i * P, P, src, [(dst(CT * half + i), 0, P)], w,
                                            last=(i == 1 and j == len(sources) - 1)))

    heads([(K.hT, lambda h: qpad[:, h, 1:L + 1])])
    heads([(K.hT, lambda h: kpad[:, h, 1:L + 1]), (hc, lambda h: kcpad[:, h, 1:L + 1])])
    for half in range(MH // CT):
        n, w = item(CW)
        for src, dst, c in ((K.hT, B.va, 0), (hc, B.vca, 1)):
            for T in range(NT):
                jobs.append(token_job(K, n, 0, CW, src, T, dst[:, T, CT * half:CT * (half + 1), 0:DH], w,
                                      last=(T == 1 and c == 1), shape=CT))
    heads([(K.hT, lambda h: B.og[:, h, :])])
    for half in range(2):
        n, w = item(CW)
        for j in range(CT):
            i = CT * half + j
            jobs.append(feature_job(K, n, j * P, P, K.hT, [(B.qh[:, 2 * i, :], 0, 64), (B.qh[:, 2 * i + 1, :], 64, 64)],
                                    w, last=(j == 1)))
    n, w = item(CW)
    for src, c in ((K.hT, 0), (hc, 1)):
        jobs.append(feature_job(K, n, 0, P, src, [(B.kh[:, 0, c * L:(c + 1) * L], 0, 64),
                                                  (B.kh[:, 1, c * L:(c + 1) * L], 64, 64)], w))
        for T in range(NT):
            jobs.append(token_job(K, n, P, P, src, T, B.vh[:, NT * c + T, :], w, last=(c == 1 and T == 1)))
    n, w = item(16)
    for src, c in ((K.hT, 0), (hc, 1)):
        for T in range(NT):
            jobs.append(token_job(K, n, 0, 16, src, T, B.gt[:, NT * c + T, :], w, last=(c == 1 and T == 1)))
    return jobs


def phase_shape(K, B, pads, lf):
    nc = K.nc
    qpad, kpad, kcpad, _ = pads
    with ExitStack() as ctx:
        s = K.signals("shape")

        def sb(nm_, shape):
            return ctx.enter_context(nc.sbuf_tensor(f"shape_{nm_}", shape, F32))

        y = sb("y", [P, 4, L])
        ab = sb("ab", [P, 3, 2 * NT, 16])
        t1 = sb("t1", [64, 2, L])
        tiles = [(qpad, i, i, B.qm) for i in range(MH)] + [(kpad, i, 4 + i, B.km) for i in range(MH)] + \
                [(kcpad, i, 4 + i, B.kcm) for i in range(MH)]
        ropes = [B.qh[:, i, :] for i in range(8)] + [B.kh[:, i, 0:L] for i in range(2)]
        with nc.Block() as block:
            @block.tensor
            def _(pe):
                for i, x in enumerate(ropes):
                    if i >= 4:
                        pe.wait_ge(s("roped"), i - 3)
                    pe.matmul(K.ps[0:64, i % 4, 0:L], K.b("permA")[0:64], x, start=True, stop=True)\
                        .then_inc(s("swapped"), 1)

            @block.scalar
            def _(act):
                act.activation(B.og[:], B.og[:], ACT.Sigmoid)
                act.wait_ge(s("gb"), 1)
                act.activation(ab[:, 0], B.gt[:], ACT.Abs).then_inc(s("abs"), 1)
                act.wait_ge(s("abs"), 1)
                act.activation(ab[:, 1], ab[:, 0], ACT.Exp, scale=-1.0).then_inc(s("ex"), 1)
                act.wait_ge(s("ex"), 1)
                act.activation(ab[:, 2], ab[:, 1], ACT.Ln, bias=1.0).then_inc(s("ln"), 1)
                for i, (_, h, _, dst) in enumerate(tiles):
                    act.wait_ge(s("conv"), i + 1)
                    act.activation(dst[:, h, :], y[:, 2 + i % 2, :], ACT.Silu).then_inc(s("silu"), 1)

            @block.vector
            def _(dve):
                link = Link(dve, s("chain"))
                dve.tensor_tensor(B.gt[:], B.gt[:], bcast(K.r("gate_b"), 2 * NT), ALU.add).then_inc(s("gb"), 1)
                dve.memset(B.va[:, :, :, DH:VW], 1.0)
                dve.memset(B.vca[:, :, :, DH:VW], 1.0)
                for i, x in enumerate(ropes):
                    dve.wait_ge(s("swapped"), i + 1)
                    link(dve.tensor_tensor(t1[:, 0, :], K.ps[0:64, i % 4, 0:L], K.b("sinA")[0:64], ALU.mult))
                    link(dve.tensor_tensor(t1[:, 1, :], x, K.b("cosA")[0:64], ALU.mult))
                    link(dve.tensor_tensor(x, t1[:, 0, :], t1[:, 1, :], ALU.add))
                    link(dve.memset(K.scratch1[:], 0.0))
                    dve.sem_inc(s("roped"), 1)
                for i, (src, h, c, _) in enumerate(tiles):
                    x = src[:, h, :]
                    wv = K.v("conv_w")
                    link(dve.tensor_scalar(y[:, 0, :], x[:, 1:L + 1], wv[:, 8 + c:9 + c], K.v("conv_b")[:, c:c + 1],
                                           ALU.mult, ALU.add))
                    link(dve.scalar_tensor_tensor(out=y[:, 1, :], in0=x[:, 0:L], scalar=wv[:, c:c + 1],
                                                  in1=y[:, 0, :], op0=ALU.mult, op1=ALU.add))
                    if i >= 2:
                        dve.wait_ge(s("silu"), i - 1)
                    dve.scalar_tensor_tensor(out=y[:, 2 + i % 2, :], in0=x[:, 2:L + 2], scalar=wv[:, 16 + c:17 + c],
                                             in1=y[:, 1, :], op0=ALU.mult, op1=ALU.add).then_inc(s("conv"), 1)
                    dve.wait_ge(s("conv"), i + 1)
                dve.wait_ge(s("ln"), 1)
                link(dve.tensor_scalar(ab[:, 0], B.gt[:], 0.0, None, ALU.min))
                dve.tensor_tensor(lf[:], ab[:, 0], ab[:, 2], ALU.subtract)

            @block.gpsimd
            def _(pool):
                K.clear_old(pool)

            @block.sync
            def _(sp):
                K.stream.issue(sp)


def phase_state(K, B, lf, C0, mB):
    nc = K.nc
    with ExitStack() as ctx:
        s = K.signals("state")

        def sb(nm_, shape):
            return ctx.enter_context(nc.sbuf_tensor(f"state_{nm_}", shape, F32))

        gr = sb("gr", [MH, 2, L])
        mr = sb("mr", [MH, 2, 2])
        dm = sb("dm", [MH, 2, MH])
        wc = sb("wc", [P, 2, NT, MH])
        kw = sb("kw", [P, 2, MH, NT, DH])
        col = {0: ("past_f", 0, 4), 1: ("past_b", 8, 12)}
        with nc.Block() as block:
            @block.tensor
            def _(pe):
                for d in range(2):
                    tab, ci, cf = col[d]
                    t = K.b(tab).rearrange("p (r s) -> p r s", r=NT)
                    o = K.ps[0:MH, d, 0:L]
                    for r in range(NT):
                        pe.matmul(o, lf[:, NT + r, cf:cf + MH], t[:, r, :], start=(r == 0), stop=False,
                                  skip_group_check=True)
                    for r in range(NT):
                        pe.matmul(o[:, r * P:(r + 1) * P], B.gt[:, NT + r, ci:ci + MH], K.a("ident"), start=False,
                                  stop=False, skip_group_check=True)
                    for r in range(NT):
                        mm = pe.matmul(K.ps[0:MH, d, L:L + 1], lf[:, NT + r, cf:cf + MH], K.a("ones")[:, 0:1],
                                       start=False, stop=(r == NT - 1), skip_group_check=True)
                    mm.then_inc(s("g"), 1)
                for h in range(MH):
                    for T in range(NT):
                        mm = pe.transpose(K.ps[:, 2 + h, T * P:(T + 1) * P], B.kcm[:, h, T * P:(T + 1) * P], K.a("ident"))
                    mm.then_inc(s("kt"), 1)
                for d in range(2):
                    pe.wait_ge(s("w"), d + 1)
                    for T in range(NT):
                        mm = pe.transpose(K.ps[:, 6, (2 * d + T) * MH:(2 * d + T + 1) * MH], gr[:, d, T * P:(T + 1) * P],
                                          K.a("ident")[0:MH, 0:MH])
                    mm.then_inc(s("wt"), 1)
                for d in range(2):
                    pe.wait_ge(s("dm"), d + 1)
                    pe.matmul(K.ps[:, 7, d * MH:(d + 1) * MH], K.a("ones")[0:MH], dm[:, d, :], start=True, stop=True)\
                        .then_inc(s("mB"), 1)
                for d in range(2):
                    for h in range(MH):
                        u = d * MH + h
                        pe.wait_ge(s("kw"), 2 * u + 2)
                        if u >= 2:
                            pe.wait_ge(s("c0"), u - 1)
                        for T in range(NT):
                            mm = pe.matmul(K.ps[:, u % 2, 0:VW], kw[:, d, h, T, :], B.vca[:, T, h, :],
                                           start=(T == 0), stop=(T == NT - 1))
                        mm.then_inc(s("c"), 1)

            @block.scalar
            def _(act):
                for d in range(2):
                    act.wait_ge(s("m"), d + 1)
                    act.activation(gr[:, d, :], K.ps[0:MH, d, 0:L], ACT.Exp, bias=mr[:, d, 0:1]).then_inc(s("w"), 1)
                for u in range(2 * MH):
                    act.wait_ge(s("c"), u + 1)
                    act.activation(C0[:, u, :], K.ps[:, u % 2, 0:VW], ACT.Copy).then_inc(s("c0"), 1)

            @block.vector
            def _(dve):
                link = Link(dve, s("chain"))
                for d in range(2):
                    dve.wait_ge(s("g"), d + 1)
                    dve.tensor_reduce(mr[:, d, 0:1], K.ps[0:MH, d, 0:L + 1], AX.X, ALU.max, negate=True)\
                        .then_inc(s("m"), 1)
                    dve.wait_ge(s("m"), d + 1)
                    dve.tensor_scalar(dm[:, d, :], K.a("ident")[0:MH, 0:MH], mr[:, d, 0:1], -1.0, ALU.mult, ALU.mult)\
                        .then_inc(s("dm"), 1)
                dve.wait_ge(s("mB"), 2)
                dve.tensor_copy(mB[:], K.ps[:, 7, 0:2 * MH])
                dve.wait_ge(s("wt"), 2)
                link(dve.tensor_scalar(wc[:].rearrange("p d t h -> p (d t h)"), K.ps[:, 6, 0:4 * MH], DH ** -0.5, None,
                                       ALU.mult))
                dve.wait_ge(s("kt"), MH)
                for d in range(2):
                    for h in range(MH):
                        for T in range(NT):
                            dve.tensor_scalar(kw[:, d, h, T, :], K.ps[:, 2 + h, T * P:(T + 1) * P],
                                              wc[:, d, T, h:h + 1], None, ALU.mult).then_inc(s("kw"), 1)

            @block.gpsimd
            def _(pool):
                K.clear_old(pool)

            @block.sync
            def _(sp):
                K.stream.issue(sp)


def phase_mlstm(K, B, lf, C0, mB, hid):
    nc = K.nc
    units = [(d, h, T) for d in range(2) for h in range(MH) for T in range(NT)]
    U = len(units)
    with ExitStack() as ctx:
        s = K.signals("mlstm")

        def sb(nm_, shape):
            return ctx.enter_context(nc.sbuf_tensor(f"mlstm_{nm_}", shape, F32))

        G = sb("G", [P, 2, NT, L + 2])
        gi = sb("gi", [P, 2, NT, P])
        Dm = sb("Dm", [P, 2, L + 1])
        E = sb("E", [P, 2, L + 1])
        S = sb("S", [P, 2, L])
        ST = sb("ST", [P, 2, L])
        nm = sb("nm", [P, U, 4])
        cm = sb("cm", [P, 2, VW])
        inter = sb("inter", [P, 2, VW])
        hd = sb("hd", [P, 2, DH])
        col = {0: ("upto_f", "past_f", "mask_f", 0, 4), 1: ("upto_b", "past_b", "mask_b", 8, 12)}

        def keys(u):
            d, _, T = units[u]
            return (0, T + 1) if d == 0 else (T, NT)

        def span(u):
            first_tile, end_tile = keys(u)
            return first_tile * P, end_tile * P

        tabs = {n: K.b(n).rearrange("p (r s) -> p r s", r=NT) for d in range(2) for n in col[d][0:3]}
        with nc.Block() as block:
            @block.tensor
            def _(pe):
                def front(u):
                    d, h, T = units[u]
                    g = u // NT
                    pe.wait_ge(s("G"), g + 1)
                    if u >= 2:
                        pe.wait_ge(s("S"), u - 1)
                    for r in range(NT):
                        mm = pe.matmul(K.ps[:, u % 2, 0:L + 2], tabs[col[d][0]][:, r, T * P:(T + 1) * P],
                                       G[:, g % 2, r, :], start=(r == 0), stop=(r == NT - 1))
                    mm.then_inc(s("D"), 1)
                    a, z = span(u)
                    pe.matmul(K.ps[:, 2 + u % 2, a:z], B.qm[:, h, T * P:(T + 1) * P], B.km[:, h, a:z], start=True, stop=True)\
                        .then_inc(s("qk"), 1)

                def back(u):
                    d, h, T = units[u]
                    pe.wait_ge(s("S"), u + 1)
                    for r in range(*keys(u)):
                        mm = pe.transpose(K.ps[:, 4, r * P:(r + 1) * P], S[:, u % 2, r * P:(r + 1) * P], K.a("ident"))
                    mm.then_inc(s("turned"), 1)
                    if u >= 1:
                        pe.wait_ge(s("sum"), u)
                    pe.matmul(K.ps[:, 5, 0:VW], B.qm[:, h, T * P:(T + 1) * P], C0[:, d * MH + h, :], start=True, stop=True)\
                        .then_inc(s("qc"), 1)
                    pe.wait_ge(s("ST"), u + 1)
                    for r in range(*keys(u)):
                        mm = pe.matmul(K.ps[:, 6, 0:VW], ST[:, u % 2, r * P:(r + 1) * P], B.va[:, r, h, :],
                                       start=(r == keys(u)[0]), stop=(r == keys(u)[1] - 1))
                    mm.then_inc(s("sv"), 1)

                front(0)
                for u in range(U):
                    if u + 1 < U:
                        front(u + 1)
                    back(u)

            @block.scalar
            def _(act):
                def exps(u):
                    act.wait_ge(s("m"), u + 1)
                    if u >= 2:
                        act.wait_ge(s("inter"), u - 1)
                    a, z = span(u)
                    act.activation(E[:, u % 2, a:z + 1], Dm[:, u % 2, a:z + 1], ACT.Exp, bias=nm[:, u, 0:1])
                    act.activation(nm[:, u, 1:2], nm[:, u, 0:1], ACT.Exp).then_inc(s("E"), 1)

                exps(0)
                for u in range(U):
                    if u + 1 < U:
                        exps(u + 1)
                    act.wait_ge(s("turned"), u + 1)
                    if u >= 2:
                        act.wait_ge(s("sv"), u - 1)
                    a, z = span(u)
                    act.activation(ST[:, u % 2, a:z], K.ps[:, 4, a:z], ACT.Copy).then_inc(s("ST"), 1)
                    act.wait_ge(s("qc"), u + 1)
                    act.wait_ge(s("E"), u + 1)
                    if u >= 2:
                        act.wait_ge(s("sum"), u - 1)
                    act.activation(inter[:, u % 2, :], K.ps[:, 5, 0:VW], ACT.Copy, scale=E[:, u % 2, z:z + 1])\
                       .then_inc(s("inter"), 1)

            @block.vector
            def _(dve):
                link = Link(dve, s("chain"))

                def build(g):
                    d, h = g // MH, g % MH
                    _, past, _, ci, cf = col[d]
                    if g >= 2:
                        dve.wait_ge(s("D"), NT * (g - 1))
                    for r in range(NT):
                        f = lf[:, r, cf + h:cf + h + 1]
                        dve.tensor_scalar(gi[:, g % 2, r, :], K.a("ident"), B.gt[:, r, ci + h:ci + h + 1], None, ALU.mult)
                        dve.tensor_scalar(G[:, g % 2, r, L:L + 2], K.a("ones")[:, 0:2], f, None, ALU.mult)
                        link(dve.tensor_scalar(G[:, g % 2, r, 0:L], tabs[past][:, r, :], f, None, ALU.mult))
                    for r in range(NT):
                        v = G[:, g % 2, r, r * P:(r + 1) * P]
                        x = dve.tensor_tensor(v, v, gi[:, g % 2, r, :], ALU.add)
                    x.then_inc(s("G"), 1)

                def first(u):
                    d, h, T = units[u]
                    dve.wait_ge(s("D"), u + 1)
                    if u >= 2:
                        dve.wait_ge(s("E"), u - 1)
                    a, z = span(u)
                    dve.tensor_tensor(Dm[:, u % 2, a:z], K.ps[:, u % 2, a:z], tabs[col[d][2]][:, T, a:z], ALU.add)
                    link(dve.tensor_tensor(Dm[:, u % 2, z:z + 1], K.ps[:, u % 2, L:L + 1], mB[:, d * MH + h:d * MH + h + 1],
                                           ALU.add))
                    dve.tensor_reduce(nm[:, u, 0:1], Dm[:, u % 2, a:z + 1], AX.X, ALU.max, negate=True).then_inc(s("m"), 1)

                def second(u):
                    dve.wait_ge(s("E"), u + 1)
                    dve.wait_ge(s("qk"), u + 1)
                    if u >= 2:
                        dve.wait_ge(s("turned"), u - 1)
                    a, z = span(u)
                    dve.scalar_tensor_tensor(out=S[:, u % 2, a:z], in0=K.ps[:, 2 + u % 2, a:z], scalar=DH ** -0.5,
                                             in1=E[:, u % 2, a:z], op0=ALU.mult, op1=ALU.mult).then_inc(s("S"), 1)

                def third(u):
                    d, h, T = units[u]
                    dve.wait_ge(s("inter"), u + 1)
                    dve.wait_ge(s("sv"), u + 1)
                    dve.tensor_tensor(cm[:, u % 2, :], K.ps[:, 6, 0:VW], inter[:, u % 2, :], ALU.add).then_inc(s("sum"), 1)
                    dve.wait_ge(s("sum"), u + 1)
                    den = cm[:, u % 2, DH:VW]
                    link(dve.scalar_tensor_tensor(out=nm[:, u, 2:3], in0=den, scalar=-1.0, in1=den,
                                                  op0=ALU.mult, op1=ALU.max))
                    link(dve.tensor_tensor(nm[:, u, 3:4], nm[:, u, 2:3], nm[:, u, 1:2], ALU.max))
                    link(dve.reciprocal(nm[:, u, 2:3], nm[:, u, 3:4]))
                    out = hid[:, T, h, :]
                    if d == 0:
                        link(dve.tensor_scalar(out, cm[:, u % 2, 0:DH], nm[:, u, 2:3], None, ALU.mult))
                    else:
                        link(dve.scalar_tensor_tensor(out=out, in0=cm[:, u % 2, 0:DH], scalar=nm[:, u, 2:3], in1=out,
                                                      op0=ALU.mult, op1=ALU.add))

                build(0)
                build(1)
                first(0)
                for u in range(U):
                    if u % NT == 0 and u // NT >= 1 and u // NT + 1 < U // NT:
                        build(u // NT + 1)
                    if u + 1 < U:
                        first(u + 1)
                    second(u)
                    if u >= 1:
                        third(u - 1)
                third(U - 1)

            @block.gpsimd
            def _(pool):
                K.clear_old(pool)

            @block.sync
            def _(sp):
                K.stream.issue(sp)


def window_batches(K, B, oa):
    out = []
    for T in range(NT):
        for p in range(4):
            kv = p // 2
            out.append((
                lambda m, p=p, kv=kv, T=T: (B.qh[:, 2 * p + m, T * P:(T + 1) * P], B.kh[:, kv, :]),
                lambda m, kb, kv=kv: B.vh[:, kb, kv * 64:(kv + 1) * 64],
                bcast(K.b("window")[:, T * 2 * L:(T + 1) * 2 * L], 2), 64 ** -0.5,
                oa[:, T, 2 * p * 64:(2 * p + 2) * 64].rearrange("p (m e) -> p m e", m=2),
                K.r("sink")[:, 2 * p:2 * p + 2].unsqueeze(2), 2 * NT))
    return out


def phase_second_out(K, B, hid, oa):
    nc, st = K.nc, K.stream
    with ExitStack() as ctx:
        s = K.signals("sout")

        def sb(nm_, shape):
            return ctx.enter_context(nc.sbuf_tensor(f"sout_{nm_}", shape, F32))

        sq = sb("sq", [P, NT * MH, DH])
        st8 = sb("st8", [P, 3, NT * MH])
        with nc.Block() as block:
            @block.vector
            def _(dve):
                link = Link(dve, s("chain"))
                hv = hid[:].rearrange("p t h e -> p (t h) e")
                link(dve.tensor_tensor(sq[:], hv, hv, ALU.mult))
                link(dve.tensor_reduce(st8[:, 0, :], sq[:], AX.X, ALU.add))
                dve.tensor_scalar(st8[:, 1, :], st8[:, 0, :], 1.0 / DH, EPS, ALU.mult, ALU.add).then_inc(s("ms"), 1)
                dve.wait_ge(s("root"), 1)
                link(dve.reciprocal(st8[:, 0, :], st8[:, 2, :]))
                dve.tensor_tensor(sq[:], hv, spread(st8[:, 0, :], DH), ALU.mult).then_inc(s("hn"), 1)
                for h in range(MH):
                    dve.wait_ge(s("turned"), 5 + h)
                    dve.scalar_tensor_tensor(out=K.hT[:, h, :], in0=K.ps[:, h, 0:L], scalar=K.v("mlstm_g")[:, h:h + 1],
                                             in1=B.og[:, h, :], op0=ALU.mult, op1=ALU.mult).then_inc(s("ym"), 1)
                for i in range(KT):
                    dve.wait_ge(s("y"), i + 1)
                    dve.scalar_tensor_tensor(out=K.xT[:, i, :], in0=K.ps[:, 4 + i % 4, 0:L], scalar=K.mod[2][:, 0, 16 + i:17 + i],
                                             in1=K.xT[:, i, :], op0=ALU.mult, op1=ALU.add).then_inc(s("res"), 1)

            @block.scalar
            def _(act):
                act.wait_ge(s("ms"), 1)
                act.activation(st8[:, 2, :], st8[:, 1, :], ACT.Sqrt).then_inc(s("root"), 1)
                for i in range(4):
                    act.wait_ge(s("turned"), i + 1)
                    act.activation(K.hT[:, 4 + i, :], K.ps[:, i, 0:L], ACT.Copy).then_inc(s("ya"), 1)

            @block.tensor
            def _(pe):
                for i in range(4):
                    for T in range(NT):
                        mm = pe.transpose(K.ps[:, i, T * P:(T + 1) * P], oa[:, T, i * P:(i + 1) * P], K.a("ident"))
                    mm.then_inc(s("turned"), 1)
                pe.wait_ge(s("hn"), 1)
                for h in range(MH):
                    pe.wait_ge(s("ya"), h + 1)
                    for T in range(NT):
                        mm = pe.transpose(K.ps[:, h, T * P:(T + 1) * P], sq[:, T * MH + h, :], K.a("ident"))
                    mm.then_inc(s("turned"), 1)
                pe.wait_ge(s("ym"), MH)
                for c in range(KT // CT):
                    n = st.take()
                    st.wait(pe, n)
                    w = st.view(n, KT, CW)
                    for m in range(CT):
                        i = CT * c + m
                        if i >= 4:
                            pe.wait_ge(s("res"), i - 3)
                        for k in range(KT):
                            mm = pe.matmul(K.ps[:, 4 + i % 4, 0:L], w[:, k, m * P:(m + 1) * P], K.hT[:, k, :],
                                           start=(k == 0), stop=(k == KT - 1))
                        mm.then_inc(s("y"), 1)
                    pe.wait_ge(s("y"), CT * (c + 1))
                    pe.sem_inc(st.freed[n % RING], 1)

            @block.gpsimd
            def _(pool):
                K.clear_old(pool)

            @block.sync
            def _(sp):
                st.issue(sp)


def phase_second_load(K, A, cT, pads):
    nc = K.nc
    with ExitStack() as ctx:
        s = K.signals("sload")
        with nc.Block() as block:
            @block.scalar
            def _(act):
                act.dma_start(cT[:], A["ctxT"].rearrange("(k p) t -> p k t", p=P)).then_inc(K.second_in, 16)
                act.dma_start(K.cb_[:], A["const_b"]).then_inc(K.second_in, 16)

            @block.vector
            def _(dve):
                for pad in pads[0:3]:
                    dve.memset(pad[:, :, 0:1], 0.0)
                    dve.memset(pad[:, :, L + 1:L + 2], 0.0)

            @block.gpsimd
            def _(pool):
                K.clear_old(pool)

            @block.sync
            def _(sp):
                K.stream.issue(sp)


def second_mixer(K, A):
    nc = K.nc
    with ExitStack() as ctx:
        def sb(name, shape, c=ctx):
            return c.enter_context(nc.sbuf_tensor(f"sm_{name}", shape, F32))
        K.cb_ = sb("const_b", [P, WIDTH_B])
        B = SecondBuffers(nc, ctx)
        lf = sb("lf", [P, 2 * NT, 16])
        with ExitStack() as early:
            pads = [sb(n, [P, MH, L + 2], early) for n in ("qpad", "kpad", "kcpad")]
            cT = sb("cT", [P, KT, L], early)
            pads.append(cT)
            phase_second_load(K, A, cT, pads)
            phase_norm(K, "final1", K.xT, K.xT, K.v("final_g"), None)
            phase_norm(K, "xnorm", K.xT, K.hT, K.gain[2][:, 0, :], K.mod[2][:, 0, 0:8])
            phase_norm(K, "cnorm", cT, cT, K.gain[2][:, 2, :], K.mod[2][:, 1, 0:8], arrived=(K.second_in, 32))
            phase_project(K, "sproj", second_projections(K, B, pads), K.ada_project[2], 2)
            phase_shape(K, B, pads, lf)
        C0, mB = sb("C0", [P, 2 * MH, VW]), sb("mB", [P, 2 * MH])
        hid, oa = sb("hid", [P, NT, MH, DH]), sb("oa", [P, NT, 512])
        phase_state(K, B, lf, C0, mB)
        phase_mlstm(K, B, lf, C0, mB, hid)
        phase_attention(K, "win", B, window_batches(K, B, oa), 2, 4, extra=1)
        phase_second_out(K, B, hid, oa)


def build(nc, A, outT):
    with ExitStack() as ctx:
        K = Kit()
        K.nc, K.old, K.now = nc, None, None

        def sb(name, shape):
            return ctx.enter_context(nc.sbuf_tensor(name, shape, F32))

        K.band = A["band"]
        K.second_in = ctx.enter_context(nc.semaphore("second_in"))
        K.stream = Stream(nc, ctx)
        K.ps = ctx.enter_context(nc.psum_tensor("ps", [P, 8, 512], F32))
        K.ca = sb("const_a", [P, WIDTH_A])
        K.vec = sb("vec", [P, WIDTH_V])
        K.row = sb("row", [P, WIDTH_R])
        K.xT, K.hT = sb("xT", [P, KT, L]), sb("hT", [P, KT, L])
        K.silu_c = sb("silu_c", [P, 24])
        K.mod = [sb(f"mod{l}", [P, 1 + (l == 2), MODS]) for l in range(3)]
        K.gain = [sb(f"gain{l}", [P, 3, KT]) for l in range(3)]
        K.lam, K.scratch1 = sb("lam", [P, 2]), sb("scratch1", [P, 64])
        K.a = lambda n: K.ca[:, COLS_A[n][0]:sum(COLS_A[n])]
        K.b = lambda n: K.cb_[:, COLS_B[n][0]:sum(COLS_B[n])]
        K.v = lambda n: K.vec[:, COLS_V[n][0]:sum(COLS_V[n])]
        K.r = lambda n: K.row[:, COLS_R[n][0]:sum(COLS_R[n])]
        K.mask = lambda T: K.a("mask")[:, T * L:(T + 1) * L]
        K.alibi = lambda T: K.a("alibi")[:, T * HEADS * L:(T + 1) * HEADS * L].rearrange("p (h s) -> p h s", h=HEADS)
        K.ada_w = [A["ada_w"][0], A["ada_w"][1], A["w_ada_2"][0]]
        K.ada_project = [[(l, i) for i in range(KT, ADA_N)] for l in range(3)]
        K.ada_ffn = [(1, i) for i in range(KT)] + [(2, i) for i in range(KT)]
        plan_stream(K, A)

        phase_load(K, A)
        mixer(K, 0)
        phase_norm(K, "fnorm0", K.xT, K.hT, K.gain[0][:, 1, :], K.mod[0][:, 0, 24:32])
        phase_ffn(K, "ffn0", K.mod[0][:, 0, 40:48], beside=K.ada_ffn)
        mixer(K, 1)
        phase_norm(K, "fnorm1", K.xT, K.hT, K.gain[1][:, 1, :], K.mod[1][:, 0, 24:32])
        moe(K, A)
        second_mixer(K, A)
        phase_norm(K, "fnorm2", K.xT, K.hT, K.gain[2][:, 1, :], K.mod[2][:, 0, 24:32])
        fw, fb = K.v("fconv_w"), K.v("fconv_b")
        NF = FF // P
        phase_ffn(K, "ffn2", K.mod[2][:, 0, 40:48],
                  conv=(lambda j, i: fw[:, j * NF + i:j * NF + i + 1], lambda i: fb[:, i:i + 1]))
        phase_norm(K, "final2", K.xT, K.hT, K.v("final_g2"), None, out=outT.rearrange("(k p) t -> p k t", p=P))
        K.old.ctx.close()
        K.now.ctx.close()
        assert K.stream.taken == len(K.stream.items) == K.stream.issued



def rope_rows(pos, base=10000.0, pairs=16):
    inv = (base ** (-np.arange(pairs, dtype=np.float32) / pairs)).astype(np.float32)
    ang = pos[None, :].astype(np.float32) * inv[:, None]
    return np.cos(ang), np.sin(ang)


def swap_matrix(n, first, half):
    m = np.eye(n, dtype=np.float32)
    for b in range(first, n, 2 * half):
        for i in range(half):
            x, y = b + i, b + half + i
            m[[x, y]] = m[[y, x]]
    return m


def tables():
    t, r = np.arange(L), np.arange(P)
    f = np.float32

    def tok(m):
        return np.concatenate([m[T * P:(T + 1) * P].reshape(P, -1) for T in range(NT)], axis=1).astype(f)

    def rows(m):
        out = np.zeros((P, m.shape[1]), f)
        out[:m.shape[0]] = m
        return out

    chunk = np.where(t[None, :] // CHUNK <= t[:, None] // CHUNK, 0.0, NEG)
    slopes = 2.0 ** (-8.0 * np.arange(1, HEADS + 1) / HEADS)
    alibi = -slopes[None, :, None] * np.abs(t[:, None] - t[None, :])[:, None, :]
    alibi = np.where(chunk[:, None, :] < 0, NEG, alibi)
    cos, sin = rope_rows(t)
    cos32, sin32 = np.concatenate([cos, cos]), np.concatenate([-sin, sin])
    cos96 = np.concatenate([np.ones((64, L)), cos32])
    sin96 = np.concatenate([np.zeros((64, L)), sin32])
    pick = np.zeros((P, NE, P))
    for e in range(NE):
        pick[e, e] = 1
    a = {"ident": np.eye(P), "ones": np.ones((P, P)), "flip": np.eye(P)[::-1], "mask": tok(chunk), "alibi": tok(alibi),
         "cos96": rows(cos96), "sin96": rows(sin96), "perm96": rows(swap_matrix(96, 64, 16)), "cos32": rows(cos32),
         "sin32": rows(sin32), "perm32": rows(swap_matrix(32, 0, 16)), "pick": pick.reshape(P, -1)}
    (cr, sr), (cc, sc) = rope_rows(t // 64), rope_rows(t % 64)
    far = np.abs(t[:, None] - t[None, :]) > 128
    window = np.concatenate([np.where(far, NEG, 0.0), np.zeros((L, L))], axis=1)
    b = {"upto_f": tok(t[:, None] <= t[None, :]), "upto_b": tok(t[:, None] >= t[None, :]),
         "past_f": tok(t[:, None] > t[None, :]), "past_b": tok(t[:, None] < t[None, :]),
         "mask_f": tok(np.where(t[None, :] <= t[:, None], 0.0, NEG)),
         "mask_b": tok(np.where(t[None, :] >= t[:, None], 0.0, NEG)), "window": tok(window),
         "cosA": rows(np.concatenate([cr, cr, cc, cc])), "sinA": rows(np.concatenate([-sr, sr, -sc, sc])),
         "permA": rows(swap_matrix(64, 0, 16))}
    c = {"before": tok(t[:, None] < t[None, :]), "slots": np.tile(t[None, :], (P, 1)),
         "slot_of": np.stack([r, r + P], axis=1)}
    out = []
    for names, d in ((CONST_A, a), (CONST_B, b), (CONST_C, c)):
        out.append(np.ascontiguousarray(np.concatenate([d[n].astype(f) for n, _ in names], axis=1)))
        assert all(d[n].shape[1] == w for n, w in names)
    return out


def feature_columns(v):
    v = np.asarray(v)
    v = v.reshape(-1, v.shape[-1])
    return v.reshape(v.shape[0], -1, P).transpose(2, 0, 1).reshape(P, -1)


WEIGHTS = ["ada_w", "w_in", "w_out", "mla_w_uq", "mla_w_ukv", "ffn_w1", "ffn_w3", "ffn_w2", "moe_router", "moe_w1",
           "moe_w3", "moe_w2", "w_ada_2", "w_in_2", "w_out_2", "w_up_2", "w_down_2"]


def kernel(**inp):
    import concourse.bacc as bacc
    from concourse.bass_utils import run_bass_kernel_spmd as run

    fc = feature_columns
    x = {k: np.asarray(v) for k, v in inp.items()}
    c2 = np.stack([x["c_2"][0], x["c_ctx_2"]])
    vec = {"c": fc(x["c"]), "c2": c2.reshape(2, KT, P).transpose(2, 1, 0).reshape(P, -1),
           "ada_b0": fc(x["ada_b"][0]), "ada_b1": fc(x["ada_b"][1]), "ada_b2": fc(x["b_ada_2"][0]),
           "mix_g0": fc(x["mix_norm_g"][0]), "mix_g1": fc(x["mix_norm_g"][1]), "ffn_g0": fc(x["ffn_norm_g"][0]),
           "ffn_g1": fc(x["ffn_norm_g"][1]), "final_g": fc(x["final_norm_g"]), "mix_g2": fc(x["norm_mix_2"]),
           "ffn_g2": fc(x["norm_ffn_2"]), "final_g2": fc(x["final_norm_2"]), "qn_g0": fc(x["mla_q_norm_g"][0]),
           "qn_g1": fc(x["mla_q_norm_g"][1]), "kvn_g0": fc(x["mla_kv_norm_g"][0]), "kvn_g1": fc(x["mla_kv_norm_g"][1]),
           "conv_w": fc(x["qk_conv_w_2"][0]), "conv_b": fc(x["qk_conv_b_2"][0]), "mlstm_g": fc(x["mlstm_norm_2"][0]),
           "fconv_w": fc(x["ffn_conv_w_2"][0]), "fconv_b": fc(x["ffn_conv_b_2"][0])}
    row = {"lam0": x["diff_lambda"][0], "lam1": x["diff_lambda"][1], "dng0": x["diff_norm_g"][0],
           "dng1": x["diff_norm_g"][1], "gate_b": x["gate_b_2"][0], "sink": x["attn_sink_2"][0]}
    rb = x["band_rel_bias"]
    band = np.concatenate([np.repeat(rb[:, :, -1:], 127, axis=2), rb[:, :, ::-1], np.repeat(rb[:, :, 0:1], 127, axis=2)],
                          axis=2)
    const_a, const_b, const_c = tables()
    arrays = {n: x[n] for n in WEIGHTS}
    arrays.update(vecs=np.concatenate([vec[n] for n, _ in VECS], axis=1),
                  rows=np.concatenate([row[n].reshape(-1) for n, _ in ROWS])[None, :],
                  band=band, const_a=const_a, const_b=const_b, const_c=const_c, xT=x["x"][0].T, ctxT=x["ctx_2"][0].T)
    arrays = {n: np.ascontiguousarray(a) for n, a in arrays.items()}
    nc = bacc.Bacc("TRN2", target_bir_lowering=False, num_devices=1)
    A = {n: nc.dram_tensor("in_" + n, a.shape, F32, kind="ExternalInput").ap() for n, a in arrays.items()}
    outT = nc.dram_tensor("outT", (D, L), F32, kind="ExternalOutput").ap()
    build(nc, A, outT)
    r = run(nc, [{"in_" + n: a for n, a in arrays.items()}], core_ids=[0])
    return np.ascontiguousarray(r.results[0]["outT"].T)[None]
```
